# Optimizing a Trainium2 kernel written in Bass

```python
import jax, jax.numpy as jnp
from jax import lax
import numpy as np

D_MODEL = 1024
BATCH = 1
SEQ = 256
DEPTH = 1

SB_HEADS = 8
SB_HEAD_DIM = 64
MLA_HEADS = 8
QK_NOPE_DIM = 64
QK_ROPE_DIM = 32
V_HEAD_DIM = 64
Q_LORA_RANK = 256
KV_LORA_RANK = 128
SB_WIDTH = SB_HEADS * SB_HEAD_DIM
MLA_WIDTH = MLA_HEADS * V_HEAD_DIM
D_MIX = SB_WIDTH + MLA_WIDTH
IN_COLS = 3 * SB_WIDTH + Q_LORA_RANK + KV_LORA_RANK + QK_ROPE_DIM
D_FF = 2816
CONV_WIDTH = 3
PLE_DIM = 256
Q_BLOCK = 128
ROPE_THETA = 10000.0
NORM_EPS = 1e-6
MAX_POS_OFFSET = 4096


def rms_norm(x, gain):
    xf = x.astype(jnp.float32)
    y = xf * lax.rsqrt(jnp.mean(xf * xf, axis=-1, keepdims=True) + NORM_EPS)
    return (y * gain.astype(jnp.float32)).astype(x.dtype)

def rope_tables(positions, dtype):
    inv_freq = 1.0 / (ROPE_THETA ** (jnp.arange(0, QK_ROPE_DIM, 2, dtype=jnp.float32) / QK_ROPE_DIM))
    ang = positions.astype(jnp.float32)[..., None] * inv_freq
    return jnp.cos(ang).astype(dtype), jnp.sin(ang).astype(dtype)

def apply_rope(x, cos, sin):
    x1, x2 = jnp.split(x, 2, axis=-1)
    return jnp.concatenate([x1 * cos - x2 * sin, x2 * cos + x1 * sin], axis=-1)

def stick_breaking_attention(q, k, v):
    seq = q.shape[1]
    scale = SB_HEAD_DIM ** -0.5
    outs = []
    for start in range(0, seq, Q_BLOCK):
        end = start + Q_BLOCK
        z = jnp.einsum('bqhd,bkhd->bhqk', q[:, start:end], k[:, :end]).astype(jnp.float32) * scale
        t_idx = start + jnp.arange(Q_BLOCK)[:, None]
        s_idx = jnp.arange(end)[None, :]
        strict = s_idx < t_idx
        log_keep = jnp.where(strict, -jax.nn.softplus(z), 0.0)
        log_keep_after = lax.cumsum(log_keep, axis=3, reverse=True) - log_keep
        weights = jnp.where(strict, jnp.exp(jax.nn.log_sigmoid(z) + log_keep_after), 0.0)
        outs.append(jnp.einsum('bhqk,bkhd->bqhd', weights.astype(v.dtype), v[:, :end]))
    return jnp.concatenate(outs, axis=1)

def mla_attention(q_nope, q_rope, k_nope, k_rope, v):
    seq = q_nope.shape[1]
    scale = (QK_NOPE_DIM + QK_ROPE_DIM) ** -0.5
    outs = []
    for start in range(0, seq, Q_BLOCK):
        end = start + Q_BLOCK
        s = (jnp.einsum('bqhd,bkhd->bhqk', q_nope[:, start:end], k_nope[:, :end])
             + jnp.einsum('bqhd,bkd->bhqk', q_rope[:, start:end], k_rope[:, :end]))
        s = s.astype(jnp.float32) * scale
        causal = jnp.arange(end)[None, :] <= (start + jnp.arange(Q_BLOCK)[:, None])
        probs = jax.nn.softmax(jnp.where(causal, s, -jnp.inf), axis=-1)
        outs.append(jnp.einsum('bhqk,bkhd->bqhd', probs.astype(v.dtype), v[:, :end]))
    return jnp.concatenate(outs, axis=1)

def causal_depthwise_conv(u, w, b):
    c = u.shape[-1]
    y = lax.conv_general_dilated(u, w[:, None, :].astype(u.dtype), window_strides=(1,),
                                 padding=[(CONV_WIDTH - 1, 0)],
                                 dimension_numbers=('NWC', 'WIO', 'NWC'),
                                 feature_group_count=c)
    return y + b.astype(u.dtype)

def first_inputs(seed: int = 0) -> dict:
    key = jax.random.key(seed)
    ks = jax.random.split(key, 24)
    f32 = jnp.float32

    def normal(k, shape, scale):
        return jax.random.normal(k, shape, f32) * scale

    def gain(k, shape):
        return 1.0 + 0.05 * jax.random.normal(k, shape, f32)

    L = DEPTH
    x = normal(ks[0], (BATCH, SEQ, D_MODEL), 1.0)
    p = normal(ks[1], (DEPTH, BATCH, SEQ, PLE_DIM), 1.0)
    offsets = jax.random.randint(ks[2], (BATCH, 1), 0, MAX_POS_OFFSET, dtype=jnp.int32)
    positions = offsets + jnp.arange(SEQ, dtype=jnp.int32)[None, :]
    return {
        'x': x,
        'p': p,
        'positions': positions,
        'w_in': normal(ks[3], (L, D_MODEL, IN_COLS), D_MODEL ** -0.5),
        'g_pre_mix': gain(ks[4], (L, D_MODEL)),
        'g_q_lat': gain(ks[5], (L, Q_LORA_RANK)),
        'w_q_up': normal(ks[6], (L, Q_LORA_RANK, MLA_HEADS * (QK_NOPE_DIM + QK_ROPE_DIM)), Q_LORA_RANK ** -0.5),
        'g_kv_lat': gain(ks[7], (L, KV_LORA_RANK)),
        'w_kv_up': normal(ks[8], (L, KV_LORA_RANK, MLA_HEADS * (QK_NOPE_DIM + V_HEAD_DIM)), KV_LORA_RANK ** -0.5),
        'g_grp_sb': gain(ks[9], (L, SB_WIDTH)),
        'g_grp_mla': gain(ks[10], (L, MLA_WIDTH)),
        'w_o': normal(ks[11], (L, D_MIX, D_MODEL), D_MIX ** -0.5),
        'g_post_mix': gain(ks[12], (L, D_MODEL)),
        'g_pre_ffn': gain(ks[13], (L, D_MODEL)),
        'w_up': normal(ks[14], (L, D_MODEL, 2 * D_FF), D_MODEL ** -0.5),
        'conv_w': normal(ks[15], (L, CONV_WIDTH, 2 * D_FF), CONV_WIDTH ** -0.5),
        'conv_b': normal(ks[16], (L, 2 * D_FF), 0.01),
        'w_down': normal(ks[17], (L, D_FF, D_MODEL), D_FF ** -0.5),
        'g_post_ffn': gain(ks[18], (L, D_MODEL)),
        'w_ple': normal(ks[19], (L, PLE_DIM, D_MODEL), PLE_DIM ** -0.5),
        'g_ple_gate': gain(ks[20], (L, D_MODEL)),
        'w_ple_gate': normal(ks[21], (L, D_MODEL, D_MODEL), D_MODEL ** -0.5),
        'b_ple_gate': normal(ks[22], (L, D_MODEL), 0.01),
        'g_post_ple': gain(ks[23], (L, D_MODEL)),
    }

def first_block(x, p, positions, w_in, g_pre_mix, g_q_lat, w_q_up, g_kv_lat, w_kv_up,
              g_grp_sb, g_grp_mla, w_o, g_post_mix, g_pre_ffn, w_up, conv_w, conv_b,
              w_down, g_post_ffn, w_ple, g_ple_gate, w_ple_gate, b_ple_gate, g_post_ple):
    b, s, _ = x.shape
    cos, sin = rope_tables(positions, x.dtype)
    split_at = [SB_WIDTH, 2 * SB_WIDTH, 3 * SB_WIDTH,
                3 * SB_WIDTH + Q_LORA_RANK, 3 * SB_WIDTH + Q_LORA_RANK + KV_LORA_RANK]
    for i in range(DEPTH):
        h = rms_norm(x, g_pre_mix[i])
        proj = h @ w_in[i]
        sb_q, sb_k, sb_v, q_lat, kv_lat, k_rope = jnp.split(proj, split_at, axis=-1)

        o_sb = stick_breaking_attention(sb_q.reshape(b, s, SB_HEADS, SB_HEAD_DIM),
                                        sb_k.reshape(b, s, SB_HEADS, SB_HEAD_DIM),
                                        sb_v.reshape(b, s, SB_HEADS, SB_HEAD_DIM)).reshape(b, s, SB_WIDTH)

        q = (rms_norm(q_lat, g_q_lat[i]) @ w_q_up[i]).reshape(b, s, MLA_HEADS, QK_NOPE_DIM + QK_ROPE_DIM)
        q_nope, q_rope = jnp.split(q, [QK_NOPE_DIM], axis=-1)
        q_rope = apply_rope(q_rope, cos[:, :, None, :], sin[:, :, None, :])
        kv = (rms_norm(kv_lat, g_kv_lat[i]) @ w_kv_up[i]).reshape(b, s, MLA_HEADS, QK_NOPE_DIM + V_HEAD_DIM)
        k_nope, v_mla = jnp.split(kv, [QK_NOPE_DIM], axis=-1)
        k_rope = apply_rope(k_rope, cos, sin)
        o_mla = mla_attention(q_nope, q_rope, k_nope, k_rope, v_mla).reshape(b, s, MLA_WIDTH)

        mix = jnp.concatenate([rms_norm(o_sb, g_grp_sb[i]), rms_norm(o_mla, g_grp_mla[i])], axis=-1) @ w_o[i]
        x = x + rms_norm(mix, g_post_mix[i])

        h = rms_norm(x, g_pre_ffn[i])
        u = causal_depthwise_conv(h @ w_up[i], conv_w[i], conv_b[i])
        gate, val = jnp.split(u, 2, axis=-1)
        f = (jax.nn.gelu(gate, approximate=True) * val) @ w_down[i]
        x = x + rms_norm(f, g_post_ffn[i])

        e = p[i] @ w_ple[i]
        g = jax.nn.sigmoid(rms_norm(x, g_ple_gate[i]) @ w_ple_gate[i] + b_ple_gate[i])
        x = x + rms_norm(g * e, g_post_ple[i])
    return x


MEM_LEN = 256
HEAD_DIM = 64
NSA_HEADS = 8
NSA_GROUPS = 2
NSA_HPG = NSA_HEADS // NSA_GROUPS
NSA_WIDTH = NSA_HEADS * HEAD_DIM
KV_WIDTH = NSA_GROUPS * HEAD_DIM
CMP_BLOCK = 32
CMP_STRIDE = 16
CMP_HIDDEN = 256
SLC_BLOCK = 64
SLC_TOPK = 16
WINDOW = 512
NSA_Q_BLOCK = 64
FORCE = 1e6
CONV_WIDTH_2 = 512
CONV_KSIZE = 31
MEM_HEADS = 4
MEM_HEAD_DIM = 128
MEM_WIDTH = MEM_HEADS * MEM_HEAD_DIM
N_BRANCH = 3
D_FF_2 = -(-8 * D_MODEL // (3 * 256)) * 256
IN_COLS_2 = NSA_WIDTH + 6 * KV_WIDTH + 3 * NSA_HEADS + 2 * CONV_WIDTH_2 + MEM_WIDTH + N_BRANCH * D_MODEL
RMS_EPS = 1e-6
LN_EPS = 1e-5


def rms_norm_2(x, g):
    xf = x.astype(jnp.float32)
    y = xf * lax.rsqrt(jnp.mean(xf * xf, axis=-1, keepdims=True) + RMS_EPS)
    return (y * g.astype(jnp.float32)).astype(x.dtype)

def layer_norm(x, g, b):
    xf = x.astype(jnp.float32)
    mu = jnp.mean(xf, axis=-1, keepdims=True)
    var = jnp.mean(jnp.square(xf - mu), axis=-1, keepdims=True)
    y = (xf - mu) * lax.rsqrt(var + LN_EPS) * g.astype(jnp.float32) + b.astype(jnp.float32)
    return y.astype(x.dtype)

def masked_softmax(s, mask):
    s = jnp.where(mask, s.astype(jnp.float32), -jnp.inf)
    m = jnp.max(s, axis=-1, keepdims=True)
    m = jnp.where(jnp.isfinite(m), m, 0.0)
    e = jnp.exp(s - m)
    den = jnp.sum(e, axis=-1, keepdims=True)
    return e / jnp.where(den > 0, den, 1.0)

def compress_blocks(kv, pos, w1, w2):
    b, g, s, dh = kv.shape
    chunks = kv.reshape(b, g, s // CMP_STRIDE, CMP_STRIDE, dh)
    blocks = jnp.concatenate([chunks[:, :, :-1], chunks[:, :, 1:]], axis=3)
    blocks = (blocks + pos).reshape(b, g, blocks.shape[2], CMP_BLOCK * dh)
    return jax.nn.gelu(blocks @ w1) @ w2

def nsa_attention(q, kc, vc, ks, vs, kw, vw, gate):
    b, g, hpg, s, dh = q.shape
    n_c = kc.shape[2]
    n_sel = ks.shape[2]
    topk = min(SLC_TOPK, n_sel)
    ratio = SLC_BLOCK // CMP_STRIDE
    scale = dh ** -0.5
    qb_len = NSA_Q_BLOCK
    cmp_end = jnp.arange(n_c) * CMP_STRIDE + CMP_BLOCK - 1
    sel_ids = jnp.arange(n_sel)
    bi = jnp.arange(b)[:, None, None, None]
    gi = jnp.arange(g)[None, :, None, None]

    def block(qb):
        q0 = qb * qb_len
        t = q0 + jnp.arange(qb_len)
        qq = lax.dynamic_slice_in_dim(q, q0, qb_len, axis=3) * scale
        gg = lax.dynamic_slice_in_dim(gate, q0, qb_len, axis=3)

        s_c = jnp.einsum('bghqd,bgcd->bghqc', qq, kc)
        p_c = masked_softmax(s_c, cmp_end[None, :] <= t[:, None])
        o_c = jnp.einsum('bghqc,bgcd->bghqd', p_c.astype(vc.dtype), vc)

        imp = jnp.sum(p_c, axis=2)
        imp = jnp.pad(imp, ((0, 0), (0, 0), (0, 0), (1, ratio * (n_sel + 1) - n_c - 1)))
        rows = imp.reshape(b, g, qb_len, n_sel + 1, ratio)
        imp_s = jnp.sum(rows[..., :-1, :], axis=-1) + rows[..., 1:, 0]
        cur = t // SLC_BLOCK
        forced = (sel_ids[None, :] == 0) | (sel_ids[None, :] == cur[:, None]) | (sel_ids[None, :] == cur[:, None] - 1)
        future = sel_ids[None, :] * SLC_BLOCK > t[:, None]
        imp_s = jnp.where(forced, FORCE, jnp.where(future, -FORCE, imp_s))
        _, idx = lax.top_k(imp_s, topk)

        k_g = ks[bi, gi, idx]
        v_g = vs[bi, gi, idx]
        tok = idx[..., None] * SLC_BLOCK + jnp.arange(SLC_BLOCK)
        s_s = jnp.einsum('bghqd,bgqkld->bghqkl', qq, k_g).reshape(b, g, hpg, qb_len, topk * SLC_BLOCK)
        m_s = (tok <= t[:, None, None]).reshape(b, g, 1, qb_len, topk * SLC_BLOCK)
        p_s = masked_softmax(s_s, m_s).reshape(b, g, hpg, qb_len, topk, SLC_BLOCK)
        o_s = jnp.einsum('bghqkl,bgqkld->bghqd', p_s.astype(v_g.dtype), v_g)

        kwb = lax.dynamic_slice_in_dim(kw, q0, WINDOW + qb_len, axis=2)
        vwb = lax.dynamic_slice_in_dim(vw, q0, WINDOW + qb_len, axis=2)
        pos = q0 - WINDOW + jnp.arange(WINDOW + qb_len)
        diff = t[:, None] - pos[None, :]
        m_w = (diff >= 0) & (diff < WINDOW) & (pos[None, :] >= 0)
        s_w = jnp.einsum('bghqd,bgkd->bghqk', qq, kwb)
        p_w = masked_softmax(s_w, m_w)
        o_w = jnp.einsum('bghqk,bgkd->bghqd', p_w.astype(vwb.dtype), vwb)

        return gg[..., 0:1] * o_c + gg[..., 1:2] * o_s + gg[..., 2:3] * o_w

    out = lax.map(block, jnp.arange(s // qb_len))
    out = jnp.transpose(out, (1, 0, 4, 2, 3, 5))
    return out.reshape(b, s, g * hpg * dh)

def hybrid_layer(x, mem, norm_mix, w_in, nsa_qk_norm, cmp_pos, cmp_w1, cmp_w2, w_nsa_out,
                 conv_w, conv_b, conv_ln_g, conv_ln_b, w_conv_out, norm_mem, w_mem_kv,
                 mem_qk_norm, w_mem_out, w_out, norm_ffn, w_gate, w_up, w_down):
    b, s, _ = x.shape
    xn = rms_norm_2(x, norm_mix)
    proj = xn @ w_in
    sizes = [NSA_WIDTH, 6 * KV_WIDTH, 3 * NSA_HEADS, 2 * CONV_WIDTH_2, MEM_WIDTH, N_BRANCH * D_MODEL]
    points = [int(p) for p in np.cumsum(sizes)[:-1]]
    q_nsa, kv_nsa, g_nsa, conv_in, q_mem, g_merge = jnp.split(proj, points, axis=-1)

    def heads(t_, n):
        return jnp.transpose(t_.reshape(b, s, n, HEAD_DIM), (0, 2, 1, 3))
    q = rms_norm_2(heads(q_nsa, NSA_HEADS), nsa_qk_norm[0]).reshape(b, NSA_GROUPS, NSA_HPG, s, HEAD_DIM)
    k_c, v_c, k_s, v_s, k_w, v_w = [heads(t_, NSA_GROUPS) for t_ in jnp.split(kv_nsa, 6, axis=-1)]
    kc = rms_norm_2(compress_blocks(k_c, cmp_pos[0], cmp_w1[0], cmp_w2[0]), nsa_qk_norm[1])
    vc = compress_blocks(v_c, cmp_pos[1], cmp_w1[1], cmp_w2[1])
    n_sel = s // SLC_BLOCK
    ks = rms_norm_2(k_s, nsa_qk_norm[2]).reshape(b, NSA_GROUPS, n_sel, SLC_BLOCK, HEAD_DIM)
    vs = v_s.reshape(b, NSA_GROUPS, n_sel, SLC_BLOCK, HEAD_DIM)
    pad = ((0, 0), (0, 0), (WINDOW, 0), (0, 0))
    kw = jnp.pad(rms_norm_2(k_w, nsa_qk_norm[3]), pad)
    vw = jnp.pad(v_w, pad)
    gate = jnp.transpose(jax.nn.sigmoid(g_nsa).reshape(b, s, NSA_GROUPS, NSA_HPG, 3), (0, 2, 3, 1, 4))
    o_nsa = nsa_attention(q, kc, vc, ks, vs, kw, vw, gate)
    br_nsa = o_nsa @ w_nsa_out

    a, ag = jnp.split(conv_in, 2, axis=-1)
    u = a * jax.nn.sigmoid(ag)
    u = jnp.pad(u, ((0, 0), (CONV_KSIZE - 1, 0), (0, 0)))
    u = lax.conv_general_dilated(u, conv_w, (1,), 'VALID', dimension_numbers=('NWC', 'WIO', 'NWC'),
                                 feature_group_count=CONV_WIDTH_2) + conv_b
    u = jax.nn.silu(layer_norm(u, conv_ln_g, conv_ln_b))
    br_conv = u @ w_conv_out

    qm = rms_norm_2(q_mem.reshape(b, s, MEM_HEADS, MEM_HEAD_DIM), mem_qk_norm[0])
    kvm = rms_norm_2(mem, norm_mem) @ w_mem_kv
    km, vm = jnp.split(kvm, 2, axis=-1)
    km = rms_norm_2(km.reshape(b, -1, MEM_HEADS, MEM_HEAD_DIM), mem_qk_norm[1])
    vm = vm.reshape(b, -1, MEM_HEADS, MEM_HEAD_DIM)
    s_m = jnp.einsum('bshd,bmhd->bhsm', qm, km).astype(jnp.float32) * (MEM_HEAD_DIM ** -0.5)
    p_m = jax.nn.softmax(s_m, axis=-1)
    o_m = jnp.einsum('bhsm,bmhd->bshd', p_m.astype(vm.dtype), vm).reshape(b, s, MEM_WIDTH)
    br_mem = o_m @ w_mem_out

    gm = jax.nn.sigmoid(g_merge).reshape(b, s, N_BRANCH, D_MODEL)
    merged = gm[:, :, 0] * br_nsa + gm[:, :, 1] * br_conv + gm[:, :, 2] * br_mem
    h = x + merged @ w_out

    hn = rms_norm_2(h, norm_ffn)
    return h + (jax.nn.silu(hn @ w_gate) * (hn @ w_up)) @ w_down

def second_inputs(seed: int = 0) -> dict:
    key = jax.random.key(seed)
    k = jax.random.split(key, 24)
    f32 = jnp.float32
    L = DEPTH

    def nrm(kk, shape, fan_in):
        return jax.random.normal(kk, shape, f32) * (fan_in ** -0.5)

    def gain(kk, shape):
        return 1.0 + 0.02 * jax.random.normal(kk, shape, f32)

    def small(kk, shape):
        return 0.01 * jax.random.normal(kk, shape, f32)

    return {
        "x": jax.random.normal(k[0], (BATCH, SEQ, D_MODEL), f32),
        "mem": jax.random.normal(k[1], (BATCH, MEM_LEN, D_MODEL), f32),
        "norm_mix": gain(k[2], (L, D_MODEL)),
        "w_in": nrm(k[3], (L, D_MODEL, IN_COLS_2), D_MODEL),
        "nsa_qk_norm": gain(k[4], (L, 4, HEAD_DIM)),
        "cmp_pos": 2.0 * small(k[5], (L, 2, CMP_BLOCK, HEAD_DIM)),
        "cmp_w1": nrm(k[6], (L, 2, CMP_BLOCK * HEAD_DIM, CMP_HIDDEN), CMP_BLOCK * HEAD_DIM),
        "cmp_w2": nrm(k[7], (L, 2, CMP_HIDDEN, HEAD_DIM), CMP_HIDDEN),
        "w_nsa_out": nrm(k[8], (L, NSA_WIDTH, D_MODEL), NSA_WIDTH),
        "conv_w": nrm(k[9], (L, CONV_KSIZE, 1, CONV_WIDTH_2), CONV_KSIZE),
        "conv_b": small(k[10], (L, CONV_WIDTH_2)),
        "conv_ln_g": gain(k[11], (L, CONV_WIDTH_2)),
        "conv_ln_b": small(k[12], (L, CONV_WIDTH_2)),
        "w_conv_out": nrm(k[13], (L, CONV_WIDTH_2, D_MODEL), CONV_WIDTH_2),
        "norm_mem": gain(k[14], (L, D_MODEL)),
        "w_mem_kv": nrm(k[15], (L, D_MODEL, 2 * MEM_WIDTH), D_MODEL),
        "mem_qk_norm": gain(k[16], (L, 2, MEM_HEAD_DIM)),
        "w_mem_out": nrm(k[17], (L, MEM_WIDTH, D_MODEL), MEM_WIDTH),
        "w_out": nrm(k[18], (L, D_MODEL, D_MODEL), D_MODEL),
        "norm_ffn": gain(k[19], (L, D_MODEL)),
        "w_gate": nrm(k[20], (L, D_MODEL, D_FF_2), D_MODEL),
        "w_up": nrm(k[21], (L, D_MODEL, D_FF_2), D_MODEL),
        "w_down": nrm(k[22], (L, D_FF_2, D_MODEL), D_FF_2),
    }

def second_block(x, mem, norm_mix, w_in, nsa_qk_norm, cmp_pos, cmp_w1, cmp_w2, w_nsa_out,
              conv_w, conv_b, conv_ln_g, conv_ln_b, w_conv_out, norm_mem, w_mem_kv,
              mem_qk_norm, w_mem_out, w_out, norm_ffn, w_gate, w_up, w_down):
    h = x
    for l in range(DEPTH):
        h = hybrid_layer(h, mem, norm_mix[l], w_in[l], nsa_qk_norm[l], cmp_pos[l], cmp_w1[l], cmp_w2[l],
                         w_nsa_out[l], conv_w[l], conv_b[l], conv_ln_g[l], conv_ln_b[l], w_conv_out[l],
                         norm_mem[l], w_mem_kv[l], mem_qk_norm[l], w_mem_out[l], w_out[l], norm_ffn[l],
                         w_gate[l], w_up[l], w_down[l])
    return h


def setup_inputs(seed=0):
    out = dict(first_inputs(seed))
    for name, value in second_inputs(seed + 1).items():
        if name != "x":
            out[name + "_2"] = value
    return out


def reference(
    x, p, positions, w_in, g_pre_mix, g_q_lat, w_q_up, g_kv_lat, w_kv_up, g_grp_sb, g_grp_mla,
    w_o, g_post_mix, g_pre_ffn, w_up, conv_w, conv_b, w_down, g_post_ffn, w_ple, g_ple_gate,
    w_ple_gate, b_ple_gate, g_post_ple, mem_2, norm_mix_2, w_in_2, nsa_qk_norm_2, cmp_pos_2,
    cmp_w1_2, cmp_w2_2, w_nsa_out_2, conv_w_2, conv_b_2, conv_ln_g_2, conv_ln_b_2, w_conv_out_2,
    norm_mem_2, w_mem_kv_2, mem_qk_norm_2, w_mem_out_2, w_out_2, norm_ffn_2, w_gate_2, w_up_2,
    w_down_2,
):
    x = first_block(
        x, p, positions, w_in, g_pre_mix, g_q_lat, w_q_up, g_kv_lat, w_kv_up, g_grp_sb,
        g_grp_mla, w_o, g_post_mix, g_pre_ffn, w_up, conv_w, conv_b, w_down, g_post_ffn, w_ple,
        g_ple_gate, w_ple_gate, b_ple_gate, g_post_ple,
    )
    return second_block(
        x, mem_2, norm_mix_2, w_in_2, nsa_qk_norm_2, cmp_pos_2, cmp_w1_2, cmp_w2_2, w_nsa_out_2,
        conv_w_2, conv_b_2, conv_ln_g_2, conv_ln_b_2, w_conv_out_2, norm_mem_2, w_mem_kv_2,
        mem_qk_norm_2, w_mem_out_2, w_out_2, norm_ffn_2, w_gate_2, w_up_2, w_down_2,
    )


_drawn_inputs = setup_inputs


def setup_inputs(seed=0):
    import zlib

    import numpy as np

    out = dict(_drawn_inputs(seed))
    spreads = {}
    factors = {'conv_b': 7.264,
     'g_ple_gate': 5.782,
     'b_ple_gate': 8.0,
     'norm_mix_2': 8.0,
     'nsa_qk_norm_2': 8.0,
     'cmp_pos_2': 23.732,
     'conv_b_2': 42.63,
     'conv_ln_g_2': 36.495,
     'conv_ln_b_2': 64.0,
     'norm_mem_2': 8.0,
     'mem_qk_norm_2': 8.0,
     'norm_ffn_2': 6.423}
    for name, (base, spread) in spreads.items():
        noise = np.random.default_rng([zlib.crc32(name.encode()), seed]).standard_normal(out[name].shape)
        drawn = base * np.exp(spread * noise) if base else spread * noise
        out[name] = __import__('jax').numpy.asarray(drawn.astype(out[name].dtype))
    for name, factor in factors.items():
        out[name] = (out[name] * factor).astype(out[name].dtype)
    return out
```

```python
import math
from contextlib import ExitStack

import numpy as np

import concourse.bass as bass
from concourse import mybir

F32 = mybir.dt.float32
F32R = mybir.dt.float32r
BF16 = mybir.dt.bfloat16
I32 = mybir.dt.int32
ALU = mybir.AluOpType
ACT = mybir.ActivationFunctionType
AX = mybir.AxisListType

P = 128
S = 256
D = 1024
DC = D // P
QT = S // P
HEADS = 8
DH = 64
ROPE = 32
FF = 2816
FC = FF // P
KSIZE = 31
MEMH = 4
CMP = 15
CSTEP = 16
EPS = 1e-6
LN_EPS = 1e-5
NEG = -1e30

BPT = 8
TILE = BPT * P
NRAW = 3
NSPLIT = 6
NBANK = 3

STAGES = [
    ("lat", 8, 4, "fm"), ("sbq", 8, 4, "fm"), ("sbk", 8, 4, "fm"), ("sbv", 8, 4, "tm"),
    ("qup", 2, 8, "fm"), ("kup", 1, 4, "fm"), ("vup", 1, 4, "tm"),
    ("memk", 8, 4, "fm"), ("memv", 8, 4, "tm"),
    ("wo", 8, 8, "fm"), ("up", 8, 2 * FC, "fm"), ("down", FC, 8, "fm"),
    ("ple", 2, 8, "fm"), ("gate", 8, 8, "fm"),
    ("kv2", 8, 4, "fm"), ("q2", 8, 4, "fm"), ("tm2", 8, 3, "tm"), ("conv2", 8, 8, "fm"), ("qmem", 8, 4, "fm"),
    ("cmpk", 16, 2, "fm"), ("cmpv", 16, 2, "fm"),
    ("brmem", 12, 8, "fm"), ("brconv", 12, 8, "fm"), ("brnsa", 12, 8, "fm"),
    ("wout", 8, 8, "fm"), ("up2", 8, 2 * FC, "fm"), ("down2", FC, 8, "fm"),
]
FIRST = {}
KC = {}
_b = 0
for _n, _k, _m, _o in STAGES:
    FIRST[_n], KC[_n] = _b, _k
    _b += _k * _m
NTILES = _b // BPT
assert _b % BPT == 0


def outputs():
    out = [("stat", "h1")]
    out += [("lat", m) for m in range(4)]
    out += [("sbq", 0), ("sbq", 1), ("stat", "qlat"), ("stat", "kvlat"), ("sbq", 2), ("sbq", 3)]
    out += [("sbk", m) for m in range(4)] + [("stat", "mem"), ("sbv", 0), ("sbv", 1)]
    out += [("qup", m) for m in range(8)] + [("kup", m) for m in range(4)] + [("vup", 0), ("vup", 1)]
    out += [("memk", m) for m in range(4)] + [("memv", 0), ("memv", 1)] + [("stat", "memk0"), ("stat", "memk1")]
    out += [("wo", m) for m in range(8)] + [("stat", "postmix"), ("stat", "preffn")]
    out += [("up", m) for m in range(2 * FC)] + [("down", m) for m in range(8)]
    out += [("ple", m) for m in range(2)] + [("stat", "postffn")] + [("ple", m) for m in range(2, 4)]
    out += [("ple", m) for m in range(4, 8)] + [("stat", "plegate")]
    out += [("gate", m) for m in range(8)] + [("stat", "postple"), ("stat", "mix2")]
    out += [("kv2", m) for m in range(4)] + [("q2", 0), ("q2", 1)] + [("stat", "ks"), ("stat", "kw")]
    out += [("q2", 2), ("q2", 3)] + [("tm2", 0), ("tm2", 1)] + [("stat", "q0"), ("stat", "q1")]
    out += [("conv2", m) for m in range(8)] + [("qmem", m) for m in range(4)]
    out += [("cmpk", 0), ("cmpk", 1), ("stat", "qm0"), ("stat", "qm1"), ("cmpv", 0), ("cmpv", 1)]
    out += [("stat", "kcT"), ("stat", "vc"), ("stat", "kc")]
    for br in ("brmem", "brconv", "brnsa"):
        for m in range(8):
            out += [(br + "g", m), (br, m)]
            if br == "brmem" and m >= 6:
                out += [("stat", ("lnmean", "lnvar")[m - 6])]
    out += [("wout", m) for m in range(8)] + [("stat", "ffn2")]
    out += [("up2", m) for m in range(2 * FC)] + [("down2", m) for m in range(8)]
    return out


OUTS = outputs()
OUT = {o: i for i, o in enumerate(OUTS)}
TM = {n for n, _, _, o in STAGES if o == "tm"}
BLOCKS = {n: k * m for n, k, m, _ in STAGES}


def last_block(o):
    name, m = o
    if name == "stat" or (name in TM and m == 0):
        return None
    if name in TM:
        return FIRST[name] + BLOCKS[name] - 1
    if name[:2] == "br":
        return FIRST[name.removesuffix("g")] + 12 * m + (7 if name.endswith("g") else 11)
    return FIRST[name] + (m + 1) * KC[name] - 1


Y_COUNT, _c = {}, 0
for _o in OUTS:
    _l = last_block(_o)
    if _l is None or _l % BPT != BPT - 1:
        _c += 1
        Y_COUNT[_o] = _c

PLAIN_STATS = ("kcT", "vc", "lnmean")
FREE_COUNT, _c = {}, [0] * NBANK
for _i, _o in enumerate(OUTS):
    if _o[0] != "stat" or _o[1] in PLAIN_STATS:
        _c[_i % NBANK] += 1
        FREE_COUNT[_o] = _c[_i % NBANK]

S_USES = ([("sb", u) for u in range(4)] + [("mla", u) for u in range(4)] + [("mem", u) for u in range(2)]
          + [("cmp", u) for u in range(2)] + [("slc", u) for u in range(4)] + [("win", u) for u in range(4)])
T_USES = [("cum", 0)]
for _u in range(1, 4):
    T_USES += [("cum", _u), ("mla", _u - 1)]
T_USES += [("mla", 3), ("osb", 0), ("omla", 0), ("mem", 0), ("mem", 1), ("omem", 0)]
T_USES += [("cmp", u) for u in range(2)] + [("slc", u) for u in range(4)] + [("win", u) for u in range(4)]
T_USES += [("onsa", 0)]
O_USES = [("sb", 0), ("mla", 0), ("sb", 1), ("mla", 1), ("sb", 2), ("mla", 2), ("sb", 3), ("mla", 3)]
O_USES += [u for u in S_USES if u[0] in ("mem", "cmp", "slc", "win")]
T_COUNT, _c = {}, 0
for _u in T_USES:
    if _u[0] not in ("osb", "omla", "omem", "onsa"):
        _c += 1
        T_COUNT[_u] = _c
SU = {u: i for i, u in enumerate(S_USES)}
TU = {u: i for i, u in enumerate(T_USES)}
OU = {u: i for i, u in enumerate(O_USES)}
UNITS = [u for u in S_USES if u[0] != "sb"]
UI = {u: i for i, u in enumerate(UNITS)}

UNITS2 = UNITS[4:]
FILL = {3: [("brmem", 0)], 4: [("brmem", 1)], 5: [("brmem", 2), ("brmem", 3)], 6: [("brmem", 4)],
        7: [("brmem", 5), ("brmem", 6), ("stat", "lnmean")], 8: [("brmem", 7), ("stat", "lnvar")],
        9: [("brconv", 0)], 10: [("brconv", 1), ("brconv", 2)], 11: [("brconv", 3)]}
FILL_TURNED = [("brconv", 4), ("brconv", 5)]
FILL_OUT = [("brconv", 6), ("brconv", 7)]

CONSTS = [
    ("g_pre_mix", 8), ("g_q_lat", 2), ("g_kv_lat", 1), ("g_grp_sb", 4), ("g_grp_mla", 4), ("g_post_mix", 8),
    ("g_pre_ffn", 8), ("conv_w", 3 * 2 * FC), ("conv_b", 2 * FC), ("g_post_ffn", 8), ("g_ple_gate", 8),
    ("b_ple_gate", 8), ("g_post_ple", 8), ("norm_mix_2", 8), ("nsa_qk_norm_2", 4), ("cmp_pos_2", 32),
    ("conv_w_2", 4 * KSIZE), ("conv_b_2", 4), ("conv_ln_g_2", 4), ("conv_ln_b_2", 4), ("norm_mem_2", 8),
    ("mem_qk_norm_2", 2), ("norm_ffn_2", 8), ("freq", 1), ("sign", 1),
]
COL, _c = {}, 0
for _n, _w in CONSTS:
    COL[_n] = _c
    _c += _w
NCONST = _c


MEM_SCALE = P ** -0.5
BIAS_STEP = 6


def bases(pairs):
    out, c = {}, 0
    for name, n in pairs:
        out[name] = c
        c += n
    return out


NORMS = [("h1", 8), ("qlat", 2), ("kvlat", 1), ("mem", 8), ("memk0", 2), ("memk1", 2), ("postmix", 8),
         ("preffn", 8), ("postffn", 8), ("plegate", 8), ("postple", 8), ("mix2", 8), ("ks", 2), ("kw", 2),
         ("q0", 2), ("q1", 2), ("qm0", 2), ("qm1", 2), ("kc", 1), ("lnvar", 4), ("ffn2", 8)]
SQ0 = bases(NORMS)
RT_ORDER = ["h1", "qlat", "kvlat", "mem", "memk0", "memk1", "osb", "omla", "postmix", "preffn", "postffn", "plegate",
            "postple", "mix2", "ks", "kw", "q0", "q1", "qm0", "qm1", "kc", "lnvar", "ffn2"]
RT = {n: i for i, n in enumerate(RT_ORDER)}
TN0 = bases([("h1", 4), ("ql", 1), ("kvl", 1), ("mem", 4), ("ffn", 4), ("ph", 4), ("xn2", 4), ("hf", 4)])
SPLITS = [("h1", 8), ("ql", 2), ("kvl", 1), ("mem", 8), ("o", 8), ("ffn", 8), ("a", FC), ("p", 2), ("ph", 8),
          ("xn2", 8), ("bk", 1), ("bv", 1), ("om", 4), ("cv", 4), ("on", 4), ("y", 8), ("hf", 8), ("a2", FC)]
SP0 = bases(SPLITS)
X0 = bases([("postmix", 4), ("postffn", 4), ("postple", 4), ("wout", 8), ("final", 8)])
O_SPLIT = {"osb": SP0["o"], "omla": SP0["o"] + 4, "omem": SP0["om"], "onsa": SP0["on"]}


def program(nc, stream, xT, memT, pT, pos, consts, w2, out):
    ctx = ExitStack()
    with ctx:
        def sb(name, shape, dt=F32):
            return ctx.enter_context(nc.sbuf_tensor(name, shape, dt))

        def sem(name):
            return ctx.enter_context(nc.semaphore(name))

        raw = sb("raw", [P, NRAW, TILE])
        whi = sb("whi", [P, NSPLIT, TILE], F32R)
        wlo = sb("wlo", [P, NSPLIT, TILE], F32R)
        CV = sb("CV", [P, NCONST])
        X = sb("X", [P, DC, S])
        Y = sb("Y", [P, DC, S])
        SQ = sb("SQ", [P, DC, S])
        HA = sb("HA", [P, DC, 2 * S], F32R)
        HB = sb("HB", [P, DC, 2 * S], F32R)
        HL = sb("HL", [P, 4, 2 * S], F32R)
        KMEM = sb("KMEM", [P, MEMH, S])
        VMEM = sb("VMEM", [P, QT, 512])
        RTT = sb("RTT", [P, 2 * S])
        RS = sb("RS", [P, 2 * S])
        ident = sb("ident", [P, P])
        ones = sb("ones", [P, P])
        ones64 = sb("ones64", [P, P])
        lower = sb("lower", [P, P])
        strict = sb("strict", [P, P])
        identb = sb("identb", [P, P], BF16)
        causalb = sb("causalb", [P, P], BF16)
        cmpb = sb("cmpb", [P, QT, CMP], BF16)
        valid = sb("valid", [P, QT])
        eps = sb("eps", [P, 2])
        hbp = sb("hbp", [P, 8])
        negstrict = sb("negstrict", [P, P])
        mx = sb("mx", [P, 2, 8])
        sums = sb("sums", [P, 2, 8])
        rsum = sb("rsum", [P, 2, 8])
        ssq = sb("ssq", [P, 2, QT])
        srt = sb("srt", [P, 2, QT])
        rst = sb("rst", [P, 2, QT])

        def region(*tensors):
            with ExitStack() as stack:
                return [stack.enter_context(nc.sbuf_tensor(n, s, d)) for n, s, d in tensors]

        (EE,) = region(("EE", [P, DC, S], F32))
        ACTS, YC, G1, PX = region(("ACTS", [P, FC, 2 * S], F32R), ("YC", [P, 2, 2, S], F32), ("G1", [P, 2, 2, S], F32),
                                  ("PX", [P, 2, S], F32))
        (COS, SIN, QS, KS1, VS1, QM, KM, VM, Z, OSB, OMLA, E0) = region(
            ("COS", [P, S], F32), ("SIN", [P, S], F32), ("QS", [P, 4, S], F32), ("KS1", [P, 4, S], F32),
            ("VS1", [P, QT, 512], F32), ("QM", [P, HEADS, S], F32), ("KM", [P, HEADS, S], F32),
            ("VM", [P, QT, 512], F32), ("Z", [P, HEADS, 384], F32), ("OSB", [P, QT, 512], F32),
            ("OMLA", [P, QT, 512], F32), ("E0", [P, HEADS, 384], F32))
        (QN, KSD, KWD, S2, TB, BS, G2, KCD, VC, VS2, GN, QME, U, CY, PR2, ONSA, OMEM, TH, W2) = region(
            ("QN", [P, 4, S], F32), ("KSD", [P, 2, S], F32), ("KWD", [P, 2, S], F32),
            ("S2", [P, 2, 2, S], F32), ("TB", [P, 2, 16, 2 * CMP], F32), ("BS", [P, 2, 2, 16, 2 * CMP], F32R),
            ("G2", [P, 2, 2, 2 * CMP], F32), ("KCD", [P, 2 * CMP], F32), ("VC", [P, 2, DH], F32),
            ("VS2", [P, QT, 280], F32), ("GN", [P, QT, 24], F32), ("QME", [P, MEMH, S], F32),
            ("U", [P, 4, S], F32), ("CY", [P, 4, S], F32), 
            ("PR2", [P, 2, 1024], F32), ("ONSA", [P, QT, 512], F32),
            ("OMEM", [P, QT, 512], F32), ("TH", [P, 2, S], F32), ("W2", [P, 384], F32))

        PROD = ctx.enter_context(nc.psum_tensor("PROD", [P, NBANK, 512], F32))
        SC = ctx.enter_context(nc.psum_tensor("SC", [P, 1024], F32))
        TP = ctx.enter_context(nc.psum_tensor("TP", [P, 1024], F32))
        OP = ctx.enter_context(nc.psum_tensor("OP", [P, 512], F32))
        PR1 = Y[:, :, :].rearrange("p c s -> p (c s)").rearrange("p (b n) -> p b n", b=2)
        MEMX = E0[:, :, :].rearrange("p h n -> p (h n)")[:, 0:DC * S].rearrange("p (c s) -> p c s", c=DC)
        PT = SQ[:, 4:8, :].rearrange("p c s -> p (c s)")

        consts_in = sem("consts_in")
        x_in = sem("x_in")
        mem_in = sem("mem_in")
        p_in = sem("p_in")
        pos_in = sem("pos_in")
        raw_in = [sem(f"raw_in{i}") for i in range(NRAW)]
        masks = sem("masks")
        hi_done = sem("hi_done")
        lo_vector = sem("lo_vector")
        lo_pool = sem("lo_pool")
        w_used = sem("w_used")
        y_done = sem("y_done")
        y_free = [sem(f"y_free{i}") for i in range(NBANK)]
        sq_ready = sem("sq_ready")
        rt_ready = sem("rt_ready")
        rs_ready = sem("rs_ready")
        tn_ready = sem("tn_ready")
        a_hi = sem("a_hi")
        a_lo = sem("a_lo")
        x_ready = sem("x_ready")
        angles = sem("angles")
        sincos = sem("sincos")
        s_ready = sem("s_ready")
        sb_z = sem("sb_z")
        sb_e = sem("sb_e")
        sb_l = sem("sb_l")
        sb_sp = sem("sb_sp")
        sb_arg = sem("sb_arg")
        sb_a = sem("sb_a")
        mx_ready = sem("mx_ready")
        p_ready = sem("p_ready")
        t_ready = sem("t_ready")
        t_free = sem("t_free")
        o_ready = sem("o_ready")
        o_free = sem("o_free")
        o_normed = sem("o_normed")
        conv0 = sem("conv0")
        gelu_done = sem("gelu_done")
        act_out = sem("act_out")
        ge_ready = sem("ge_ready")
        bias_half = sem("bias_half")
        th_done = sem("th_done")
        w2_in = sem("w2_in")
        ln_biased = sem("ln_biased")
        ln_centred = sem("ln_centred")
        ln_scaled = sem("ln_scaled")
        ln_z = sem("ln_z")
        silu_done = sem("silu_done")
        cmp_sum = sem("cmp_sum")
        conv_u = sem("conv_u")
        conv_end = sem("conv_end")
        gate_in = sem("gate_in")
        gate_th = sem("gate_th")
        attn_in = sem("attn_in")
        onsa_done = sem("onsa_done")
        th_used = sem("th_used")
        vchain = sem("vchain")
        schain = sem("schain")
        pchain = sem("pchain")
        stored = sem("stored")

        def split_wait(eng, n):
            if n % 2:
                eng.wait_ge(lo_vector, n // 2 + 1)
            else:
                eng.wait_ge(lo_pool, n // 2 + 1)

        def product(o):
            return PROD[:, OUT[o] % NBANK, :]

        def wait_product(eng, o):
            last = last_block(o)
            if last is not None and last % BPT == BPT - 1:
                eng.wait_ge(w_used, last // BPT + 1)
            else:
                eng.wait_ge(y_done, Y_COUNT[o])

        def free(o):
            return y_free[OUT[o] % NBANK]

        def wait_freed(eng, o):
            if o in FREE_COUNT:
                eng.wait_ge(y_free[OUT[o] % NBANK], FREE_COUNT[o])
            else:
                eng.wait_ge(rs_ready, RT[o[1]] + 1)

        def wait_turned(eng, use):
            if use[0] in O_SPLIT:
                eng.wait_ge(a_lo, O_SPLIT[use[0]] + 4)
            else:
                eng.wait_ge(t_free, T_COUNT[use])

        def end_tile(o):
            last = last_block(o)
            return -1 if last is None else (last + 1) // BPT - 1

        def unit_shape(unit):
            kind, u = unit
            if kind == "mem":
                return 4, S, QT, u, 0
            if kind == "cmp":
                return HEADS, CMP, 1, u, 0
            return 4, P * (u // 2 + 1), u // 2 + 1, u // 2, 4 * (u % 2)

        def score_at(kind, j):
            if kind in ("mla", "mem"):
                return j * S
            return j % 2 * 512 + j // 2 * (CMP if kind == "cmp" else S)

        block = ctx.enter_context(nc.Block())

        @block.sync
        def _(sp):
            sp.dma_start(X[:, :, :], xT).then_inc(x_in, 16)
            sp.dma_start(CV[:, :], consts).then_inc(consts_in, 16)
            for n in range(NTILES):
                if n >= NRAW:
                    split_wait(sp, n - NRAW)
                sp.dma_start(raw[:, n % NRAW, :], stream[n]).then_inc(raw_in[n % NRAW], 16)
                if n == 1:
                    sp.dma_start(Y[:, 1, :].bitcast(I32), pos).then_inc(pos_in, 16)
                if n == 6:
                    sp.dma_start(MEMX, memT).then_inc(mem_in, 16)
                if n == FIRST["up"] // BPT + NSPLIT + NRAW + 2:
                    sp.dma_start(PX[:, :, :], pT).then_inc(p_in, 16)

                if n == FIRST["kv2"] // BPT + NSPLIT + NRAW + 2:
                    sp.dma_start(W2[:, :], w2).then_inc(w2_in, 16)
            for m in range(8):
                wait_freed(sp, ("down2", m))
                sp.dma_start(out[:, m, :], X[:, m, :]).then_inc(stored, 16)
            sp.wait_ge(stored, 8 * 16)

        @block.gpsimd
        def _(pool):
            fills = [(ident, 0.0), (ones, 1.0), (ones64, 0.0), (lower, 1.0), (strict, 1.0), (negstrict, 0.0),
                     (causalb, 0.0), (cmpb, 0.0), (valid, 1.0)]
            for t, value in fills:
                nc.gpsimd.memset(t[:], value).then_inc(pchain, 1)
            nc.gpsimd.memset(eps[:, 0:1], EPS).then_inc(pchain, 1)
            nc.gpsimd.memset(eps[:, 1:2], LN_EPS).then_inc(pchain, 1)
            pool.wait_ge(pchain, 11)
            nc.gpsimd.memset(ones64[0:64, 0:64], 1.0).then_inc(pchain, 1)
            nc.gpsimd.memset(ones64[64:128, 64:128], 1.0).then_inc(pchain, 1)
            pool.wait_ge(pchain, 13)

            def select(t, op, fill, base, pattern, mult):
                nc.gpsimd.affine_select(out=t, in_=t, compare_op=op, fill=fill, base=base, pattern=pattern,
                                        channel_multiplier=mult).then_inc(pchain, 1)

            select(ident[:, :], ALU.not_equal, 1.0, 0, [[-1, P]], 1)
            select(lower[:, :], ALU.is_ge, 0.0, 0, [[-1, P]], 1)
            select(strict[:, :], ALU.is_gt, 0.0, 0, [[1, P]], -1)
            select(negstrict[:, :], ALU.is_gt, NEG, 0, [[1, P]], -1)
            select(causalb[:, :], ALU.is_ge, NEG, 0, [[-1, P]], 1)
            for qt in range(QT):
                select(cmpb[:, qt, :], ALU.is_ge, NEG, qt * P - 31, [[-CSTEP, CMP]], 1)
            select(valid[:, 0:1], ALU.is_ge, 0.0, -31, [[0, 1]], 1)
            pool.wait_ge(pchain, 21)
            nc.gpsimd.tensor_copy(identb[:, :], ident[:, :]).then_inc(masks, 1)
            for n in range(0, NTILES, 2):
                pool.wait_ge(hi_done, n + 1)
                nc.gpsimd.tensor_tensor(wlo[:, n % NSPLIT, :], raw[:, n % NRAW, :],
                                        whi[:, n % NSPLIT, :].bitcast(F32), ALU.subtract).then_inc(lo_pool, 1)

        @block.tensor
        def _(pe):
            def begin(o):
                if OUT[o] >= NBANK:
                    wait_freed(pe, OUTS[OUT[o] - NBANK])
                return product(o)

            def blk3(dst, b, hi, lo, start, stop, ends):
                n, i = divmod(b, BPT)
                if i == 0:
                    split_wait(pe, n)
                wh = whi[:, n % NSPLIT, i * P:(i + 1) * P]
                wl = wlo[:, n % NSPLIT, i * P:(i + 1) * P]
                nc.tensor.matmul(dst, wh, hi, start=start, stop=False, skip_group_check=True)
                nc.tensor.matmul(dst, wl, hi, start=False, stop=False, skip_group_check=True)
                last = nc.tensor.matmul(dst, wh, lo, start=False, stop=stop, skip_group_check=True)
                if i == BPT - 1:
                    last.then_inc(w_used, 1)
                elif ends:
                    last.then_inc(y_done, 1)

            def fm(stage, m, H, need=None, base=0):
                k = KC[stage]
                dst = begin((stage, m))[:, 0:S]
                for c in range(k):
                    if need is not None:
                        pe.wait_ge(a_lo, need + c + 1)
                    blk3(dst, FIRST[stage] + m * k + c, H[:, base + c, 0:S], H[:, base + c, S:2 * S],
                         c == 0, c == k - 1, c == k - 1)

            def tm(stage, cols, H, need=None, base=0, ks=None):
                m = BLOCKS[stage] // KC[stage]
                ks = range(KC[stage]) if ks is None else ks
                if ks[0] == 0:
                    begin((stage, 0)), begin((stage, 1))
                for c in ks:
                    if need is not None:
                        pe.wait_ge(a_lo, need + c + 1)
                    b = FIRST[stage] + c * m
                    end = b + m
                    while b < end:
                        n, i = divmod(b, BPT)
                        if i == 0:
                            split_wait(pe, n)
                        run = min(end - b, BPT - i)
                        at = (b - FIRST[stage] - c * m) * P
                        w = min(run * P, cols - at)
                        wh = whi[:, n % NSPLIT, i * P:i * P + w]
                        wl = wlo[:, n % NSPLIT, i * P:i * P + w]
                        for qt in range(QT):
                            dst = product((stage, qt))[:, at:at + w]
                            hi = H[:, base + c, qt * P:(qt + 1) * P]
                            lo = H[:, base + c, S + qt * P:S + (qt + 1) * P]
                            end_all = c == KC[stage] - 1 and b + run == end
                            nc.tensor.matmul(dst, hi, wh, start=c == 0 and at == 0, stop=False, skip_group_check=True)
                            nc.tensor.matmul(dst, hi, wl, start=False, stop=False, skip_group_check=True)
                            last = nc.tensor.matmul(dst, lo, wh, start=False, stop=end_all, skip_group_check=True)
                            if qt == 0 and end_all:
                                last.then_inc(y_done, 1)
                        if i + run == BPT:
                            last.then_inc(w_used, 1)
                        b += run

            def stat(name, chunks, mat=ones, wide=False, ready=None):
                dst = begin(("stat", name))
                if wide:
                    pe.wait_ge(sq_ready, SQ0[name] + 2)
                    nc.tensor.matmul(dst, mat[:, :], chunks, start=True, stop=True).then_inc(y_done, 1)
                    return
                for i, c in enumerate(chunks):
                    pe.wait_ge(sq_ready, SQ0[name] + i + 1)
                    w = 2 * CMP if name == "kc" else S
                    last = nc.tensor.matmul(dst[:, 0:w], mat[:, :], c[:, 0:w], start=i == 0, stop=i == len(chunks) - 1)
                last.then_inc(y_done, 1)

            def s_begin(use):
                i = SU[use]
                if i:
                    kind, u = S_USES[i - 1]
                    if kind == "sb":
                        pe.wait_ge(sb_z, u + 1)
                    else:
                        pe.wait_ge(p_ready, UI[(kind, u)] + 1)

            def t_begin(use):
                if TU[use]:
                    wait_turned(pe, T_USES[TU[use] - 1])

            def o_begin(use):
                if OU[use]:
                    pe.wait_ge(o_free, OU[use])

            def sb_scores(u):
                s_begin(("sb", u))
                for j in range(2):
                    at = slice(64 * j, 64 * j + 64)
                    nc.tensor.matmul(SC[:, 512 * j:512 * j + S], KS1[at, u, 0:P], QS[at, u, :],
                                     start=True, stop=True, skip_group_check=True)
                    last = nc.tensor.matmul(SC[:, 512 * j + S:512 * j + 384], KS1[at, u, P:S], QS[at, u, P:S],
                                            start=True, stop=True, skip_group_check=True)
                last.then_inc(s_ready, 1)

            def sb_cum(u):
                pe.wait_ge(sb_sp, u + 1)
                t_begin(("cum", u))
                for j in range(2):
                    c, h = 512 * j, 2 * u + j
                    nc.tensor.matmul(TP[:, c:c + S], lower[:, :], E0[:, h, 0:S], start=True, stop=False,
                                     skip_group_check=True)
                    nc.tensor.matmul(TP[:, c + P:c + S], ones[:, :], E0[:, h, S:384], start=False, stop=True,
                                     skip_group_check=True)
                    last = nc.tensor.matmul(TP[:, c + S:c + 384], lower[:, :], E0[:, h, S:384], start=True, stop=True,
                                            skip_group_check=True)
                last.then_inc(t_ready, 1)

            def sb_pv(u):
                pe.wait_ge(sb_a, u + 1)
                o_begin(("sb", u))
                for j in range(2):
                    h = 2 * u + j
                    v = slice(h * DH, (h + 1) * DH)
                    o0 = OP[:, j * DH:(j + 1) * DH]
                    o1 = OP[:, P + j * DH:P + (j + 1) * DH]
                    nc.tensor.matmul(o0, Z[:, h, 0:P], VS1[:, 0, v], start=True, stop=True, skip_group_check=True)
                    nc.tensor.matmul(o1, Z[:, h, P:S], VS1[:, 0, v], start=True, stop=False, skip_group_check=True)
                    last = nc.tensor.matmul(o1, Z[:, h, S:384], VS1[:, 1, v], start=False, stop=True,
                                            skip_group_check=True)
                last.then_inc(o_ready, 1)

            def scores(unit):
                kind, u = unit
                nh, kw, nkb, qt, h0 = unit_shape(unit)
                s_begin(unit)
                q = slice(qt * P, (qt + 1) * P)
                for j in range(nh):
                    h = h0 + j
                    half = slice(64 * (h % 2), 64 * (h % 2) + 64)
                    at = score_at(kind, j)
                    if kind == "mla":
                        a, b = QM[0:96, h, q], KM[0:96, h, 0:kw]
                    elif kind == "mem":
                        a, b = QME[:, h, q], KMEM[:, h, 0:kw]
                    elif kind == "cmp":
                        a, b = QN[half, h // 2, q], KCD[half, (h // 4) * CMP:(h // 4 + 1) * CMP]
                    else:
                        a, b = QN[half, h // 2, q], (KSD if kind == "slc" else KWD)[half, h // 4, 0:kw]
                    last = nc.tensor.matmul(SC[:, at:at + kw], a, b, start=True, stop=kind == "mem",
                                            skip_group_check=True)
                    if kind == "cmp":
                        last = nc.tensor.matmul(SC[:, at:at + kw], identb[:, :], cmpb[:, qt, :], start=False,
                                                stop=True, skip_group_check=True)
                    elif kind != "mem":
                        last = nc.tensor.matmul(SC[:, at + kw - P:at + kw], identb[:, :], causalb[:, :], start=False,
                                                stop=True, skip_group_check=True)
                last.then_inc(s_ready, 1)

            def turn(unit, PR):
                nh, kw, nkb, qt, h0 = unit_shape(unit)
                pe.wait_ge(p_ready, UI[unit] + 1)
                t_begin(unit)
                b = UI[unit] % 2
                for j in range(nh):
                    for kb in range(nkb):
                        w = min(P, kw)
                        i = j * nkb + kb
                        last = nc.tensor.transpose(TP[0:w, i * P:(i + 1) * P],
                                                   PR[:, b, j * kw + kb * P:j * kw + kb * P + w], ident[:, :])
                last.then_inc(t_ready, 1)

            def pv(unit):
                kind, u = unit
                nh, kw, nkb, qt, h0 = unit_shape(unit)
                wait_turned(pe, unit)
                o_begin(unit)
                w = min(P, kw)
                for j in range(nh):
                    h = h0 + j
                    dv = P if kind == "mem" else DH
                    for kb in range(nkb):
                        if kind == "mla":
                            v = VM[:, kb, h * DH:(h + 1) * DH]
                        elif kind == "mem":
                            v = VMEM[:, kb, h * P:(h + 1) * P]
                        elif kind == "cmp":
                            v = VC[0:CMP, h // 4, :]
                        else:
                            c = (P if kind == "win" else 0) + (h // 4) * DH
                            v = VS2[:, kb, c:c + DH]
                        i = j * nkb + kb
                        last = nc.tensor.matmul(OP[:, j * dv:(j + 1) * dv], PT[0:w, i * P:(i + 1) * P], v,
                                                start=kb == 0, stop=kb == nkb - 1, skip_group_check=True)
                last.then_inc(o_ready, 1)

            def turn_out(use, src, ready, count):
                pe.wait_ge(ready, count)
                t_begin(use)
                for c in range(4):
                    for qt in range(QT):
                        last = nc.tensor.transpose(TP[:, c * S + qt * P:c * S + (qt + 1) * P],
                                                   src[:, qt, c * P:(c + 1) * P], ident[:, :])
                last.then_inc(t_ready, 1)

            pe.wait_ge(masks, 1)
            stat("h1", [SQ[:, c, :] for c in range(8)])
            for m in range(4):
                fm("lat", m, HA, SP0["h1"] if m == 0 else None)
            fm("sbq", 0, HA)
            fm("sbq", 1, HA)
            stat("qlat", [SQ[:, c, :] for c in range(2)])
            stat("kvlat", [SQ[:, 2, :]])
            fm("sbq", 2, HA)
            fm("sbq", 3, HA)
            for m in range(4):
                fm("sbk", m, HA)
            stat("mem", [SQ[:, c, :] for c in range(8)])
            tm("sbv", 512, HA)
            for m in range(8):
                fm("qup", m, HL, SP0["ql"] if m == 0 else None)
            for m in range(4):
                fm("kup", m, HL, SP0["kvl"] if m == 0 else None, base=2)
            tm("vup", 512, HL, base=2)
            wait_freed(pe, ("sbk", 3))
            for u in range(4):
                sb_scores(u)
                fm("memk", u, HB, SP0["mem"] if u == 0 else None)
            tm("memv", 512, HB)
            for i in range(2):
                stat(f"memk{i}", SQ[:, 2 * i:2 * i + 2, :].rearrange("p c s -> p (c s)"), wide=True)
            for u in range(4):
                sb_cum(u)
                if u:
                    sb_pv(u - 1)
                    turn(("mla", u - 1), PR1)
                else:
                    wait_freed(pe, ("vup", 1))
                scores(("mla", u))
                if u:
                    pv(("mla", u - 1))
            sb_pv(3)
            turn(("mla", 3), PR1)
            pv(("mla", 3))
            turn_out(("osb", 0), OSB, o_normed, 2)
            turn_out(("omla", 0), OMLA, o_normed, 4)
            for m in range(8):
                fm("wo", m, HA, SP0["o"] if m == 0 else None)
            stat("postmix", [SQ[:, c, :] for c in range(8)])
            stat("preffn", [SQ[:, c, :] for c in range(8)])
            for m in range(2 * FC):
                fm("up", m, HA, SP0["ffn"] if m == 0 else None)
            for m in range(8):
                fm("down", m, ACTS, SP0["a"] if m == 0 else None)
            for m in range(2):
                fm("ple", m, HL, SP0["p"] if m == 0 else None)
            stat("postffn", [SQ[:, c, :] for c in range(8)])
            for m in range(2, 8):
                fm("ple", m, HL)
            stat("plegate", [SQ[:, c, :] for c in range(8)])
            for m in range(8):
                fm("gate", m, HA, SP0["ph"] if m == 0 else None)
            stat("postple", [SQ[:, c, :] for c in range(8)])

            stat("mix2", [SQ[:, c, :] for c in range(8)])

            def pair(i):
                return SQ[:, 2 * i:2 * i + 2, :].rearrange("p c s -> p (c s)")

            for m in range(4):
                fm("kv2", m, HA, SP0["xn2"] if m == 0 else None)
            fm("q2", 0, HA)
            fm("q2", 1, HA)
            stat("ks", pair(0), ones64, wide=True)
            stat("kw", pair(1), ones64, wide=True)
            fm("q2", 2, HA)
            fm("q2", 3, HA)
            tm("tm2", 280, HA)
            stat("q0", pair(2), ones64, wide=True)
            stat("q1", pair(3), ones64, wide=True)
            for m in range(8):
                fm("conv2", m, HA)
            for m in range(4):
                fm("qmem", m, HA)

            def compress(name, kv, m):
                dst = begin((name, m))[:, 0:2 * CMP]
                pe.wait_ge(a_lo, SP0["bk"] + kv + 1)
                for c in range(16):
                    blk3(dst, FIRST[name] + m * 16 + c, BS[:, kv, 0, c, :], BS[:, kv, 1, c, :], c == 0, c == 15,
                         c == 15)

            compress("cmpk", 0, 0)
            compress("cmpk", 0, 1)
            stat("qm0", pair(0), wide=True)
            stat("qm1", pair(1), wide=True)
            compress("cmpv", 1, 0)
            compress("cmpv", 1, 1)
            pe.wait_ge(w2_in, 16)
            wait_freed(pe, ("cmpk", 1))
            dst = begin(("stat", "kcT"))
            for m in range(2):
                last = nc.tensor.matmul(dst[:, 0:2 * CMP], W2[:, m * P:(m + 1) * P], G2[:, 0, m, :], start=m == 0,
                                        stop=m == 1)
            last.then_inc(y_done, 1)
            wait_freed(pe, ("cmpv", 1))
            dst = begin(("stat", "vc"))
            for g in range(2):
                for m in range(2):
                    last = nc.tensor.matmul(dst[0:CMP, g * DH:(g + 1) * DH], G2[:, 1, m, g * CMP:(g + 1) * CMP],
                                            W2[:, 2 * P + m * DH:2 * P + (m + 1) * DH], start=m == 0, stop=m == 1,
                                            skip_group_check=True)
            last.then_inc(y_done, 1)
            stat("kc", [SQ[:, 4, :]], ones64)

            def fill(item):
                name, m = item
                if name == "stat":
                    if m == "lnmean":
                        pe.wait_ge(ln_biased, 4)
                        dst = begin(item)
                        for c in range(4):
                            last = nc.tensor.matmul(dst[:, 0:S], ones[:, :], CY[:, c, :], start=c == 0, stop=c == 3)
                        last.then_inc(y_done, 1)
                    else:
                        stat("lnvar", [SQ[:, c, :] for c in range(4)])
                    return
                H, base, split = {"brmem": (HB, 4, "om"), "brconv": (HB, 0, "cv"), "brnsa": (HL, 0, "on")}[name]
                b = FIRST[name] + 12 * m
                dst = begin((name + "g", m))[:, 0:S]
                for c in range(8):
                    blk3(dst, b + c, HA[:, c, 0:S], HA[:, c, S:2 * S], c == 0, c == 7, c == 7)
                dst = begin((name, m))[:, 0:S]
                for c in range(4):
                    if m == 0:
                        pe.wait_ge(a_lo, SP0[split] + c + 1)
                    blk3(dst, b + 8 + c, H[:, base + c, 0:S], H[:, base + c, S:2 * S], c == 0, c == 3, c == 3)

            pe.wait_ge(attn_in, 1)
            for i, unit in enumerate(UNITS2):
                scores(unit)
                if i:
                    pv(UNITS2[i - 1])
                if i == 2:
                    turn_out(("omem", 0), OMEM, o_free, OU[("mem", 1)] + 1)
                for item in FILL.get(i, []):
                    fill(item)
                turn(unit, PR2)
            for item in FILL_TURNED:
                fill(item)
            pv(UNITS2[-1])
            for item in FILL_OUT:
                fill(item)
            turn_out(("onsa", 0), ONSA, onsa_done, 1)
            for m in range(8):
                fill(("brnsa", m))
            for m in range(8):
                fm("wout", m, HB, SP0["y"] if m == 0 else None)
            stat("ffn2", [SQ[:, c, :] for c in range(8)])
            for m in range(2 * FC):
                fm("up2", m, HA, SP0["hf"] if m == 0 else None)
            for m in range(8):
                fm("down2", m, ACTS, SP0["a2"] if m == 0 else None)

        @block.scalar
        def _(act):
            done = {"hi": 0, "links": 0}

            def link(ins):
                done["links"] += 1
                ins.then_inc(schain, 1)
                act.wait_ge(schain, done["links"])

            def weights(upto):
                while done["hi"] < min(upto, NTILES):
                    n = done["hi"]
                    act.wait_ge(raw_in[n % NRAW], 16 * (n // NRAW + 1))
                    if n >= NSPLIT:
                        act.wait_ge(w_used, n - NSPLIT + 1)
                    nc.scalar.activation(whi[:, n % NSPLIT, :], raw[:, n % NRAW, :], ACT.Copy).then_inc(hi_done, 1)
                    done["hi"] += 1

            def ahead(o):
                weights(end_tile(o) + 1 + NSPLIT)

            def squares(name, c, src, at=None):
                nc.scalar.activation(SQ[:, c if at is None else at, :], src, ACT.Square).then_inc(sq_ready, 1)

            def root(name, features, width=S, which=0):
                wait_product(act, ("stat", name))
                if RT[name]:
                    act.wait_ge(rs_ready, RT[name])
                nc.scalar.activation(RTT[:, 0:width], product(("stat", name))[:, 0:width], ACT.Sqrt,
                                     bias=eps[:, which:which + 1], scale=1.0 / features).then_inc(rt_ready, 1)

            def high(H, c, src, gain=1.0):
                nc.scalar.activation(H[:, c, 0:S], src, ACT.Copy, scale=gain).then_inc(a_hi, 1)

            def normed_high(H, name, chunks, gain, base=0):
                for c in range(chunks):
                    if c % 2 == 0:
                        act.wait_ge(tn_ready, TN0[name] + c // 2 + 1)
                    high(H, base + c, SQ[:, base + c, :], CV[:, COL[gain] + c:COL[gain] + c + 1])

            def out_block(o, m, gain=None):
                wait_product(act, o)
                src = product(o)[:, 0:S]
                squares(None, m, src)
                scale = 1.0 if gain is None else CV[:, COL[gain] + m:COL[gain] + m + 1]
                nc.scalar.activation(Y[:, m, :], src, ACT.Copy, scale=scale).then_inc(free(o), 1)
                ahead(o)

            def exps(unit, PR, scale):
                nh, kw, nkb, qt, h0 = unit_shape(unit)
                i = UI[unit]
                b = i % 2
                act.wait_ge(mx_ready, i + 1)
                if i >= 2:
                    act.wait_ge(t_ready, TU[UNITS[i - 2]] + 1)
                    act.wait_ge(o_free, OU[UNITS[i - 2]] + 1)
                for j in range(nh):
                    at = score_at(unit[0], j)
                    last = nc.scalar.activation(PR[:, b, j * kw:(j + 1) * kw], SC[:, at:at + kw], ACT.Exp,
                                                bias=mx[:, b, j:j + 1], scale=scale,
                                                accum_out=sums[:, b, j:j + 1])
                last.then_inc(p_ready, 1)

            def token_root(name, i, src):
                for qt in range(QT):
                    nc.scalar.activation(SQ[:, 0:2, :].rearrange("p c s -> p (c s)"), src[:, qt, :], ACT.Square,
                                         accum_out=ssq[:, i, qt:qt + 1]).then_inc(schain, 1)
                    done["links"] += 1
                    act.wait_ge(schain, done["links"])
                nc.scalar.activation(srt[:, i, :], ssq[:, i, :], ACT.Sqrt, bias=eps[:, 0:1],
                                     scale=1.0 / 512).then_inc(rt_ready, 1)

            def turned_high(H, use, gain, base):
                act.wait_ge(t_ready, TU[use] + 1)
                for c in range(4):
                    g = 1.0 if gain is None else CV[:, COL[gain] + c:COL[gain] + c + 1]
                    high(H, base + c, TP[:, c * S:(c + 1) * S], g)

            act.wait_ge(masks, 1)
            act.wait_ge(x_in, 16)
            for c in range(8):
                squares("h1", c, X[:, c, :])
            weights(1)
            act.wait_ge(consts_in, 16)
            root("h1", D)
            normed_high(HA, "h1", 8, "g_pre_mix")
            act.wait_ge(angles, 2)
            nc.scalar.activation(SIN[:, :], SIN[:, :], ACT.Sin).then_inc(sincos, 1)
            nc.scalar.activation(COS[:, :], COS[:, :], ACT.Sin).then_inc(sincos, 1)
            nc.scalar.activation(hbp[:, :], CV[:, COL["b_ple_gate"]:COL["b_ple_gate"] + 8], ACT.Copy,
                                 scale=0.5).then_inc(bias_half, 1)
            weights(NSPLIT)
            act.wait_ge(a_lo, SP0["h1"] + 8)
            for m in range(3):
                wait_product(act, ("lat", m))
                src = product(("lat", m))[:, 0:S]
                squares(None, m, src)
                nc.scalar.activation(Y[:, 4 + m, :], src, ACT.Copy).then_inc(free(("lat", m)), 1)
                ahead(("lat", m))

            def copy_out(o, dst, width=S, scale=1.0):
                wait_product(act, o)
                nc.scalar.activation(dst, product(o)[:, 0:width], ACT.Copy, scale=scale).then_inc(free(o), 1)
                ahead(o)

            copy_out(("sbq", 0), QS[:, 0, :])
            copy_out(("sbq", 1), QS[:, 1, :])
            root("qlat", 2 * P)
            normed_high(HL, "ql", 2, "g_q_lat")
            root("kvlat", P)
            act.wait_ge(tn_ready, TN0["kvl"] + 1)
            high(HL, 2, SQ[:, 2, :], CV[:, COL["g_kv_lat"]:COL["g_kv_lat"] + 1])
            copy_out(("sbq", 2), QS[:, 2, :])
            copy_out(("sbq", 3), QS[:, 3, :])
            copy_out(("sbk", 0), KS1[:, 0, :])
            act.wait_ge(mem_in, 16)
            act.wait_ge(a_lo, SP0["kvl"] + 1)
            for c in range(8):
                squares("mem", c, MEMX[:, c, :])
                if c % 2 and c < 7:
                    copy_out(("sbk", 1 + c // 2), KS1[:, 1 + c // 2, :])
            root("mem", D)
            normed_high(HB, "mem", 8, "norm_mem_2")
            for o in (("sbk", 3), ("sbv", 1), ("qup", 7), ("vup", 1)):
                ahead(o)
            for u in range(4):
                act.wait_ge(sb_z, u + 1)
                e = E0[:, 2 * u:2 * u + 2, :]
                link(nc.scalar.activation(e, Z[:, 2 * u:2 * u + 2, :], ACT.Abs))
                nc.scalar.activation(e, e, ACT.Exp, scale=-1.0).then_inc(sb_e, 1)
                o = ("memk", u)
                wait_product(act, o)
                if u == 0:
                    act.wait_ge(a_lo, SP0["mem"] + 8)
                src = product(o)[:, 0:S]
                squares(None, u, src)
                nc.scalar.activation(KMEM[:, u, :], src, ACT.Copy).then_inc(free(o), 1)
                ahead(o)
            act.wait_ge(sb_e, 4)
            for u in range(4):
                e = E0[:, 2 * u:2 * u + 2, :]
                nc.scalar.activation(e, e, ACT.Ln, bias=1.0).then_inc(sb_l, 1)
            ahead(("memv", 1))
            root("memk0", P, 2 * S)
            root("memk1", P, 2 * S)
            scale_mla = (DH + ROPE) ** -0.5
            for u in range(4):
                act.wait_ge(sb_arg, u + 1)
                z = Z[:, 2 * u:2 * u + 2, :]
                nc.scalar.activation(z, z, ACT.Exp).then_inc(sb_a, 1)
                exps(("mla", u), PR1, scale_mla)
            act.wait_ge(o_free, OU[("sb", 3)] + 1)
            token_root("osb", 0, OSB)
            act.wait_ge(o_free, OU[("mla", 3)] + 1)
            token_root("omla", 1, OMLA)
            turned_high(HA, ("osb", 0), "g_grp_sb", 0)
            turned_high(HA, ("omla", 0), "g_grp_mla", 4)
            for m in range(8):
                out_block(("wo", m), m, "g_post_mix")
            root("postmix", D)
            for c in range(8):
                if c % 2 == 0:
                    act.wait_ge(x_ready, X0["postmix"] + c // 2 + 1)
                squares("preffn", c, X[:, c, :])
            root("preffn", D)
            normed_high(HA, "ffn", 8, "g_pre_ffn")

            def conv_first(j, g):
                o = ("up", 2 * j + g)
                wait_product(act, o)
                if j >= 2:
                    act.wait_ge(act_out, j - 1)
                ch = g * FC + j
                nc.scalar.activation(YC[:, j % 2, g, :], product(o)[:, 0:S], ACT.Identity,
                                     scale=CV[:, COL["conv_w"] + 2 * 2 * FC + ch:COL["conv_w"] + 2 * 2 * FC + ch + 1],
                                     bias=CV[:, COL["conv_b"] + ch:COL["conv_b"] + ch + 1]).then_inc(conv0, 1)
                ahead(o)

            for j in range(FC + 1):
                if j < FC:
                    conv_first(j, 0)
                if j:
                    wait_freed(act, ("up", 2 * j - 2))
                    nc.scalar.activation(G1[:, (j - 1) % 2, 0, :], YC[:, (j - 1) % 2, 0, :],
                                         ACT.Gelu_apprx_tanh).then_inc(gelu_done, 1)
                if j < FC:
                    conv_first(j, 1)
                if j:
                    act.wait_ge(act_out, j)
                    high(ACTS, j - 1, G1[:, (j - 1) % 2, 1, :])
            act.wait_ge(p_in, 16)
            for c in range(2):
                high(HL, c, PX[:, c, :])
            act.wait_ge(a_lo, SP0["ffn"] + 8)
            for m in range(8):
                out_block(("down", m), m, "g_post_ffn")
            for m in range(2):
                copy_out(("ple", m), EE[:, m, :], scale=0.5)
            root("postffn", D)
            for m in range(2, 8):
                copy_out(("ple", m), EE[:, m, :], scale=0.5)
            for c in range(8):
                if c % 2 == 0:
                    act.wait_ge(x_ready, X0["postffn"] + c // 2 + 1)
                squares("plegate", c, X[:, c, :])
            root("plegate", D)
            normed_high(HA, "ph", 8, "g_ple_gate")
            act.wait_ge(bias_half, 1)
            for m in range(9):
                if m < 8:
                    o = ("gate", m)
                    wait_product(act, o)
                    if m >= 2:
                        act.wait_ge(ge_ready, m - 1)
                    nc.scalar.activation(G1[:, m % 2, 0, :], product(o)[:, 0:S], ACT.Tanh, scale=0.5,
                                         bias=hbp[:, m:m + 1]).then_inc(free(o), 1)
                    ahead(o)
                if m:
                    act.wait_ge(ge_ready, m)
                    if m == 1:
                        act.wait_ge(a_lo, SP0["ph"] + 8)
                    squares("postple", m - 1, Y[:, m - 1, :])
            root("postple", D)

            for c in range(8):
                if c % 2 == 0:
                    act.wait_ge(x_ready, X0["postple"] + c // 2 + 1)
                squares("mix2", c, X[:, c, :])
            root("mix2", D)
            normed_high(HA, "xn2", 8, "norm_mix_2")
            act.wait_ge(a_lo, SP0["xn2"] + 8)
            for m in range(2):
                wait_product(act, ("kv2", m))
                ahead(("kv2", m))
            for m, dst in ((2, KSD), (3, KWD)):
                o = ("kv2", m)
                wait_product(act, o)
                for g in range(2):
                    src = product(o)[64 * g:64 * g + 64, 0:S]
                    nc.scalar.activation(dst[0:64, g, :], src, ACT.Copy).then_inc(schain, 1)
                    last = nc.scalar.activation(dst[64:128, g, :], src, ACT.Copy)
                    done["links"] += 1
                    if g == 0:
                        done["links"] += 1
                        last.then_inc(schain, 1)
                last.then_inc(free(o), 1)
                wait_freed(act, o)
                for g in range(2):
                    squares(None, 2 * (m - 2) + g, dst[:, g, :])
                ahead(o)

            def head_block(o, dst, at):
                wait_product(act, o)
                src = product(o)[:, 0:S]
                squares(None, at, src)
                nc.scalar.activation(dst, src, ACT.Copy).then_inc(free(o), 1)
                ahead(o)

            head_block(("q2", 0), QN[:, 0, :], 4)
            head_block(("q2", 1), QN[:, 1, :], 5)
            root("ks", DH, 2 * S)
            root("kw", DH, 2 * S)
            for kv in range(2):
                act.wait_ge(cmp_sum, kv + 1)
                nc.scalar.activation(BS[:, kv, 0, :, :], TB[:, kv, :, :], ACT.Copy).then_inc(a_hi, 1)
            head_block(("q2", 2), QN[:, 2, :], 6)
            head_block(("q2", 3), QN[:, 3, :], 7)
            ahead(("tm2", 1))
            act.wait_ge(gate_in, 2)
            nc.scalar.activation(GN[:, :, :], VS2[:, :, 256:280], ACT.Tanh, scale=0.5).then_inc(gate_th, 1)
            root("q0", DH, 2 * S)
            root("q1", DH, 2 * S)
            for c in range(4):
                ahead(("conv2", 2 * c))
                o = ("conv2", 2 * c + 1)
                wait_product(act, o)
                if c >= 2:
                    act.wait_ge(conv_u, c - 1)
                nc.scalar.activation(TH[:, c % 2, :], product(o)[:, 0:S], ACT.Tanh, scale=0.5).then_inc(free(o), 1)
                ahead(o)
            for m in range(4):
                head_block(("qmem", m), QME[:, m, :], m)

            def compressed(name, kv):
                for m in range(2):
                    o = (name, m)
                    wait_product(act, o)
                    nc.scalar.activation(G2[:, kv, m, :], product(o)[:, 0:2 * CMP],
                                         ACT.Gelu_apprx_tanh).then_inc(free(o), 1)
                    ahead(o)

            compressed("cmpk", 0)
            root("qm0", P, 2 * S)
            root("qm1", P, 2 * S)
            compressed("cmpv", 1)
            o = ("stat", "kcT")
            wait_product(act, o)
            src = product(o)[:, 0:2 * CMP]
            nc.scalar.activation(SQ[:, 4, 0:2 * CMP], src, ACT.Square).then_inc(sq_ready, 1)
            nc.scalar.activation(KCD[:, :], src, ACT.Copy).then_inc(free(o), 1)
            root("kc", DH, 2 * CMP)

            def fill(item):
                name, m = item
                if item == ("stat", "lnmean"):
                    return
                if item == ("stat", "lnvar"):
                    for c in range(4):
                        act.wait_ge(ln_centred, c + 1)
                        squares("lnvar", c, CY[:, c, :])
                    root("lnvar", 512, S, 1)
                    for c in range(4):
                        act.wait_ge(ln_scaled, c + 1)
                        g, b = COL["conv_ln_g_2"] + c, COL["conv_ln_b_2"] + c
                        nc.scalar.activation(U[:, c, :], CY[:, c, :], ACT.Identity, scale=CV[:, g:g + 1],
                                             bias=CV[:, b:b + 1]).then_inc(ln_z, 1)
                        act.wait_ge(ln_z, 2 * c + 1)
                        if c >= 2:
                            act.wait_ge(silu_done, c - 1)
                        nc.scalar.activation(RTT[:, (c % 2) * S:(c % 2 + 1) * S], U[:, c, :], ACT.Tanh,
                                             scale=0.5).then_inc(ln_z, 1)
                    for c in range(4):
                        act.wait_ge(silu_done, c + 1)
                        high(HB, c, CY[:, c, :], 0.5)
                    return
                o = (name + "g", m)
                wait_product(act, o)
                i = {"brmem": 0, "brconv": 8, "brnsa": 16}[name] + m
                if i >= 2:
                    act.wait_ge(th_used, i - 1)
                nc.scalar.activation(TH[:, i % 2, :], product(o)[:, 0:S], ACT.Tanh, scale=0.5).then_inc(free(o), 1)
                ahead((name, m))

            for i, unit in enumerate(UNITS2):
                exps(unit, PR2, MEM_SCALE if unit[0] == "mem" else DH ** -0.5)
                if i == 2:
                    turned_high(HB, ("omem", 0), None, 4)
                if i == BIAS_STEP:
                    act.wait_ge(conv_end, 1)
                    for c in range(4):
                        b = COL["conv_b_2"] + c
                        nc.scalar.activation(CY[:, c, :], CY[:, c, :], ACT.Identity, scale=0.5,
                                             bias=CV[:, b:b + 1]).then_inc(ln_biased, 1)
                for item in FILL.get(i, []):
                    fill(item)
            for item in FILL_TURNED + FILL_OUT:
                fill(item)
            turned_high(HL, ("onsa", 0), None, 0)
            for m in range(8):
                fill(("brnsa", m))
                if m:
                    act.wait_ge(th_used, 16 + m)
                    high(HB, m - 1, Y[:, m - 1, :], 0.5)
            act.wait_ge(th_used, 24)
            high(HB, 7, Y[:, 7, :], 0.5)
            for m in range(8):
                o = ("wout", m)
                wait_freed(act, o)
                squares("ffn2", m, X[:, m, :])
                ahead(o)
            root("ffn2", D)
            normed_high(HA, "hf", 8, "norm_ffn_2")
            for j in range(FC + 1):
                if j < FC:
                    o = ("up2", 2 * j)
                    wait_product(act, o)
                    if j >= 2:
                        wait_freed(act, ("up2", 2 * j - 4))
                    nc.scalar.activation(G1[:, j % 2, 0, :], product(o)[:, 0:S], ACT.Tanh,
                                         scale=0.5).then_inc(th_done, 1)
                    ahead(o)
                if j:
                    wait_freed(act, ("up2", 2 * j - 1))
                    high(ACTS, j - 1, G1[:, (j - 1) % 2, 1, :])
                    ahead(("up2", 2 * j - 1))
            for m in range(8):
                ahead(("down2", m))

        @block.vector
        def _(dve):
            done = {"lo": 1, "links": 0}

            def link(ins):
                done["links"] += 1
                ins.then_inc(vchain, 1)
                dve.wait_ge(vchain, done["links"])

            def weights(upto):
                while done["lo"] < min(upto, NTILES):
                    n = done["lo"]
                    dve.wait_ge(hi_done, n + 1)
                    nc.vector.tensor_tensor(wlo[:, n % NSPLIT, :], raw[:, n % NRAW, :],
                                            whi[:, n % NSPLIT, :].bitcast(F32), ALU.subtract).then_inc(lo_vector, 1)
                    done["lo"] += 2

            def ahead(o):
                weights(end_tile(o) + 1 + NSPLIT)

            def inverse_root(name, width=S):
                dve.wait_ge(rt_ready, RT[name] + 1)
                nc.vector.reciprocal(RS[:, 0:width], RTT[:, 0:width]).then_inc(rs_ready, 1)
                dve.wait_ge(rs_ready, RT[name] + 1)

            def rs2():
                return RS[:, 0:S].unsqueeze(1).to_broadcast((P, 2, S))

            def scaled(name, src, chunks, base=0):
                if SP0[name]:
                    dve.wait_ge(a_lo, SP0[name])
                for c in range(0, chunks, 2):
                    n = min(2, chunks - c)
                    o, i = SQ[:, base + c:base + c + n, :], src[:, c:c + n, :]
                    r = rs2() if n == 2 else RS[:, 0:S].unsqueeze(1)
                    nc.vector.tensor_tensor(o, i, r, ALU.mult).then_inc(tn_ready, 1)
                dve.wait_ge(tn_ready, TN0[name] + (chunks + 1) // 2)

            def low(H, name, c, src, gain=1.0, base=0, extra=0):
                dve.wait_ge(a_hi, SP0[name] + c + 1)
                nc.vector.scalar_tensor_tensor(out=H[:, base + c, S:2 * S], in0=src, scalar=gain,
                                               in1=H[:, base + c, 0:S].bitcast(F32), op0=ALU.mult,
                                               op1=ALU.subtract).then_inc(a_lo, 1)

            def normed_low(H, name, tn, chunks, gain, base=0):
                for c in range(chunks):
                    low(H, name, c, SQ[:, base + c, :], CV[:, COL[gain] + c:COL[gain] + c + 1], base)

            def copy_out(o, dst, width=S):
                wait_product(dve, o)
                nc.vector.tensor_copy(dst, product(o)[:, 0:width]).then_inc(free(o), 1)
                ahead(o)

            def rope(src, dst, par):
                t1, t2 = Y[64:96, 2 * par, :], Y[64:96, 2 * par + 1, :]
                nc.vector.tensor_tensor(t1, src[64:96, 0:S], COS[64:96, :], ALU.mult).then_inc(vchain, 1)
                last = nc.vector.tensor_tensor(t2, src[96:128, 0:S], SIN[96:128, :], ALU.mult)
                done["links"] += 1
                link(last)
                return nc.vector.tensor_tensor(dst, t1, t2, ALU.add)

            def maxima(unit, scale):
                nh, kw, nkb, qt, h0 = unit_shape(unit)
                b = UI[unit] % 2
                dve.wait_ge(s_ready, SU[unit] + 1)
                step = CMP if unit[0] == "cmp" else S
                dst = mx[:, b, 0:nh]
                if unit[0] in ("mla", "mem"):
                    src = SC[:, 0:nh * step].rearrange("p (h k) -> p h k", h=nh)[:, :, 0:kw]
                else:
                    dst = dst.rearrange("p (i r) -> p r i", r=2)
                    src = SC[:, :].rearrange("p (r n) -> p r n", r=2)[:, :, 0:nh // 2 * step].rearrange(
                        "p r (i k) -> p r i k", k=step)[:, :, :, 0:kw]
                if UI[unit] >= 2:
                    dve.wait_ge(p_ready, UI[unit] - 1)
                link(nc.vector.tensor_reduce(dst, src, AX.X, ALU.max, negate=True))
                nc.vector.tensor_scalar(mx[:, b, 0:nh], mx[:, b, 0:nh], scale, None, ALU.mult).then_inc(mx_ready, 1)

            def take_turned(unit):
                nh, kw, nkb, qt, h0 = unit_shape(unit)
                dve.wait_ge(t_ready, TU[unit] + 1)
                if UI[unit]:
                    dve.wait_ge(o_ready, OU[UNITS[UI[unit] - 1]] + 1)
                w = min(P, kw)
                n = nh * nkb * P
                nc.vector.tensor_copy(PT[0:w, 0:n], TP[0:w, 0:n]).then_inc(t_free, 1)

            def take_out(unit, dst, dv):
                nh, kw, nkb, qt, h0 = unit_shape(unit)
                b = UI[unit] % 2
                dve.wait_ge(p_ready, UI[unit] + 1)
                link(nc.vector.reciprocal(rsum[:, b, 0:nh], sums[:, b, 0:nh]))
                dve.wait_ge(o_ready, OU[unit] + 1)
                nc.vector.tensor_tensor(dst[:, qt, h0 * dv:(h0 + nh) * dv].rearrange("p (h d) -> p h d", h=nh),
                                        OP[:, 0:nh * dv].rearrange("p (h d) -> p h d", h=nh),
                                        rsum[:, b, 0:nh].unsqueeze(2).to_broadcast((P, nh, dv)),
                                        ALU.mult).then_inc(o_free, 1)

            def residual(name, gain=None):
                for c in range(0, 8, 2):
                    if gain is None:
                        link(nc.vector.tensor_tensor(SQ[:, c:c + 2, :], Y[:, c:c + 2, :], rs2(), ALU.mult))
                    else:
                        for k in range(c, c + 2):
                            ins = nc.vector.scalar_tensor_tensor(
                                out=SQ[:, k, :], in0=Y[:, k, :], scalar=CV[:, COL[gain] + k:COL[gain] + k + 1],
                                in1=RS[:, 0:S], op0=ALU.mult, op1=ALU.mult)
                        link(ins)
                    nc.vector.tensor_tensor(X[:, c:c + 2, :], X[:, c:c + 2, :], SQ[:, c:c + 2, :],
                                            ALU.add).then_inc(x_ready, 1)

            magic = 1.5 * 2.0 ** 23
            c1 = 6.28125
            c2 = 2029.0 / 2 ** 20
            c3 = 2 * math.pi - c1 - c2
            ang, turns = Y[:, 0, :], Y[:, 2, :]
            dve.wait_ge(consts_in, 16)
            dve.wait_ge(pos_in, 16)
            link(nc.vector.tensor_copy(Y[:, 3, :], Y[:, 1, :].bitcast(I32)))
            link(nc.vector.tensor_scalar(ang, Y[:, 3, :], CV[:, COL["freq"]:COL["freq"] + 1], None, ALU.mult))
            for dst, quarter in ((SIN, 0.0), (COS, 0.25)):
                link(nc.vector.tensor_scalar(turns, ang, 1 / (2 * math.pi), quarter, ALU.mult, ALU.add))
                link(nc.vector.tensor_scalar(turns, turns, magic, None, ALU.add))
                link(nc.vector.tensor_scalar(turns, turns, magic, None, ALU.subtract))
                src = ang
                for c in (c1, c2, c3):
                    link(nc.vector.scalar_tensor_tensor(out=dst[:, :], in0=turns, scalar=-c, in1=src, op0=ALU.mult,
                                                        op1=ALU.add))
                    src = dst[:, :]
                link(nc.vector.tensor_scalar(dst[:, :], dst[:, :], 2 * math.pi * quarter, 3.1415925, ALU.add, ALU.min))
                nc.vector.tensor_scalar(dst[:, :], dst[:, :], -3.1415925, None, ALU.max).then_inc(angles, 1)
            inverse_root("h1")
            scaled("h1", X, 8)
            weights(2)
            normed_low(HA, "h1", "h1", 8, "g_pre_mix")
            weights(NSPLIT)
            dve.wait_ge(sincos, 2)
            link(nc.vector.tensor_scalar(SIN[:, :], SIN[:, :], CV[:, COL["sign"]:COL["sign"] + 1], None, ALU.mult))
            for m in range(3):
                ahead(("lat", m))
            o = ("lat", 3)
            wait_product(dve, o)
            rope(product(o), KM[64:96, 0, :], 0).then_inc(free(o), 1)
            wait_freed(dve, o)
            nc.vector.tensor_copy(KM[64:96, 1:8, :], KM[64:96, 0:1, :].to_broadcast((32, 7, S)))
            ahead(o)
            ahead(("sbq", 0))
            ahead(("sbq", 1))
            inverse_root("qlat")
            scaled("ql", Y[:, 4:6, :], 2)
            normed_low(HL, "ql", "ql", 2, "g_q_lat")
            inverse_root("kvlat")
            scaled("kvl", Y[:, 6:7, :], 1, base=2)
            low(HL, "kvl", 0, SQ[:, 2, :], CV[:, COL["g_kv_lat"]:COL["g_kv_lat"] + 1], base=2)
            for o in (("sbq", 2), ("sbq", 3), ("sbk", 0), ("sbk", 1), ("sbk", 2)):
                wait_product(dve, o)
                ahead(o)
            inverse_root("mem")
            scaled("mem", MEMX, 8)
            normed_low(HB, "mem", "mem", 8, "norm_mem_2")
            ahead(("sbk", 3))
            for qt in range(QT):
                copy_out(("sbv", qt), VS1[:, qt, :], 512)
            for h in range(HEADS):
                o = ("qup", h)
                wait_product(dve, o)
                nc.vector.tensor_copy(QM[0:64, h, :], product(o)[0:64, 0:S])
                if h:
                    wait_freed(dve, ("qup", h - 1))
                rope(product(o), QM[64:96, h, :], h % 2).then_inc(free(o), 1)
                ahead(o)
            for m in range(4):
                o = ("kup", m)
                wait_product(dve, o)
                nc.vector.tensor_copy(KM[0:64, 2 * m, :], product(o)[0:64, 0:S])
                nc.vector.tensor_copy(KM[0:64, 2 * m + 1, :], product(o)[64:128, 0:S]).then_inc(free(o), 1)
                ahead(o)
            for qt in range(QT):
                copy_out(("vup", qt), VM[:, qt, :], 512)
            for u in range(4):
                dve.wait_ge(s_ready, u + 1)
                nc.vector.tensor_scalar(Z[:, 2 * u:2 * u + 2, :],
                                        SC[:, :].rearrange("p (h k) -> p h k", h=2)[:, :, 0:384], DH ** -0.5, None,
                                        ALU.mult).then_inc(sb_z, 1)
                wait_product(dve, ("memk", u))
                ahead(("memk", u))
            for u in range(4):
                dve.wait_ge(sb_l, u + 1)
                e, z = E0[:, 2 * u:2 * u + 2, :], Z[:, 2 * u:2 * u + 2, :]
                link(nc.vector.scalar_tensor_tensor(out=e, in0=z, scalar=0.0, in1=e, op0=ALU.max, op1=ALU.add))
                for at in (0, S):
                    last = nc.vector.tensor_tensor(e[:, :, at:at + P], e[:, :, at:at + P],
                                                   strict[:, :].unsqueeze(1).to_broadcast((P, 2, P)), ALU.mult)
                last.then_inc(sb_sp, 1)
            for qt in range(QT):
                copy_out(("memv", qt), VMEM[:, qt, :], 512)

            def head_norm(name, dst, gain, g=None):
                inverse_root(name, 2 * S)
                for i in range(2):
                    last = nc.vector.scalar_tensor_tensor(out=dst[i], in0=dst[i], scalar=gain,
                                                          in1=RS[:, i * S:(i + 1) * S], op0=ALU.mult, op1=ALU.mult)
                link(last)

            kg = CV[:, COL["mem_qk_norm_2"] + 1:COL["mem_qk_norm_2"] + 2]
            for i in range(2):
                head_norm(f"memk{i}", [KMEM[:, 2 * i, :], KMEM[:, 2 * i + 1, :]], kg)
            scale_mla = (DH + ROPE) ** -0.5

            def take_sb(u):
                dve.wait_ge(o_ready, OU[("sb", u)] + 1)
                nc.vector.tensor_copy(OSB[:, :, u * P:(u + 1) * P],
                                      OP[:, 0:S].rearrange("p (q d) -> p q d", q=2)).then_inc(o_free, 1)

            for u in range(4):
                dve.wait_ge(t_ready, TU[("cum", u)] + 1)
                z = Z[:, 2 * u:2 * u + 2, :]
                nc.vector.scalar_tensor_tensor(out=z, in0=TP[:, :].rearrange("p (h k) -> p h k", h=2)[:, :, 0:384],
                                               scalar=-1.0, in1=z, op0=ALU.mult, op1=ALU.add).then_inc(t_free, 1)
                wait_turned(dve, ("cum", u))
                for at in (0, S):
                    last = nc.vector.tensor_tensor(z[:, :, at:at + P], z[:, :, at:at + P],
                                                   negstrict[:, :].unsqueeze(1).to_broadcast((P, 2, P)), ALU.add)
                last.then_inc(sb_arg, 1)
                if u:
                    take_sb(u - 1)
                    take_turned(("mla", u - 1))
                maxima(("mla", u), scale_mla)
                if u:
                    take_out(("mla", u - 1), OMLA, DH)
            take_sb(3)
            take_turned(("mla", 3))
            take_out(("mla", 3), OMLA, DH)

            def token_norm(name, i, dst):
                dve.wait_ge(rt_ready, RT[name] + 1)
                nc.vector.reciprocal(rst[:, i, :], srt[:, i, :]).then_inc(rs_ready, 1)
                dve.wait_ge(rs_ready, RT[name] + 1)
                for qt in range(QT):
                    nc.vector.tensor_scalar(dst[:, qt, :], dst[:, qt, :], rst[:, i, qt:qt + 1], None,
                                            ALU.mult).then_inc(o_normed, 1)

            def turned_low(H, use, name, gain, base, c0=0):
                for c in range(4):
                    g = 1.0 if gain is None else CV[:, COL[gain] + c:COL[gain] + c + 1]
                    dve.wait_ge(a_hi, SP0[name] + c0 + c // 2 * 2 + 2)
                    nc.vector.scalar_tensor_tensor(out=H[:, base + c, S:2 * S], in0=TP[:, c * S:(c + 1) * S],
                                                   scalar=g, in1=H[:, base + c, 0:S].bitcast(F32), op0=ALU.mult,
                                                   op1=ALU.subtract).then_inc(a_lo, 1)

            token_norm("osb", 0, OSB)
            token_norm("omla", 1, OMLA)
            turned_low(HA, ("osb", 0), "o", "g_grp_sb", 0)
            turned_low(HA, ("omla", 0), "o", "g_grp_mla", 4, 4)
            for m in range(8):
                wait_product(dve, ("wo", m))
                ahead(("wo", m))
            inverse_root("postmix")
            residual("postmix")
            inverse_root("preffn")
            scaled("ffn", X, 8)
            normed_low(HA, "ffn", "ffn", 8, "g_pre_ffn")

            def conv_rest(j, g):
                o = ("up", 2 * j + g)
                y, src = YC[:, j % 2, g, :], product(o)
                dve.wait_ge(conv0, 2 * j + g + 1)
                for tap in (1, 0):
                    shift = 2 - tap
                    at = COL["conv_w"] + tap * 2 * FC + g * FC + j
                    ins = nc.vector.scalar_tensor_tensor(out=y[:, shift:S], in0=src[:, 0:S - shift],
                                                         scalar=CV[:, at:at + 1], in1=y[:, shift:S], op0=ALU.mult,
                                                         op1=ALU.add)
                    if tap:
                        link(ins)
                ins.then_inc(free(o), 1)
                ahead(o)

            for j in range(FC + 1):
                if j < FC:
                    conv_rest(j, 0)
                if j:
                    dve.wait_ge(gelu_done, j)
                    wait_freed(dve, ("up", 2 * j - 1))
                    if j >= 3:
                        dve.wait_ge(a_lo, SP0["a"] + j - 2)
                    nc.vector.tensor_tensor(G1[:, (j - 1) % 2, 1, :], G1[:, (j - 1) % 2, 0, :],
                                            YC[:, (j - 1) % 2, 1, :], ALU.mult).then_inc(act_out, 1)
                if j < FC:
                    conv_rest(j, 1)
                if j:
                    low(ACTS, "a", j - 1, G1[:, (j - 1) % 2, 1, :])
            for c in range(2):
                low(HL, "p", c, PX[:, c, :])
            for m in range(8):
                wait_product(dve, ("down", m))
                ahead(("down", m))
            ahead(("ple", 1))
            inverse_root("postffn")
            residual("postffn")
            inverse_root("plegate")
            scaled("ph", X, 8)
            normed_low(HA, "ph", "ph", 8, "g_ple_gate")
            for m in range(8):
                o = ("gate", m)
                wait_freed(dve, o)
                nc.vector.scalar_tensor_tensor(out=Y[:, m, :], in0=G1[:, m % 2, 0, :], scalar=1.0, in1=EE[:, m, :],
                                               op0=ALU.add, op1=ALU.mult).then_inc(ge_ready, 1)
                ahead(o)
            inverse_root("postple")
            residual("postple", "g_post_ple")

            inverse_root("mix2")
            scaled("xn2", X, 8)
            normed_low(HA, "xn2", "xn2", 8, "norm_mix_2")
            for m in range(2):
                o = ("kv2", m)
                wait_product(dve, o)
                for g in range(2):
                    src = product(o)[64 * g:64 * g + 64, :]
                    nc.vector.tensor_copy(S2[0:64, m, g, :], src[:, 0:S])
                    last = nc.vector.tensor_copy(S2[64:128, m, g, 0:S - 1], src[:, 1:S])
                last.then_inc(free(o), 1)
                ahead(o)
            for kv in range(2):
                wait_freed(dve, ("kv2", kv))
                for g in range(2):
                    for half in range(2):
                        src = S2[:, kv, g, CSTEP * half:CSTEP * half + CMP * CSTEP].rearrange(
                            "p (i c l) -> p c i l", c=8, l=2)[:, :, :, 0]
                        at = COL["cmp_pos_2"] + kv * 16 + 8 * half
                        last = nc.vector.tensor_tensor(
                            TB[:, kv, 8 * half:8 * half + 8, g * CMP:(g + 1) * CMP], src,
                            CV[:, at:at + 8].unsqueeze(2).to_broadcast((P, 8, CMP)), ALU.add)
                last.then_inc(cmp_sum, 1)
            ahead(("q2", 1))
            gains = {n: CV[:, COL["nsa_qk_norm_2"] + i:COL["nsa_qk_norm_2"] + i + 1]
                     for i, n in enumerate(("q", "c", "s", "w"))}
            head_norm("ks", [KSD[:, 0, :], KSD[:, 1, :]], gains["s"])
            head_norm("kw", [KWD[:, 0, :], KWD[:, 1, :]], gains["w"])
            for kv in range(2):
                dve.wait_ge(a_hi, SP0["bk"] + kv + 1)
                nc.vector.tensor_tensor(BS[:, kv, 1, :, :], TB[:, kv, :, :], BS[:, kv, 0, :, :].bitcast(F32),
                                        ALU.subtract).then_inc(a_lo, 1)
            ahead(("q2", 2))
            ahead(("q2", 3))
            for qt in range(QT):
                o = ("tm2", qt)
                wait_product(dve, o)
                nc.vector.tensor_copy(VS2[:, qt, :], product(o)[:, 0:280]).then_inc(free(o), 1)
                wait_freed(dve, o)
                nc.vector.tensor_copy(VS2[:, qt, 0:1], VS2[:, qt, 0:1]).then_inc(gate_in, 1)
                ahead(o)
            head_norm("q0", [QN[:, 0, :], QN[:, 1, :]], gains["q"])
            head_norm("q1", [QN[:, 2, :], QN[:, 3, :]], gains["q"])
            dve.wait_ge(gate_th, 1)
            nc.vector.tensor_scalar(GN[:, :, :], GN[:, :, :], 0.5, 0.5, ALU.mult, ALU.add).then_inc(vchain, 1)
            done["links"] += 1

            taps = [(c, k) for c0 in (0, 2) for k in range(KSIZE - 1, -1, -1) for c in (c0, c0 + 1)]
            at_tap = {}
            done["taps"] = 0

            def conv_taps(n):
                for c, k in taps[done["taps"]:done["taps"] + n]:
                    dve.wait_ge(conv_u, c + 1)
                    if c in at_tap:
                        dve.wait_ge(vchain, at_tap[c])
                    w = COL["conv_w_2"] + c * KSIZE + k
                    shift = KSIZE - 1 - k
                    if shift == 0:
                        ins = nc.vector.tensor_scalar(CY[:, c, :], U[:, c, :], CV[:, w:w + 1], None, ALU.mult)
                    else:
                        ins = nc.vector.scalar_tensor_tensor(out=CY[:, c, shift:S], in0=U[:, c, 0:S - shift],
                                                             scalar=CV[:, w:w + 1], in1=CY[:, c, shift:S],
                                                             op0=ALU.mult, op1=ALU.add)
                    ins.then_inc(vchain, 1)
                    done["links"] += 1
                    at_tap[c] = done["links"]
                    done["taps"] += 1

            for c in range(4):
                o = ("conv2", 2 * c)
                wait_product(dve, o)
                ahead(o)
                wait_freed(dve, ("conv2", 2 * c + 1))
                nc.vector.scalar_tensor_tensor(out=U[:, c, :], in0=TH[:, c % 2, :], scalar=1.0,
                                               in1=product(o)[:, 0:S], op0=ALU.add, op1=ALU.mult).then_inc(free(o), 1)
                wait_freed(dve, o)
                nc.vector.tensor_copy(U[:, c, 0:1], U[:, c, 0:1]).then_inc(conv_u, 1)
                ahead(("conv2", 2 * c + 1))
                if c:
                    conv_taps(6)
            for m in range(4):
                wait_product(dve, ("qmem", m))
                ahead(("qmem", m))
                conv_taps(6)
            for m in range(2):
                wait_product(dve, ("cmpk", m))
                ahead(("cmpk", m))
                conv_taps(8)
            qg = CV[:, COL["mem_qk_norm_2"]:COL["mem_qk_norm_2"] + 1]
            head_norm("qm0", [QME[:, 0, :], QME[:, 1, :]], qg)
            head_norm("qm1", [QME[:, 2, :], QME[:, 3, :]], qg)
            for m in range(2):
                wait_product(dve, ("cmpv", m))
                ahead(("cmpv", m))
            o = ("stat", "vc")
            wait_product(dve, o)
            nc.vector.tensor_copy(VC[0:CMP, :, :], product(o)[0:CMP, 0:P].rearrange("p (g d) -> p g d", g=2)).then_inc(
                free(o), 1)
            inverse_root("kc", 2 * CMP)
            nc.vector.scalar_tensor_tensor(out=KCD[:, :], in0=KCD[:, :], scalar=gains["c"], in1=RS[:, 0:2 * CMP],
                                           op0=ALU.mult, op1=ALU.mult).then_inc(attn_in, 1)

            def take_nsa(unit):
                kind, u = unit
                nh, kw, nkb, qt, h0 = unit_shape(unit)
                b = UI[unit] % 2
                branch = ("cmp", "slc", "win").index(kind)
                dve.wait_ge(p_ready, UI[unit] + 1)
                link(nc.vector.reciprocal(rsum[:, b, 0:nh], sums[:, b, 0:nh]))
                gate = GN[:, qt, :].rearrange("p (h r) -> p r h", r=3)[:, branch, h0:h0 + nh]
                link(nc.vector.tensor_tensor(rsum[:, b, 0:nh], rsum[:, b, 0:nh], gate, ALU.mult))
                if kind == "cmp":
                    link(nc.vector.tensor_scalar(rsum[:, b, 0:nh], rsum[:, b, 0:nh], valid[:, qt:qt + 1], None,
                                                 ALU.mult))
                dve.wait_ge(o_ready, OU[unit] + 1)
                dst = ONSA[:, qt, h0 * DH:(h0 + nh) * DH]
                tmp = OMEM[:, 1, 0:nh * DH]
                out_ap = dst if kind == "cmp" else tmp
                nc.vector.tensor_tensor(out_ap.rearrange("p (h d) -> p h d", h=nh),
                                        OP[:, 0:nh * DH].rearrange("p (h d) -> p h d", h=nh),
                                        rsum[:, b, 0:nh].unsqueeze(2).to_broadcast((P, nh, DH)),
                                        ALU.mult).then_inc(o_free, 1)
                dve.wait_ge(o_free, OU[unit] + 1)
                if kind != "cmp":
                    ins = nc.vector.tensor_tensor(dst, dst, tmp, ALU.add)
                    if unit == UNITS2[-1]:
                        ins.then_inc(onsa_done, 1)
                    else:
                        link(ins)

            def fill(item):
                name, m = item
                if item == ("stat", "lnmean"):
                    wait_product(dve, item)
                    mean = OMEM[:, 0, 0:S]
                    nc.vector.tensor_scalar(mean, product(item)[:, 0:S], 1.0 / 512, None, ALU.mult).then_inc(
                        free(item), 1)
                    wait_freed(dve, item)
                    for c in range(4):
                        nc.vector.tensor_tensor(CY[:, c, :], CY[:, c, :], mean, ALU.subtract).then_inc(ln_centred, 1)
                    return
                if item == ("stat", "lnvar"):
                    inverse_root("lnvar")
                    dve.wait_ge(ln_centred, 4)
                    for c in range(4):
                        nc.vector.tensor_tensor(CY[:, c, :], CY[:, c, :], RS[:, 0:S], ALU.mult).then_inc(ln_scaled, 1)
                    for c in range(4):
                        dve.wait_ge(ln_z, 2 * c + 2)
                        nc.vector.scalar_tensor_tensor(out=CY[:, c, :], in0=RTT[:, (c % 2) * S:(c % 2 + 1) * S],
                                                       scalar=1.0, in1=U[:, c, :], op0=ALU.add,
                                                       op1=ALU.mult).then_inc(silu_done, 1)
                    for c in range(4):
                        low(HB, "cv", c, CY[:, c, :], 0.5)
                    return
                i = {"brmem": 0, "brconv": 8, "brnsa": 16}[name] + m
                wait_product(dve, (name + "g", m))
                ahead((name + "g", m))
                o = (name, m)
                wait_freed(dve, (name + "g", m))
                wait_product(dve, o)
                dst = Y[:, m, :] if name == "brmem" else U[:, m % 2, :]
                nc.vector.scalar_tensor_tensor(out=dst, in0=TH[:, i % 2, :], scalar=1.0, in1=product(o)[:, 0:S],
                                               op0=ALU.add, op1=ALU.mult).then_inc(free(o), 1)
                wait_freed(dve, o)
                if name == "brmem":
                    nc.vector.tensor_copy(Y[:, m, 0:1], Y[:, m, 0:1]).then_inc(th_used, 1)
                else:
                    ins = nc.vector.tensor_tensor(Y[:, m, :], Y[:, m, :], dst, ALU.add)
                    ins.then_inc(th_used, 1)
                    dve.wait_ge(th_used, i + 1)
                ahead(o)

            for i, unit in enumerate(UNITS2):
                maxima(unit, MEM_SCALE if unit[0] == "mem" else DH ** -0.5)
                if 1 <= i <= 2:
                    take_out(UNITS2[i - 1], OMEM, P)
                elif i:
                    take_nsa(UNITS2[i - 1])
                if i == 2:
                    turned_low(HB, ("omem", 0), "om", None, 4)
                if i < BIAS_STEP:
                    conv_taps(len(taps) if i == BIAS_STEP - 1 else 12)
                    if i == BIAS_STEP - 1:
                        dve.wait_ge(vchain, done["links"])
                        nc.vector.tensor_copy(CY[:, 0, 0:1], CY[:, 0, 0:1]).then_inc(conv_end, 1)
                for item in FILL.get(i, []):
                    fill(item)
                take_turned(unit)
            for item in FILL_TURNED:
                fill(item)
            take_nsa(UNITS2[-1])
            for item in FILL_OUT:
                fill(item)
            turned_low(HL, ("onsa", 0), "on", None, 0)
            for m in range(8):
                fill(("brnsa", m))
                low(HB, "y", m, Y[:, m, :], 0.5)
            for m in range(8):
                o = ("wout", m)
                wait_product(dve, o)
                nc.vector.tensor_tensor(X[:, m, :], product(o)[:, 0:S], X[:, m, :], ALU.add).then_inc(free(o), 1)
                ahead(o)
            inverse_root("ffn2")
            scaled("hf", X, 8)
            normed_low(HA, "hf", "hf", 8, "norm_ffn_2")
            for j in range(FC):
                g, u = ("up2", 2 * j), ("up2", 2 * j + 1)
                wait_product(dve, g)
                ahead(g)
                dve.wait_ge(th_done, j + 1)
                nc.vector.scalar_tensor_tensor(out=YC[:, j % 2, 0, :], in0=G1[:, j % 2, 0, :], scalar=1.0,
                                               in1=product(g)[:, 0:S], op0=ALU.add, op1=ALU.mult).then_inc(free(g), 1)
                if j:
                    low(ACTS, "a2", j - 1, G1[:, (j - 1) % 2, 1, :])
                wait_product(dve, u)
                wait_freed(dve, g)
                if j >= 2:
                    dve.wait_ge(a_lo, SP0["a2"] + j - 1)
                nc.vector.scalar_tensor_tensor(out=G1[:, j % 2, 1, :], in0=YC[:, j % 2, 0, :], scalar=0.5,
                                               in1=product(u)[:, 0:S], op0=ALU.mult, op1=ALU.mult).then_inc(free(u), 1)
                ahead(u)
            low(ACTS, "a2", FC - 1, G1[:, (FC - 1) % 2, 1, :])
            for m in range(8):
                o = ("down2", m)
                wait_product(dve, o)
                nc.vector.tensor_tensor(X[:, m, :], product(o)[:, 0:S], X[:, m, :], ALU.add).then_inc(free(o), 1)
                ahead(o)


def rows_to_partitions(v):
    return v.reshape(-1, P).T


def fm_blocks(w):
    k, m = w.shape
    return w.reshape(k // P, P, m // P, P).transpose(1, 2, 0, 3).reshape(P, -1)


def tm_blocks(w):
    k, m = w.shape
    return w.reshape(k // P, P, m).transpose(1, 0, 2).reshape(P, -1)


def swapped(w):
    return np.concatenate([w[:, ROPE // 2:ROPE], w[:, :ROPE // 2]], axis=1)


def padded(w, m):
    return np.concatenate([w, np.zeros((w.shape[0], m - w.shape[1]), w.dtype)], axis=1)


def lay_out(inp):
    a = {k: np.asarray(v) for k, v in inp.items()}
    w_in = a["w_in"][0]
    sb = HEADS * DH
    cuts = np.cumsum([sb, sb, sb, 256, 128, ROPE])
    q, k, v, ql, kvl, kr = np.split(w_in, cuts[:-1], axis=1)
    kr_block = np.concatenate([np.zeros((D, 64), np.float32), kr, swapped(kr)], axis=1)
    segs = {"lat": fm_blocks(np.concatenate([ql, kvl, kr_block], axis=1)), "sbq": fm_blocks(q), "sbk": fm_blocks(k),
            "sbv": tm_blocks(v)}
    qu = a["w_q_up"][0].reshape(256, HEADS, DH + ROPE)
    qu = np.concatenate([np.concatenate([qu[:, h], swapped(qu[:, h, DH:])], axis=1) for h in range(HEADS)], axis=1)
    segs["qup"] = fm_blocks(qu)
    kvu = a["w_kv_up"][0].reshape(128, HEADS, 2 * DH)
    segs["kup"] = fm_blocks(kvu[:, :, :DH].reshape(128, -1))
    segs["vup"] = tm_blocks(kvu[:, :, DH:].reshape(128, -1))
    mk = a["w_mem_kv_2"][0]
    segs["memk"], segs["memv"] = fm_blocks(mk[:, :512]), tm_blocks(mk[:, 512:])
    segs["wo"] = fm_blocks(a["w_o"][0])

    def pairs(g, u):
        return np.stack([g.reshape(D, FC, P), u.reshape(D, FC, P)], axis=2).reshape(D, -1)

    up = a["w_up"][0]
    segs["up"] = fm_blocks(pairs(up[:, :FF], up[:, FF:]))
    segs["down"] = fm_blocks(a["w_down"][0])
    segs["ple"], segs["gate"] = fm_blocks(a["w_ple"][0]), fm_blocks(a["w_ple_gate"][0])
    w2 = a["w_in_2"][0]
    cuts = np.cumsum([512] + [128] * 6 + [24, 512, 512, 512] + [D] * 3)
    qn, kc, vc, ks, vs, kw, vw, gn, ca, cg, qm, m0, m1, m2 = np.split(w2, cuts[:-1], axis=1)
    segs["kv2"] = fm_blocks(np.concatenate([kc, vc, ks, kw], axis=1))
    segs["q2"] = fm_blocks(qn)
    segs["tm2"] = tm_blocks(padded(np.concatenate([vs, vw, gn], axis=1), 384))
    segs["conv2"] = fm_blocks(np.stack([ca.reshape(D, 4, P), cg.reshape(D, 4, P)], axis=2).reshape(D, -1))
    segs["qmem"] = fm_blocks(qm)
    segs["cmpk"], segs["cmpv"] = fm_blocks(a["cmp_w1_2"][0, 0]), fm_blocks(a["cmp_w1_2"][0, 1])
    for name, g, w in (("brnsa", m0, a["w_nsa_out_2"][0]), ("brconv", m1, a["w_conv_out_2"][0]),
                       ("brmem", m2, a["w_mem_out_2"][0])):
        gb, wb = fm_blocks(g).reshape(P, 8, -1), fm_blocks(w).reshape(P, 8, -1)
        segs[name] = np.concatenate([gb, wb], axis=2).reshape(P, -1)
    segs["wout"] = fm_blocks(a["w_out_2"][0])
    segs["up2"] = fm_blocks(pairs(a["w_gate_2"][0], a["w_up_2"][0]))
    segs["down2"] = fm_blocks(a["w_down_2"][0])
    stream = np.empty((NTILES, P, TILE), np.float32)
    at = 0
    for name, kk, mm, _ in STAGES:
        seg = segs[name]
        assert seg.shape == (P, kk * mm * P), name
        n = seg.shape[1]
        while n:
            t, o = divmod(at, TILE)
            if t >= NTILES:
                break
            w = min(n, TILE - o)
            stream[t, :, o:o + w] = seg[:, seg.shape[1] - n:seg.shape[1] - n + w]
            at, n = at + w, n - w

    def features(x):
        return np.ascontiguousarray(x.reshape(S, -1, P).transpose(2, 1, 0))

    cols = {}
    for name in ("g_pre_mix", "g_q_lat", "g_kv_lat", "g_grp_sb", "g_grp_mla", "g_post_mix", "g_pre_ffn", "conv_w",
                 "conv_b", "g_post_ffn", "g_ple_gate", "b_ple_gate", "g_post_ple", "norm_mix_2", "conv_b_2",
                 "conv_ln_g_2", "conv_ln_b_2", "norm_mem_2", "mem_qk_norm_2", "norm_ffn_2"):
        cols[name] = rows_to_partitions(a[name])
    nq = a["nsa_qk_norm_2"][0]
    cols["nsa_qk_norm_2"] = np.concatenate([nq, nq], axis=1).T
    cols["cmp_pos_2"] = a["cmp_pos_2"][0].reshape(2, 16, 2, DH).transpose(2, 3, 0, 1).reshape(P, 32)
    cols["conv_w_2"] = a["conv_w_2"][0, :, 0].reshape(KSIZE, 4, P).transpose(2, 1, 0).reshape(P, -1)
    i = np.arange(P) % 16
    inv = np.float32(1.0) / np.float32(10000.0) ** (np.arange(0, ROPE, 2, dtype=np.float32) / np.float32(ROPE))
    cols["freq"] = inv.astype(np.float32)[i][:, None]
    cols["sign"] = np.where(np.arange(P) % 32 < 16, -1.0, 1.0).astype(np.float32)[:, None]
    consts = np.concatenate([cols[n] for n, _ in CONSTS], axis=1).astype(np.float32, copy=False)
    w2k = a["cmp_w2_2"][0, 0].reshape(2, P, DH)
    w2k = np.concatenate([w2k, w2k], axis=2).transpose(1, 0, 2).reshape(P, 256)
    w2v = a["cmp_w2_2"][0, 1].reshape(2, P, DH).transpose(1, 0, 2).reshape(P, 128)
    return {
        "stream": stream, "xT": features(a["x"][0]), "memT": features(a["mem_2"][0]),
        "pT": features(a["p"][0, 0]), "pos": np.ascontiguousarray(np.broadcast_to(a["positions"], (P, S))),
        "consts": np.ascontiguousarray(consts), "w2": np.ascontiguousarray(np.concatenate([w2k, w2v], axis=1)),
    }


def kernel(**inputs):
    import concourse.bacc as bacc
    from concourse.bass_utils import run_bass_kernel_spmd

    nc = bacc.Bacc("TRN2", target_bir_lowering=False, num_devices=1)
    arrays = lay_out(inputs)
    aps = [nc.dram_tensor(n, v.shape, mybir.dt.from_np(v.dtype), kind="ExternalInput").ap() for n, v in arrays.items()]
    out = nc.dram_tensor("out", (P, DC, S), F32, kind="ExternalOutput").ap()
    program(nc, *aps, out)
    got = run_bass_kernel_spmd(nc, [arrays], core_ids=[0]).results[0]["out"]
    return np.asarray(got).transpose(2, 1, 0).reshape(1, S, D)
```

```python
import math
from contextlib import ExitStack

import numpy as np

import concourse.bass as bass
from concourse import mybir

F32 = mybir.dt.float32
F32R = mybir.dt.float32r
BF16 = mybir.dt.bfloat16
I32 = mybir.dt.int32
ALU = mybir.AluOpType
ACT = mybir.ActivationFunctionType
AX = mybir.AxisListType

P = 128
S = 256
D = 1024
DC = D // P
QT = S // P
HEADS = 8
DH = 64
ROPE = 32
FF = 2816
FC = FF // P
KSIZE = 31
MEMH = 4
CMP = 15
CSTEP = 16
EPS = 1e-6
LN_EPS = 1e-5
NEG = -1e30

BPT = 8
TILE = BPT * P
NRAW = 5
NSPLIT = 6
NBANK = 3

STAGES = [
    ("lat", 8, 4, "fm"), ("sbq", 8, 4, "fm"), ("sbk", 8, 4, "fm"), ("sbv", 8, 4, "tm"),
    ("qup", 2, 8, "fm"), ("kup", 1, 4, "fm"), ("vup", 1, 4, "tm"),
    ("wo", 8, 8, "fm"), ("memk", 8, 4, "fm"), ("up", 8, 2 * FC, "fm"), ("down", FC, 8, "fm"),
    ("ple", 2, 8, "fm"), ("gate", 8, 8, "fm"), ("memv", 8, 4, "tm"),
    ("kv2", 8, 4, "fm"), ("q2", 8, 4, "fm"), ("tm2", 8, 3, "tm"), ("conv2", 8, 8, "fm"), ("qmem", 8, 4, "fm"),
    ("cmpk", 16, 2, "tm"), ("gnsa", 8, 1, "fm"), ("cmpv", 16, 2, "tm"), ("gnsb", 8, 7, "fm"),
    ("brmem", 12, 8, "fm"), ("brconv", 12, 8, "fm"), ("brnsa", 4, 8, "fm"),
    ("wout", 8, 8, "fm"), ("up2", 8, 2 * FC, "fm"), ("down2", FC, 8, "fm"),
]
FIRST = {}
KC = {}
_b = 0
for _n, _k, _m, _o in STAGES:
    FIRST[_n], KC[_n] = _b, _k
    _b += _k * _m
NTILES = _b // BPT
assert _b % BPT == 0


FILL = {
    0: [("gnsb", 1), ("stat", "kcT"), ("stat", "vc"), ("gnsb", 2), ("stat", "kc")],
    1: [("gnsb", 3)], 2: [("gnsb", 4), ("gnsb", 5)], 3: [("gnsb", 6), ("brmem", 0)],
    4: [("brmem", 1)], 5: [("brmem", 2)], 6: [("brmem", 3)],
    7: [("brmem", 4), ("stat", "lnmean")], 8: [("brmem", 5), ("stat", "lnvar")],
    9: [("brmem", 6)], 10: [("brmem", 7)], 11: [("brconv", 0), ("brconv", 1)],
}
AFTER = {9: ("ln", "norm"), 10: ("ln", "silu")}
FILL_TURNED = [("brconv", 2)]
FILL_OUT = [("brconv", 3), ("brconv", 4), ("brconv", 5)]
FILL_SPLIT = [("brconv", 6), ("brconv", 7)]


def outputs():
    out = [("stat", "h1")]
    out += [("lat", m) for m in range(4)]
    out += [("sbq", 0), ("sbq", 1), ("stat", "qlat"), ("stat", "kvlat"), ("sbq", 2), ("sbq", 3)]
    out += [("sbk", m) for m in range(4)] + [("stat", "mem"), ("sbv", 0), ("sbv", 1)]
    out += [("qup", m) for m in range(8)] + [("kup", m) for m in range(4)] + [("vup", 0), ("vup", 1)]
    out += [("wo", m) for m in range(8)] + [("stat", "postmix")] + [("memk", m) for m in range(4)]
    out += [("stat", "preffn"), ("up", 0), ("up", 1), ("stat", "memk0"), ("stat", "memk1")]
    out += [("up", m) for m in range(2, 2 * FC)] + [("down", m) for m in range(8)]
    out += [("ple", m) for m in range(2)] + [("stat", "postffn")] + [("ple", m) for m in range(2, 4)]
    out += [("ple", m) for m in range(4, 8)] + [("stat", "plegate")]
    out += [("gate", m) for m in range(8)] + [("stat", "postple"), ("stat", "mix2"), ("memv", 0), ("memv", 1)]
    out += [("kv2", m) for m in range(4)] + [("q2", 0), ("q2", 1)] + [("stat", "ks"), ("stat", "kw")]
    out += [("q2", 2), ("q2", 3)] + [("tm2", 0), ("tm2", 1)] + [("stat", "q0"), ("stat", "q1")]
    out += [("conv2", m) for m in range(8)] + [("qmem", m) for m in range(4)]
    out += [("stat", "qm0"), ("stat", "qm1"), ("cmpk", 1), ("gnsa", 0), ("stat", "gk"), ("cmpv", 1), ("gnsb", 0)]
    out += [("stat", "gv")]
    for items in list(FILL.values()) + [FILL_TURNED, FILL_OUT, FILL_SPLIT]:
        for name, m in items:
            out += [(name + "g", m), (name, m)] if name[:2] == "br" else [(name, m)]
    out += [("brnsa", m) for m in range(8)]
    out += [("wout", m) for m in range(8)] + [("stat", "ffn2")]
    out += [("up2", m) for m in range(2 * FC)] + [("down2", m) for m in range(8)]
    return out


OUTS = outputs()
OUT = {o: i for i, o in enumerate(OUTS)}
TM = {n for n, _, _, o in STAGES if o == "tm"}
BLOCKS = {n: k * m for n, k, m, _ in STAGES}


def last_block(o):
    name, m = o
    if name == "stat" or (name in TM and m == 0):
        return None
    if name in TM:
        return FIRST[name] + BLOCKS[name] - 1
    if name.removesuffix("g") in ("brmem", "brconv"):
        return FIRST[name.removesuffix("g")] + 12 * m + (7 if name.endswith("g") else 11)
    return FIRST[name] + (m + 1) * KC[name] - 1


Y_COUNT, _c = {}, 0
for _o in OUTS:
    _l = last_block(_o)
    if _l is None or _l % BPT != BPT - 1:
        _c += 1
        Y_COUNT[_o] = _c

PLAIN_STATS = ("gk", "gv", "kcT", "vc", "lnmean")
FREE_COUNT, _c = {}, [0] * NBANK
for _i, _o in enumerate(OUTS):
    if _o[0] != "stat" or _o[1] in PLAIN_STATS:
        _c[_i % NBANK] += 1
        FREE_COUNT[_o] = _c[_i % NBANK]

S_USES = ([("sb", u) for u in range(4)] + [("mla", u) for u in range(4)] + [("mem", u) for u in range(2)]
          + [("cmp", u) for u in range(2)] + [("slc", u) for u in range(4)] + [("win", u) for u in range(4)])
T_USES = [("cum", 0)]
for _u in range(1, 4):
    T_USES += [("cum", _u), ("mla", _u - 1)]
T_USES += [("mla", 3), ("osb", 0), ("omla", 0), ("mem", 0), ("mem", 1), ("omem", 0)]
T_USES += [("cmp", u) for u in range(2)] + [("slc", u) for u in range(4)] + [("win", u) for u in range(4)]
T_USES += [("onsa", 0)]
O_USES = [("sb", 0), ("mla", 0), ("sb", 1), ("mla", 1), ("sb", 2), ("mla", 2), ("sb", 3), ("mla", 3)]
O_USES += [u for u in S_USES if u[0] in ("mem", "cmp", "slc", "win")]
T_COUNT, _c = {}, 0
for _u in T_USES:
    if _u[0] not in ("osb", "omla", "omem", "onsa"):
        _c += 1
        T_COUNT[_u] = _c
SU = {u: i for i, u in enumerate(S_USES)}
TU = {u: i for i, u in enumerate(T_USES)}
OU = {u: i for i, u in enumerate(O_USES)}
UNITS = [u for u in S_USES if u[0] != "sb"]
UI = {u: i for i, u in enumerate(UNITS)}
UNITS2 = UNITS[4:]

CONSTS = [
    ("g_pre_mix", 8), ("g_q_lat", 2), ("g_kv_lat", 1), ("g_grp_sb", 4), ("g_grp_mla", 4), ("g_post_mix", 8),
    ("g_pre_ffn", 8), ("conv_w", 3 * 2 * FC), ("conv_b", 2 * FC), ("g_post_ffn", 8), ("g_ple_gate", 8),
    ("b_ple_gate", 8), ("g_post_ple", 8), ("norm_mix_2", 8), ("nsa_qk_norm_2", 4), ("cmp_pos_2", 32),
    ("conv_w_2", 4 * KSIZE), ("conv_b_2", 4), ("conv_ln_g_2", 4), ("conv_ln_b_2", 4), ("norm_mem_2", 8),
    ("mem_qk_norm_2", 2), ("norm_ffn_2", 8), ("freq", 1), ("sign", 1),
]
COL, _c = {}, 0
for _n, _w in CONSTS:
    COL[_n] = _c
    _c += _w
NCONST = _c


MEMK_AT = {2: 0, 4: 1}
MEM_SCALE = P ** -0.5
BIAS_STEP = 6


def bases(pairs):
    out, c = {}, 0
    for name, n in pairs:
        out[name] = c
        c += n
    return out


NORMS = [("h1", 8), ("qlat", 2), ("kvlat", 1), ("mem", 8), ("postmix", 8),
         ("preffn", 8), ("memk0", 1), ("memk1", 1), ("postffn", 8), ("plegate", 8), ("postple", 8), ("mix2", 8), ("ks", 2), ("kw", 2),
         ("q0", 2), ("q1", 2), ("qm0", 2), ("qm1", 2), ("kc", 1), ("lnvar", 4), ("ffn2", 8)]
SQ0 = bases(NORMS)
RT_ORDER = ["h1", "qlat", "kvlat", "mem", "osb", "omla", "postmix", "preffn", "memk0", "memk1", "postffn", "plegate",
            "postple", "mix2", "ks", "kw", "q0", "q1", "qm0", "qm1", "kc", "lnvar", "ffn2"]
RT = {n: i for i, n in enumerate(RT_ORDER)}
TN0 = bases([("h1", 4), ("ql", 1), ("kvl", 1), ("mem", 4), ("xn2", 4)])
SPLITS = [("h1", 8), ("ql", 2), ("kvl", 1), ("mem", 8), ("o", 8), ("ffn", 8), ("a", FC), ("p", 2), ("ph", 8),
          ("xn2", 8), ("bk", 1), ("bv", 1), ("om", 4), ("cv", 4), ("on", 4), ("y", 8), ("hf", 8), ("a2", FC)]
SP0 = bases(SPLITS)
X0 = bases([("postmix", 4), ("postffn", 4), ("postple", 4), ("wout", 8), ("final", 8)])
O_SPLIT = {"osb": SP0["o"], "omla": SP0["o"] + 4, "omem": SP0["om"], "onsa": SP0["on"]}


def program(nc, stream, xT, memT, pT, pos, consts, w2, out):
    ctx = ExitStack()
    with ctx:
        def sb(name, shape, dt=F32):
            return ctx.enter_context(nc.sbuf_tensor(name, shape, dt))

        def sem(name):
            return ctx.enter_context(nc.semaphore(name))

        raw = sb("raw", [P, NRAW, TILE])
        whi = sb("whi", [P, NSPLIT, TILE], F32R)
        wlo = sb("wlo", [P, NSPLIT, TILE], F32R)
        CV = sb("CV", [P, NCONST])
        X = sb("X", [P, DC, S])
        Y = sb("Y", [P, DC, S])
        SQ = sb("SQ", [P, DC, S])
        HA = sb("HA", [P, DC, 2 * S], F32R)
        HB = sb("HB", [P, DC, 2 * S], F32R)
        HL = sb("HL", [P, 4, 2 * S], F32R)
        KMEM = sb("KMEM", [P, MEMH, S])
        VMEM = sb("VMEM", [P, QT, 512])
        RTT = sb("RTT", [P, 2, 2 * S])
        RS = sb("RS", [P, 2 * S])
        RSF = sb("RSF", [P, S])
        ident = sb("ident", [P, P])
        ones = sb("ones", [P, P])
        ones64 = sb("ones64", [P, P])
        lower = sb("lower", [P, P])
        strict = sb("strict", [P, P])
        identb = sb("identb", [P, P], BF16)
        causalb = sb("causalb", [P, P], BF16)
        cmpb = sb("cmpb", [P, QT, CMP], BF16)
        valid = sb("valid", [P, QT])
        eps = sb("eps", [P, 2])
        warmed = sb("warmed", [P, 16])
        hbp = sb("hbp", [P, 8])
        negstrict = sb("negstrict", [P, P])
        mx = sb("mx", [P, 2, 8])
        sums = sb("sums", [P, 2, 8])
        rsum = sb("rsum", [P, 2, 8])
        ssq = sb("ssq", [P, 2, QT])
        srt = sb("srt", [P, 2, QT])
        rst = sb("rst", [P, 2, QT])

        def region(*tensors):
            with ExitStack() as stack:
                return [stack.enter_context(nc.sbuf_tensor(n, s, d)) for n, s, d in tensors]

        (EE,) = region(("EE", [P, DC, S], F32))
        ACTS, YC, G1, PX = region(("ACTS", [P, FC, 2 * S], F32R), ("YC", [P, 2, 2, S], F32), ("G1", [P, 2, 2, S], F32),
                                  ("PX", [P, 2, S], F32))
        (COS, SIN, QS, KS1, VS1, QM, KM, Z, E0) = region(
            ("COS", [P, S], F32), ("SIN", [P, S], F32), ("QS", [P, 4, S], F32), ("KS1", [P, 4, S], F32),
            ("VS1", [P, QT, 512], F32), ("QM", [P, HEADS, S], F32), ("KM", [P, HEADS, S], F32),
            ("Z", [P, HEADS, 384], F32),
            ("E0", [P, HEADS, 384], F32))
        (QN, KSD, KWD, CW, BS, G2, KCD, VC, VS2, GN, QME, U, CY, PR2, OMEM, TH) = region(
            ("QN", [P, 4, S], F32), ("KSD", [P, 2, S], F32), ("KWD", [P, 2, S], F32),
            ("CW", [P, 8 * S], F32), ("BS", [P, 2, 2, 16, 2 * CMP], F32R),
            ("G2", [P, 2, 2, 2 * CMP], F32), ("KCD", [P, 2 * CMP], F32), ("VC", [P, 2, DH], F32),
            ("VS2", [P, QT, 280], F32), ("GN", [P, QT, 24], F32), ("QME", [P, MEMH, S], F32),
            ("U", [P, 4, S], F32), ("CY", [P, 4, S], F32),
            ("PR2", [P, 2, 1024], F32), 
            ("OMEM", [P, QT, 512], F32), ("TH", [P, 2, S], F32))

        PROD = ctx.enter_context(nc.psum_tensor("PROD", [P, NBANK, 512], F32))
        SC = ctx.enter_context(nc.psum_tensor("SC", [P, 1024], F32))
        TP = ctx.enter_context(nc.psum_tensor("TP", [P, 1024], F32))
        OP = ctx.enter_context(nc.psum_tensor("OP", [P, 512], F32))
        PR1 = Y[:, :, :].rearrange("p c s -> p (c s)").rearrange("p (b n) -> p b n", b=2)
        MEMX = E0[:, :, :].rearrange("p h n -> p (h n)")[:, 0:DC * S].rearrange("p (c s) -> p c s", c=DC)
        VM = SQ[:, 0:4, :].rearrange("p c s -> p (c s)").rearrange("p (q n) -> p q n", q=QT)
        UU = Y[:, 4:8, :].rearrange("p (a b) s -> p a b s", a=2)
        GT = OMEM[:, 0, :].rearrange("p (k s) -> p k s", k=2)
        ONSA = KMEM[:, :, :].rearrange("p c s -> p (c s)").rearrange("p (q n) -> p q n", q=QT)
        W2 = Y[:, :, :].rearrange("p c s -> p (c s)")
        OMLA = KS1[:, :, :].rearrange("p c s -> p (c s)").rearrange("p (q n) -> p q n", q=QT)
        OSB = QS[:, :, :].rearrange("p c s -> p (c s)").rearrange("p (q n) -> p q n", q=QT)
        S2 = CW[:, 0:4 * S].rearrange("p (m g s) -> p m g s", m=2, g=2)
        TB = CW[:, 4 * S:4 * S + 64 * CMP].rearrange("p (m c n) -> p m c n", m=2, c=16)
        TG = CW[:, :].rearrange("p (m s) -> p m s", m=8)
        KSQ = Y[:, :, :].rearrange("p c s -> p (c s)")
        PT = SQ[:, 4:8, :].rearrange("p c s -> p (c s)")

        consts_in = sem("consts_in")
        x_in = [sem(f"x_in{i}") for i in range(2)]
        mem_in = sem("mem_in")
        p_in = sem("p_in")
        pos_in = sem("pos_in")
        raw_in = [sem(f"raw_in{i}") for i in range(NRAW)]
        masks = sem("masks")
        hi_done = sem("hi_done")
        lo_vector = sem("lo_vector")
        lo_pool = sem("lo_pool")
        w_used = sem("w_used")
        y_done = sem("y_done")
        y_free = [sem(f"y_free{i}") for i in range(NBANK)]
        sq_ready = sem("sq_ready")
        rt_ready = sem("rt_ready")
        rs_ready = sem("rs_ready")
        tn_ready = sem("tn_ready")
        a_hi = sem("a_hi")
        a_lo = sem("a_lo")
        x_ready = sem("x_ready")
        angles = sem("angles")
        sincos = sem("sincos")
        s_ready = sem("s_ready")
        sb_z = sem("sb_z")
        sb_e = sem("sb_e")
        sb_l = sem("sb_l")
        sb_sp = sem("sb_sp")
        sb_arg = sem("sb_arg")
        sb_a = sem("sb_a")
        mx_ready = sem("mx_ready")
        p_ready = sem("p_ready")
        t_ready = sem("t_ready")
        t_free = sem("t_free")
        o_ready = sem("o_ready")
        o_free = sem("o_free")
        o_normed = sem("o_normed")
        conv0 = sem("conv0")
        gelu_done = sem("gelu_done")
        act_out = sem("act_out")
        conv_done = sem("conv_done")
        gate_tanh = sem("gate_tanh")
        gated = sem("gated")
        act2_out = sem("act2_out")
        ge_ready = sem("ge_ready")
        bias_half = sem("bias_half")
        th_done = sem("th_done")
        w2_in = sem("w2_in")
        ln_biased = sem("ln_biased")
        ln_centred = sem("ln_centred")
        ln_scaled = sem("ln_scaled")
        ln_z = sem("ln_z")
        silu_done = sem("silu_done")
        cmp_sum = sem("cmp_sum")
        conv_u = sem("conv_u")
        conv_end = sem("conv_end")
        gate_in = sem("gate_in")
        gate_th = sem("gate_th")
        attn_in = sem("attn_in")
        qm_normed = sem("qm_normed")
        onsa_done = sem("onsa_done")
        th_used = sem("th_used")
        vchain = sem("vchain")
        schain = sem("schain")
        pchain = sem("pchain")
        stored = sem("stored")

        def split_wait(eng, n):
            if n % 3 == 2:
                eng.wait_ge(lo_vector, n // 3 + 1)
            else:
                eng.wait_ge(lo_pool, n - n // 3 + 1)

        def product(o):
            return PROD[:, OUT[o] % NBANK, :]

        def wait_product(eng, o):
            last = last_block(o)
            if last is not None and last % BPT == BPT - 1:
                eng.wait_ge(w_used, last // BPT + 1)
            else:
                eng.wait_ge(y_done, Y_COUNT[o])

        def free(o):
            return y_free[OUT[o] % NBANK]

        def wait_freed(eng, o):
            if o in FREE_COUNT:
                eng.wait_ge(y_free[OUT[o] % NBANK], FREE_COUNT[o])
            else:
                eng.wait_ge(rt_ready, RT[o[1]] + 1)

        def wait_turned(eng, use):
            if use[0] in O_SPLIT:
                eng.wait_ge(a_lo, O_SPLIT[use[0]] + 4)
            else:
                eng.wait_ge(t_free, T_COUNT[use])

        def end_tile(o):
            last = last_block(o)
            return -1 if last is None else (last + 1) // BPT - 1

        def unit_shape(unit):
            kind, u = unit
            if kind == "mem":
                return 4, S, QT, u, 0
            if kind == "cmp":
                return HEADS, CMP, 1, u, 0
            return 4, P * (u // 2 + 1), u // 2 + 1, u // 2, 4 * (u % 2)

        def score_at(kind, j):
            if kind in ("mla", "mem"):
                return j * S
            return j % 2 * 512 + j // 2 * (CMP if kind == "cmp" else S)

        block = ctx.enter_context(nc.Block())

        @block.sync
        def _(sp):
            sp.dma_start(Y[:, 1, :].bitcast(I32), pos).then_inc(pos_in, 16)
            sp.dma_start(CV[:, :], consts).then_inc(consts_in, 16)
            for i in range(2):
                sp.dma_start(X[:, 4 * i:4 * i + 4, :], xT[:, 4 * i:4 * i + 4, :]).then_inc(x_in[i], 16)
            for n in range(NTILES):
                if n >= NRAW:
                    split_wait(sp, n - NRAW)
                sp.dma_start(raw[:, n % NRAW, :], stream[n]).then_inc(raw_in[n % NRAW], 16)
                if n == 6:
                    sp.dma_start(MEMX, memT).then_inc(mem_in, 16)
                if n == FIRST["up"] // BPT + NSPLIT + NRAW + 2:
                    sp.dma_start(PX[:, :, :], pT).then_inc(p_in, 16)

                if n == FIRST["kv2"] // BPT + NSPLIT + NRAW + 2:
                    sp.dma_start(W2[:, 0:384], w2).then_inc(w2_in, 16)
            for m in range(8):
                wait_freed(sp, ("down2", m))
                sp.dma_start(out[:, m, :], X[:, m, :]).then_inc(stored, 16)
            sp.wait_ge(stored, 8 * 16)

        @block.gpsimd
        def _(pool):
            fills = [(ident, 0.0), (ones, 1.0), (ones64, 0.0), (lower, 1.0), (strict, 1.0), (negstrict, 0.0),
                     (causalb, 0.0), (cmpb, 0.0), (valid, 1.0)]
            for t, value in fills:
                nc.gpsimd.memset(t[:], value).then_inc(pchain, 1)
            nc.gpsimd.memset(eps[:, 0:1], EPS).then_inc(pchain, 1)
            nc.gpsimd.memset(eps[:, 1:2], LN_EPS).then_inc(pchain, 1)
            pool.wait_ge(pchain, 11)
            nc.gpsimd.memset(ones64[0:64, 0:64], 1.0).then_inc(pchain, 1)
            nc.gpsimd.memset(ones64[64:128, 64:128], 1.0).then_inc(pchain, 1)
            pool.wait_ge(pchain, 13)

            def select(t, op, fill, base, pattern, mult):
                nc.gpsimd.affine_select(out=t, in_=t, compare_op=op, fill=fill, base=base, pattern=pattern,
                                        channel_multiplier=mult).then_inc(pchain, 1)

            select(ident[:, :], ALU.not_equal, 1.0, 0, [[-1, P]], 1)
            select(lower[:, :], ALU.is_ge, 0.0, 0, [[-1, P]], 1)
            select(strict[:, :], ALU.is_gt, 0.0, 0, [[1, P]], -1)
            select(negstrict[:, :], ALU.is_gt, NEG, 0, [[1, P]], -1)
            select(causalb[:, :], ALU.is_ge, NEG, 0, [[-1, P]], 1)
            for qt in range(QT):
                select(cmpb[:, qt, :], ALU.is_ge, NEG, qt * P - 31, [[-CSTEP, CMP]], 1)
            select(valid[:, 0:1], ALU.is_ge, 0.0, -31, [[0, 1]], 1)
            pool.wait_ge(pchain, 21)
            nc.gpsimd.tensor_copy(identb[:, :], ident[:, :]).then_inc(masks, 1)
            for n in range(NTILES):
                if n % 3 == 2:
                    continue
                pool.wait_ge(hi_done, n + 1)
                nc.gpsimd.tensor_tensor(wlo[:, n % NSPLIT, :], raw[:, n % NRAW, :],
                                        whi[:, n % NSPLIT, :].bitcast(F32), ALU.subtract).then_inc(lo_pool, 1)

        @block.tensor
        def _(pe):
            def begin(o):
                if OUT[o] >= NBANK:
                    wait_freed(pe, OUTS[OUT[o] - NBANK])
                return product(o)

            def blk3(dst, b, hi, lo, start, stop, ends):
                n, i = divmod(b, BPT)
                if i == 0:
                    split_wait(pe, n)
                wh = whi[:, n % NSPLIT, i * P:(i + 1) * P]
                wl = wlo[:, n % NSPLIT, i * P:(i + 1) * P]
                nc.tensor.matmul(dst, wh, hi, start=start, stop=False, skip_group_check=True)
                nc.tensor.matmul(dst, wl, hi, start=False, stop=False, skip_group_check=True)
                last = nc.tensor.matmul(dst, wh, lo, start=False, stop=stop, skip_group_check=True)
                if i == BPT - 1:
                    last.then_inc(w_used, 1)
                elif ends:
                    last.then_inc(y_done, 1)

            def fm(stage, m, H, need=None, base=0):
                k = KC[stage]
                dst = begin((stage, m))[:, 0:S]
                for c in range(k):
                    if need is not None:
                        pe.wait_ge(a_lo, need + c + 1)
                    blk3(dst, FIRST[stage] + m * k + c, H[:, base + c, 0:S], H[:, base + c, S:2 * S],
                         c == 0, c == k - 1, c == k - 1)

            def tm(stage, cols, H, need=None, base=0, ks=None):
                m = BLOCKS[stage] // KC[stage]
                ks = range(KC[stage]) if ks is None else ks
                if ks[0] == 0:
                    begin((stage, 0)), begin((stage, 1))
                for c in ks:
                    if need is not None:
                        pe.wait_ge(a_lo, need + c + 1)
                    b = FIRST[stage] + c * m
                    end = b + m
                    while b < end:
                        n, i = divmod(b, BPT)
                        if i == 0:
                            split_wait(pe, n)
                        run = min(end - b, BPT - i)
                        at = (b - FIRST[stage] - c * m) * P
                        w = min(run * P, cols - at)
                        wh = whi[:, n % NSPLIT, i * P:i * P + w]
                        wl = wlo[:, n % NSPLIT, i * P:i * P + w]
                        for qt in range(QT):
                            dst = product((stage, qt))[:, at:at + w]
                            hi = H[:, base + c, qt * P:(qt + 1) * P]
                            lo = H[:, base + c, S + qt * P:S + (qt + 1) * P]
                            end_all = c == KC[stage] - 1 and b + run == end
                            nc.tensor.matmul(dst, hi, wh, start=c == 0 and at == 0, stop=False, skip_group_check=True)
                            nc.tensor.matmul(dst, hi, wl, start=False, stop=False, skip_group_check=True)
                            last = nc.tensor.matmul(dst, lo, wh, start=False, stop=end_all, skip_group_check=True)
                            if qt == 0 and end_all:
                                last.then_inc(y_done, 1)
                        if i + run == BPT:
                            last.then_inc(w_used, 1)
                        b += run

            def stat(name, chunks, mat=ones, wide=False):
                dst = begin(("stat", name))
                if wide:
                    pe.wait_ge(sq_ready, SQ0[name] + dict(NORMS)[name])
                    nc.tensor.matmul(dst, mat[:, :], chunks, start=True, stop=True).then_inc(y_done, 1)
                    return
                for i in range(len(chunks)):
                    pe.wait_ge(sq_ready, SQ0[name] + i + 1)
                    w = 2 * CMP if name == "kc" else S
                    last = nc.tensor.matmul(dst[:, 0:w], mat[:, :], chunks[i][:, 0:w], start=i == 0,
                                            stop=i == len(chunks) - 1)
                last.then_inc(y_done, 1)

            def s_begin(use):
                i = SU[use]
                if i:
                    kind, u = S_USES[i - 1]
                    if kind == "sb":
                        pe.wait_ge(sb_z, u + 1)
                    else:
                        pe.wait_ge(p_ready, UI[(kind, u)] + 1)

            def t_begin(use):
                if TU[use]:
                    wait_turned(pe, T_USES[TU[use] - 1])

            def o_begin(use):
                if OU[use]:
                    pe.wait_ge(o_free, OU[use])

            def sb_scores(u):
                s_begin(("sb", u))
                for j in range(2):
                    at = slice(64 * j, 64 * j + 64)
                    nc.tensor.matmul(SC[:, 512 * j:512 * j + S], KS1[at, u, 0:P], QS[at, u, :],
                                     start=True, stop=True, skip_group_check=True)
                    last = nc.tensor.matmul(SC[:, 512 * j + S:512 * j + 384], KS1[at, u, P:S], QS[at, u, P:S],
                                            start=True, stop=True, skip_group_check=True)
                last.then_inc(s_ready, 1)

            def sb_cum(u):
                pe.wait_ge(sb_sp, u + 1)
                t_begin(("cum", u))
                for j in range(2):
                    c, h = 512 * j, 2 * u + j
                    nc.tensor.matmul(TP[:, c:c + S], lower[:, :], E0[:, h, 0:S], start=True, stop=False,
                                     skip_group_check=True)
                    nc.tensor.matmul(TP[:, c + P:c + S], ones[:, :], E0[:, h, S:384], start=False, stop=True,
                                     skip_group_check=True)
                    last = nc.tensor.matmul(TP[:, c + S:c + 384], lower[:, :], E0[:, h, S:384], start=True, stop=True,
                                            skip_group_check=True)
                last.then_inc(t_ready, 1)

            def sb_pv(u):
                pe.wait_ge(sb_a, u + 1)
                o_begin(("sb", u))
                for j in range(2):
                    h = 2 * u + j
                    v = slice(h * DH, (h + 1) * DH)
                    o0 = OP[:, j * DH:(j + 1) * DH]
                    o1 = OP[:, P + j * DH:P + (j + 1) * DH]
                    nc.tensor.matmul(o0, Z[:, h, 0:P], VS1[:, 0, v], start=True, stop=True, skip_group_check=True)
                    nc.tensor.matmul(o1, Z[:, h, P:S], VS1[:, 0, v], start=True, stop=False, skip_group_check=True)
                    last = nc.tensor.matmul(o1, Z[:, h, S:384], VS1[:, 1, v], start=False, stop=True,
                                            skip_group_check=True)
                last.then_inc(o_ready, 1)

            def scores(unit):
                kind, u = unit
                nh, kw, nkb, qt, h0 = unit_shape(unit)
                s_begin(unit)
                q = slice(qt * P, (qt + 1) * P)
                for j in range(nh):
                    h = h0 + j
                    half = slice(64 * (h % 2), 64 * (h % 2) + 64)
                    at = score_at(kind, j)
                    if kind == "mla":
                        a, b = QM[0:96, h, q], KM[0:96, h, 0:kw]
                    elif kind == "mem":
                        a, b = QME[:, h, q], KMEM[:, h, 0:kw]
                    elif kind == "cmp":
                        a, b = QN[half, h // 2, q], KCD[half, (h // 4) * CMP:(h // 4 + 1) * CMP]
                    else:
                        a, b = QN[half, h // 2, q], (KSD if kind == "slc" else KWD)[half, h // 4, 0:kw]
                    last = nc.tensor.matmul(SC[:, at:at + kw], a, b, start=True, stop=kind == "mem",
                                            skip_group_check=True)
                    if kind == "cmp":
                        last = nc.tensor.matmul(SC[:, at:at + kw], identb[:, :], cmpb[:, qt, :], start=False,
                                                stop=True, skip_group_check=True)
                    elif kind != "mem":
                        last = nc.tensor.matmul(SC[:, at + kw - P:at + kw], identb[:, :], causalb[:, :], start=False,
                                                stop=True, skip_group_check=True)
                last.then_inc(s_ready, 1)

            def turn(unit, PR):
                nh, kw, nkb, qt, h0 = unit_shape(unit)
                pe.wait_ge(p_ready, UI[unit] + 1)
                t_begin(unit)
                b = UI[unit] % 2
                for j in range(nh):
                    for kb in range(nkb):
                        w = min(P, kw)
                        i = j * nkb + kb
                        last = nc.tensor.transpose(TP[0:w, i * P:(i + 1) * P],
                                                   PR[:, b, j * kw + kb * P:j * kw + kb * P + w], ident[:, :])
                last.then_inc(t_ready, 1)

            def pv(unit):
                kind, u = unit
                nh, kw, nkb, qt, h0 = unit_shape(unit)
                wait_turned(pe, unit)
                o_begin(unit)
                w = min(P, kw)
                for j in range(nh):
                    h = h0 + j
                    dv = P if kind == "mem" else DH
                    for kb in range(nkb):
                        if kind == "mla":
                            v = VM[:, kb, h * DH:(h + 1) * DH]
                        elif kind == "mem":
                            v = VMEM[:, kb, h * P:(h + 1) * P]
                        elif kind == "cmp":
                            v = VC[0:CMP, h // 4, :]
                        else:
                            c = (P if kind == "win" else 0) + (h // 4) * DH
                            v = VS2[:, kb, c:c + DH]
                        i = j * nkb + kb
                        last = nc.tensor.matmul(OP[:, j * dv:(j + 1) * dv], PT[0:w, i * P:(i + 1) * P], v,
                                                start=kb == 0, stop=kb == nkb - 1, skip_group_check=True)
                last.then_inc(o_ready, 1)

            def turn_out(use, src, ready, count):
                pe.wait_ge(ready, count)
                t_begin(use)
                for c in range(4):
                    for qt in range(QT):
                        last = nc.tensor.transpose(TP[:, c * S + qt * P:c * S + (qt + 1) * P],
                                                   src[:, qt, c * P:(c + 1) * P], ident[:, :])
                last.then_inc(t_ready, 1)

            pe.wait_ge(masks, 1)
            stat("h1", [SQ[:, c, :] for c in range(8)])
            for m in range(4):
                fm("lat", m, HA, SP0["h1"] if m == 0 else None)
            fm("sbq", 0, HA)
            fm("sbq", 1, HA)
            stat("qlat", [SQ[:, c, :] for c in range(2)])
            stat("kvlat", [SQ[:, 2, :]])
            fm("sbq", 2, HA)
            fm("sbq", 3, HA)
            for m in range(4):
                fm("sbk", m, HA)
            stat("mem", [SQ[:, c, :] for c in range(8)])
            tm("sbv", 512, HA)
            for m in range(8):
                fm("qup", m, HL, SP0["ql"] if m == 0 else None)
                if m == 1:
                    wait_freed(pe, ("sbk", 3))
                if m % 2:
                    sb_scores(m // 2)
            for m in range(4):
                fm("kup", m, HL, SP0["kvl"] if m == 0 else None, base=2)
            tm("vup", 512, HL, base=2)
            for u in range(4):
                sb_cum(u)
                if u:
                    sb_pv(u - 1)
                    turn(("mla", u - 1), PR1)
                else:
                    wait_freed(pe, ("vup", 1))
                scores(("mla", u))
                if u:
                    pv(("mla", u - 1))
            sb_pv(3)
            turn(("mla", 3), PR1)
            pv(("mla", 3))
            turn_out(("osb", 0), OSB, o_normed, 2)
            turn_out(("omla", 0), OMLA, o_normed, 4)
            for m in range(8):
                fm("wo", m, HA, SP0["o"] if m == 0 else None)
            stat("postmix", [SQ[:, c, :] for c in range(8)])
            for m in range(4):
                fm("memk", m, HB, SP0["mem"] if m == 0 else None)
            stat("preffn", [SQ[:, c, :] for c in range(8)])
            for m in range(2 * FC):
                fm("up", m, HA, SP0["ffn"] if m == 0 else None)
                if m == 1:
                    for i in range(2):
                        stat(f"memk{i}", KSQ[:, 2 * S * i:2 * S * (i + 1)], wide=True)
            for m in range(8):
                fm("down", m, ACTS, SP0["a"] if m == 0 else None)
            for m in range(2):
                fm("ple", m, HL, SP0["p"] if m == 0 else None)
            stat("postffn", [SQ[:, c, :] for c in range(8)])
            for m in range(2, 8):
                fm("ple", m, HL)
            stat("plegate", [SQ[:, c, :] for c in range(8)])
            for m in range(8):
                fm("gate", m, HA, SP0["ph"] if m == 0 else None)
            stat("postple", [SQ[:, c, :] for c in range(8)])
            tm("memv", 512, HB, ks=range(0, 5))
            stat("mix2", [SQ[:, c, :] for c in range(8)])
            tm("memv", 512, HB, ks=range(5, 8))


            def pair(i):
                return SQ[:, 2 * i:2 * i + 2, :].rearrange("p c s -> p (c s)")

            for m in range(4):
                fm("kv2", m, HA, SP0["xn2"] if m == 0 else None)
            fm("q2", 0, HA)
            fm("q2", 1, HA)
            stat("ks", pair(0), ones64, wide=True)
            stat("kw", pair(1), ones64, wide=True)
            fm("q2", 2, HA)
            fm("q2", 3, HA)
            tm("tm2", 280, HA)
            stat("q0", pair(2), ones64, wide=True)
            stat("q1", pair(3), ones64, wide=True)
            for m in range(8):
                fm("conv2", m, HA)
            for m in range(4):
                fm("qmem", m, HA)

            stat("qm0", pair(0), wide=True)
            stat("qm1", pair(1), wide=True)
            def turn_hidden(kv):
                wait_freed(pe, (("cmpk", "cmpv")[kv], 1))
                dst = begin(("stat", ("gk", "gv")[kv]))
                for k in range(2):
                    last = nc.tensor.transpose(dst[:, k * 2 * CMP:(k + 1) * 2 * CMP],
                                               GT[0:2 * CMP, kv, k * P:(k + 1) * P],
                                               ident[0:2 * CMP, 0:2 * CMP])
                last.then_inc(y_done, 1)

            for name, kv in (("cmpk", 0), ("cmpv", 1)):
                dst = begin((name, 1))[0:2 * CMP, 0:S]
                pe.wait_ge(a_lo, SP0["bk"] + kv + 1)
                for c in range(16):
                    n, i = divmod(FIRST[name] + 2 * c, BPT)
                    if i == 0:
                        split_wait(pe, n)
                    wh, wl = whi[:, n % NSPLIT, i * P:(i + 2) * P], wlo[:, n % NSPLIT, i * P:(i + 2) * P]
                    hi, lo = BS[:, kv, 0, c, :], BS[:, kv, 1, c, :]
                    nc.tensor.matmul(dst, hi, wh, start=c == 0, stop=False, skip_group_check=True)
                    nc.tensor.matmul(dst, hi, wl, start=False, stop=False, skip_group_check=True)
                    last = nc.tensor.matmul(dst, lo, wh, start=False, stop=c == 15, skip_group_check=True)
                    if i + 2 == BPT:
                        last.then_inc(w_used, 1)
                    elif c == 15:
                        last.then_inc(y_done, 1)
                fm(("gnsa", "gnsb")[kv], 0, HA)
                turn_hidden(kv)

            def fill(item):
                name, m = item
                if name == "stat":
                    if m == "kcT":
                        pe.wait_ge(w2_in, 16)
                        wait_freed(pe, ("stat", "gk"))
                        dst = begin(item)
                        for k in range(2):
                            last = nc.tensor.matmul(dst[:, 0:2 * CMP], W2[:, k * P:(k + 1) * P], G2[:, 0, k, :],
                                                    start=k == 0, stop=k == 1)
                        last.then_inc(y_done, 1)
                    elif m == "vc":
                        wait_freed(pe, ("stat", "gv"))
                        dst = begin(item)
                        for g in range(2):
                            for k in range(2):
                                last = nc.tensor.matmul(dst[0:CMP, g * DH:(g + 1) * DH],
                                                        G2[:, 1, k, g * CMP:(g + 1) * CMP],
                                                        W2[:, 2 * P + k * DH:2 * P + (k + 1) * DH], start=k == 0,
                                                        stop=k == 1, skip_group_check=True)
                        last.then_inc(y_done, 1)
                    elif m == "kc":
                        stat("kc", [SQ[:, 3, :]], ones64)
                    elif m == "lnmean":
                        pe.wait_ge(ln_biased, 4)
                        dst = begin(item)
                        for c in range(4):
                            last = nc.tensor.matmul(dst[:, 0:S], ones[:, :], CY[:, c, :], start=c == 0, stop=c == 3)
                        last.then_inc(y_done, 1)
                    else:
                        stat("lnvar", [SQ[:, c, :] for c in range(4)])
                    return
                if name in ("gnsb", "brnsa"):
                    fm(name, m, HA if name == "gnsb" else HL, SP0["on"] if name == "brnsa" and m == 0 else None)
                    return
                H, base, split = {"brmem": (HB, 4, "om"), "brconv": (HB, 0, "cv")}[name]
                b = FIRST[name] + 12 * m
                dst = begin((name + "g", m))[:, 0:S]
                for c in range(8):
                    blk3(dst, b + c, HA[:, c, 0:S], HA[:, c, S:2 * S], c == 0, c == 7, c == 7)
                dst = begin((name, m))[:, 0:S]
                for c in range(4):
                    if m == 0:
                        pe.wait_ge(a_lo, SP0[split] + c + 1)
                    blk3(dst, b + 8 + c, H[:, base + c, 0:S], H[:, base + c, S:2 * S], c == 0, c == 3, c == 3)

            pe.wait_ge(qm_normed, 2)
            for i, unit in enumerate(UNITS2):
                if i == 2:
                    pe.wait_ge(attn_in, 1)
                scores(unit)
                if i:
                    pv(UNITS2[i - 1])
                if i == 2:
                    turn_out(("omem", 0), OMEM, o_free, OU[("mem", 1)] + 1)
                for item in FILL.get(i, []):
                    fill(item)
                turn(unit, PR2)
            for item in FILL_TURNED:
                fill(item)
            pv(UNITS2[-1])
            for item in FILL_OUT:
                fill(item)
            turn_out(("onsa", 0), ONSA, onsa_done, 1)
            for item in FILL_SPLIT:
                fill(item)
            for m in range(8):
                fill(("brnsa", m))
            for m in range(8):
                fm("wout", m, HB, SP0["y"] if m == 0 else None)
            stat("ffn2", [SQ[:, c, :] for c in range(8)])
            for m in range(2 * FC):
                fm("up2", m, HA, SP0["hf"] if m == 0 else None)
            for m in range(8):
                fm("down2", m, ACTS, SP0["a2"] if m == 0 else None)

        @block.scalar
        def _(act):
            done = {"hi": 0, "links": 0, "warm": 0}

            def link(ins):
                done["links"] += 1
                ins.then_inc(schain, 1)
                act.wait_ge(schain, done["links"])

            def weights(upto):
                while done["hi"] < min(upto, NTILES):
                    n = done["hi"]
                    act.wait_ge(raw_in[n % NRAW], 16 * (n // NRAW + 1))
                    if n >= NSPLIT:
                        act.wait_ge(w_used, n - NSPLIT + 1)
                    nc.scalar.activation(whi[:, n % NSPLIT, :], raw[:, n % NRAW, :], ACT.Copy).then_inc(hi_done, 1)
                    done["hi"] += 1

            def ahead(o):
                weights(end_tile(o) + 1 + NSPLIT)

            def warm(function):
                nc.scalar.activation(warmed[:, done["warm"]:done["warm"] + 1], eps[:, 0:1], function)
                done["warm"] += 1

            def squares(name, c, src, at=None):
                nc.scalar.activation(SQ[:, c if at is None else at, :], src, ACT.Square).then_inc(sq_ready, 1)

            def root(name, features, width=S, which=0):
                wait_product(act, ("stat", name))
                if RT[name] >= 2:
                    act.wait_ge(rs_ready, RT[name] - 1)
                nc.scalar.activation(RTT[:, RT[name] % 2, 0:width], product(("stat", name))[:, 0:width], ACT.Sqrt,
                                     bias=eps[:, which:which + 1], scale=1.0 / features).then_inc(rt_ready, 1)

            def high(H, c, src, gain=1.0):
                nc.scalar.activation(H[:, c, 0:S], src, ACT.Copy, scale=gain).then_inc(a_hi, 1)

            def normed_high(H, name, chunks, gain, base=0):
                for c in range(chunks):
                    if c % 2 == 0:
                        act.wait_ge(tn_ready, TN0[name] + c // 2 + 1)
                    high(H, base + c, SQ[:, base + c, :], CV[:, COL[gain] + c:COL[gain] + c + 1])

            def out_block(o, m, gain=None):
                wait_product(act, o)
                src = product(o)[:, 0:S]
                squares(None, m, src)
                scale = 1.0 if gain is None else CV[:, COL[gain] + m:COL[gain] + m + 1]
                nc.scalar.activation(Y[:, m, :], src, ACT.Copy, scale=scale).then_inc(free(o), 1)
                ahead(o)

            def exps(unit, PR, scale):
                nh, kw, nkb, qt, h0 = unit_shape(unit)
                i = UI[unit]
                b = i % 2
                act.wait_ge(mx_ready, i + 1)
                if i >= 2:
                    act.wait_ge(t_ready, TU[UNITS[i - 2]] + 1)
                    act.wait_ge(o_free, OU[UNITS[i - 2]] + 1)
                for j in range(nh):
                    at = score_at(unit[0], j)
                    last = nc.scalar.activation(PR[:, b, j * kw:(j + 1) * kw], SC[:, at:at + kw], ACT.Exp,
                                                bias=mx[:, b, j:j + 1], scale=scale,
                                                accum_out=sums[:, b, j:j + 1])
                last.then_inc(p_ready, 1)

            def token_root(name, i, src):
                for qt in range(QT):
                    nc.scalar.activation(E0[:, 4:6, 0:S], src[:, qt, :].rearrange("p (c s) -> p c s", c=2), ACT.Square,
                                         accum_out=ssq[:, i, qt:qt + 1]).then_inc(schain, 1)
                    done["links"] += 1
                    act.wait_ge(schain, done["links"])
                nc.scalar.activation(srt[:, i, :], ssq[:, i, :], ACT.Sqrt, bias=eps[:, 0:1],
                                     scale=1.0 / 512).then_inc(rt_ready, 1)

            def turned_high(H, use, gain, base):
                act.wait_ge(t_ready, TU[use] + 1)
                for c in range(4):
                    g = 1.0 if gain is None else CV[:, COL[gain] + c:COL[gain] + c + 1]
                    high(H, base + c, TP[:, c * S:(c + 1) * S], g)

            act.wait_ge(masks, 1)
            warm(ACT.Sin)
            for c in range(8):
                if c % 4 == 0:
                    act.wait_ge(x_in[c // 4], 16)
                squares("h1", c, X[:, c, :])
            weights(1)
            act.wait_ge(consts_in, 16)
            act.wait_ge(angles, 2)
            nc.scalar.activation(SIN[:, :], SIN[:, :], ACT.Sin).then_inc(sincos, 1)
            nc.scalar.activation(COS[:, :], COS[:, :], ACT.Sin).then_inc(sincos, 1)
            root("h1", D)
            normed_high(HA, "h1", 8, "g_pre_mix")
            nc.scalar.activation(hbp[:, :], CV[:, COL["b_ple_gate"]:COL["b_ple_gate"] + 8], ACT.Copy,
                                 scale=0.5).then_inc(bias_half, 1)
            weights(NSPLIT)
            act.wait_ge(a_lo, SP0["h1"] + 8)
            for m in range(3):
                wait_product(act, ("lat", m))
                src = product(("lat", m))[:, 0:S]
                squares(None, m, src)
                nc.scalar.activation(Y[:, 4 + m, :], src, ACT.Copy).then_inc(free(("lat", m)), 1)
                ahead(("lat", m))

            def copy_out(o, dst, width=S, scale=1.0):
                wait_product(act, o)
                nc.scalar.activation(dst, product(o)[:, 0:width], ACT.Copy, scale=scale).then_inc(free(o), 1)
                ahead(o)

            copy_out(("sbq", 0), QS[:, 0, :])
            copy_out(("sbq", 1), QS[:, 1, :])
            root("qlat", 2 * P)
            normed_high(HL, "ql", 2, "g_q_lat")
            root("kvlat", P)
            act.wait_ge(tn_ready, TN0["kvl"] + 1)
            high(HL, 2, SQ[:, 2, :], CV[:, COL["g_kv_lat"]:COL["g_kv_lat"] + 1])
            copy_out(("sbq", 2), QS[:, 2, :])
            copy_out(("sbq", 3), QS[:, 3, :])
            copy_out(("sbk", 0), KS1[:, 0, :])
            act.wait_ge(mem_in, 16)
            act.wait_ge(a_lo, SP0["kvl"] + 1)
            for c in range(8):
                squares("mem", c, MEMX[:, c, :])
                if c % 2 and c < 7:
                    copy_out(("sbk", 1 + c // 2), KS1[:, 1 + c // 2, :])
            root("mem", D)
            normed_high(HB, "mem", 8, "norm_mem_2")
            warm(ACT.Exp)
            for o in (("sbk", 3), ("sbv", 1)):
                ahead(o)

            def sb_exp(u):
                act.wait_ge(sb_z, u + 1)
                e = E0[:, 2 * u:2 * u + 2, :]
                link(nc.scalar.activation(e, Z[:, 2 * u:2 * u + 2, :], ACT.Abs))
                nc.scalar.activation(e, e, ACT.Exp, scale=-1.0).then_inc(sb_e, 1)

            for h in range(HEADS):
                copy_out(("qup", h), QM[:, h, :])
                if h in (3, 5, 7):
                    sb_exp(h // 2 - 1)
            for m in range(4):
                if m == 2:
                    sb_exp(3)
                o = ("kup", m)
                wait_product(act, o)
                nc.scalar.activation(KM[0:64, 2 * m, :], product(o)[0:64, 0:S], ACT.Copy)
                nc.scalar.activation(KM[0:64, 2 * m + 1, :], product(o)[64:128, 0:S], ACT.Copy).then_inc(free(o), 1)
                ahead(o)
            act.wait_ge(sb_e, 4)
            for u in range(4):
                e = E0[:, 2 * u:2 * u + 2, :]
                nc.scalar.activation(e, e, ACT.Ln, bias=1.0).then_inc(sb_l, 1)
            warm(ACT.Exp)
            ahead(("vup", 1))
            scale_mla = (DH + ROPE) ** -0.5
            for u in range(4):
                act.wait_ge(sb_arg, u + 1)
                z = Z[:, 2 * u:2 * u + 2, :]
                nc.scalar.activation(z, z, ACT.Exp).then_inc(sb_a, 1)
                exps(("mla", u), PR1, scale_mla)
            warm(ACT.Sqrt)
            act.wait_ge(o_free, OU[("sb", 3)] + 1)
            token_root("osb", 0, OSB)
            act.wait_ge(o_free, OU[("mla", 3)] + 1)
            token_root("omla", 1, OMLA)
            turned_high(HA, ("osb", 0), "g_grp_sb", 0)
            turned_high(HA, ("omla", 0), "g_grp_mla", 4)
            for m in range(8):
                out_block(("wo", m), m, "g_post_mix")
            root("postmix", D)
            for c in range(0, 8, 2):
                copy_out(("memk", c // 2), KMEM[:, c // 2, :])
                act.wait_ge(x_ready, X0["postmix"] + c // 2 + 1)
                for k in range(c, c + 2):
                    squares("preffn", k, X[:, k, :])
                    high(HA, k, X[:, k, :], CV[:, COL["g_pre_ffn"] + k:COL["g_pre_ffn"] + k + 1])
            root("preffn", D)
            for i in range(2):
                nc.scalar.activation(KSQ[:, 2 * S * i:2 * S * (i + 1)],
                                     KMEM[:, 2 * i:2 * i + 2, :].rearrange("p c s -> p (c s)"),
                                     ACT.Square).then_inc(sq_ready, 1)

            def conv_first(j, g):
                o = ("up", 2 * j + g)
                wait_freed(act, o)
                if j >= 2:
                    act.wait_ge(act_out, j - 1)
                ch = g * FC + j
                nc.scalar.activation(YC[:, j % 2, g, :], UU[:, j % 2, g, :], ACT.Identity,
                                     scale=CV[:, COL["conv_w"] + 2 * 2 * FC + ch:COL["conv_w"] + 2 * 2 * FC + ch + 1],
                                     bias=CV[:, COL["conv_b"] + ch:COL["conv_b"] + ch + 1]).then_inc(conv0, 1)
                ahead(o)

            for j in range(FC + 1):
                if j:
                    act.wait_ge(conv_done, 2 * j - 1)
                    nc.scalar.activation(G1[:, (j - 1) % 2, 0, :], YC[:, (j - 1) % 2, 0, :],
                                         ACT.Gelu_apprx_tanh).then_inc(gelu_done, 1)
                if j < FC:
                    conv_first(j, 0)
                if j:
                    act.wait_ge(act_out, j)
                    high(ACTS, j - 1, G1[:, (j - 1) % 2, 1, :])
                if j < FC:
                    conv_first(j, 1)
                if j == 0:
                    root("memk0", P, 2 * S)
                    root("memk1", P, 2 * S)
            warm(ACT.Sqrt)
            act.wait_ge(p_in, 16)
            for c in range(2):
                high(HL, c, PX[:, c, :])
            act.wait_ge(a_lo, SP0["ffn"] + 8)
            for m in range(8):
                out_block(("down", m), m, "g_post_ffn")
            for m in range(2):
                copy_out(("ple", m), EE[:, m, :], scale=0.5)
            root("postffn", D)
            for m in range(2, 8):
                copy_out(("ple", m), EE[:, m, :], scale=0.5)
            for c in range(8):
                if c % 2 == 0:
                    act.wait_ge(x_ready, X0["postffn"] + c // 2 + 1)
                squares("plegate", c, X[:, c, :])
                high(HA, c, X[:, c, :], CV[:, COL["g_ple_gate"] + c:COL["g_ple_gate"] + c + 1])
            root("plegate", D)
            warm(ACT.Tanh)
            act.wait_ge(bias_half, 1)
            for m in range(9):
                if m < 8:
                    o = ("gate", m)
                    wait_freed(act, o)
                    if m >= 2:
                        act.wait_ge(ge_ready, m - 1)
                    nc.scalar.activation(G1[:, m % 2, 0, :], Y[:, m, :], ACT.Tanh, scale=0.5,
                                         bias=hbp[:, m:m + 1]).then_inc(gate_tanh, 1)
                    ahead(o)
                else:
                    warm(ACT.Sqrt)
                if m:
                    act.wait_ge(ge_ready, m)
                    if m == 1:
                        act.wait_ge(a_lo, SP0["ph"] + 8)
                    squares("postple", m - 1, Y[:, m - 1, :])
            root("postple", D)

            for c in range(8):
                if c % 2 == 0:
                    act.wait_ge(x_ready, X0["postple"] + c // 2 + 1)
                squares("mix2", c, X[:, c, :])
                if c in (3, 7):
                    weights(FIRST["memv"] // BPT + NSPLIT + (c + 1) // 4)
            root("mix2", D)
            normed_high(HA, "xn2", 8, "norm_mix_2")
            for qt in range(QT):
                copy_out(("memv", qt), VMEM[:, qt, :], 512)
            act.wait_ge(a_lo, SP0["xn2"] + 8)
            for m in range(2):
                wait_product(act, ("kv2", m))
                ahead(("kv2", m))
            for m, dst in ((2, KSD), (3, KWD)):
                o = ("kv2", m)
                wait_product(act, o)
                for g in range(2):
                    src = product(o)[64 * g:64 * g + 64, 0:S]
                    nc.scalar.activation(dst[0:64, g, :], src, ACT.Copy).then_inc(schain, 1)
                    last = nc.scalar.activation(dst[64:128, g, :], src, ACT.Copy)
                    done["links"] += 1
                    if g == 0:
                        done["links"] += 1
                        last.then_inc(schain, 1)
                last.then_inc(free(o), 1)
                wait_freed(act, o)
                for g in range(2):
                    squares(None, 2 * (m - 2) + g, dst[:, g, :])
                ahead(o)

            def head_block(o, dst, at):
                wait_product(act, o)
                src = product(o)[:, 0:S]
                squares(None, at, src)
                nc.scalar.activation(dst, src, ACT.Copy).then_inc(free(o), 1)
                ahead(o)

            head_block(("q2", 0), QN[:, 0, :], 4)
            head_block(("q2", 1), QN[:, 1, :], 5)
            root("ks", DH, 2 * S)
            root("kw", DH, 2 * S)
            for kv in range(2):
                act.wait_ge(cmp_sum, kv + 1)
                nc.scalar.activation(BS[:, kv, 0, :, :], TB[:, kv, :, :], ACT.Copy).then_inc(a_hi, 1)
            head_block(("q2", 2), QN[:, 2, :], 6)
            head_block(("q2", 3), QN[:, 3, :], 7)
            ahead(("tm2", 1))
            act.wait_ge(gate_in, 2)
            nc.scalar.activation(GN[:, :, :], VS2[:, :, 256:280], ACT.Tanh, scale=0.5).then_inc(gate_th, 1)
            root("q0", DH, 2 * S)
            root("q1", DH, 2 * S)
            for c in range(4):
                ahead(("conv2", 2 * c))
                o = ("conv2", 2 * c + 1)
                wait_product(act, o)
                if c >= 2:
                    act.wait_ge(conv_u, c - 1)
                nc.scalar.activation(TH[:, c % 2, :], product(o)[:, 0:S], ACT.Tanh, scale=0.5).then_inc(free(o), 1)
                ahead(o)
            for m in range(4):
                head_block(("qmem", m), QME[:, m, :], m)

            root("qm0", P, 2 * S)
            root("qm1", P, 2 * S)

            def nsa_gate(o, m):
                wait_product(act, o)
                nc.scalar.activation(TG[:, m, :], product(o)[:, 0:S], ACT.Tanh, scale=0.5).then_inc(free(o), 1)
                ahead(o)

            for kv, name in enumerate(("cmpk", "cmpv")):
                o = (name, 1)
                wait_product(act, o)
                nc.scalar.activation(GT[0:2 * CMP, kv, :], product(o)[0:2 * CMP, 0:S],
                                     ACT.Gelu_apprx_tanh).then_inc(free(o), 1)
                ahead(o)
                nsa_gate((("gnsa", "gnsb")[kv], 0), kv)
                item = ("stat", ("gk", "gv")[kv])
                wait_product(act, item)
                nc.scalar.activation(G2[:, kv, :, :].rearrange("p k n -> p (k n)"), product(item)[:, 0:4 * CMP],
                                     ACT.Copy).then_inc(free(item), 1)
            warm(ACT.Exp)

            def fill(item):
                name, m = item
                if item == ("stat", "kcT"):
                    wait_product(act, item)
                    src = product(item)[:, 0:2 * CMP]
                    nc.scalar.activation(SQ[:, 3, 0:2 * CMP], src, ACT.Square).then_inc(sq_ready, 1)
                    nc.scalar.activation(KCD[:, :], src, ACT.Copy).then_inc(free(item), 1)
                    return
                if item == ("stat", "kc"):
                    root("kc", DH, 2 * CMP)
                    return
                if item in (("stat", "lnmean"), ("stat", "vc")):
                    return
                if item == ("stat", "lnvar"):
                    for c in range(4):
                        act.wait_ge(ln_centred, c + 1)
                        squares("lnvar", c, CY[:, c, :])
                    root("lnvar", 512, S, 1)
                    return
                if item == ("ln", "norm"):
                    for c in range(4):
                        act.wait_ge(ln_scaled, c + 1)
                        g, b = COL["conv_ln_g_2"] + c, COL["conv_ln_b_2"] + c
                        nc.scalar.activation(U[:, c, :], CY[:, c, :], ACT.Identity, scale=CV[:, g:g + 1],
                                             bias=CV[:, b:b + 1]).then_inc(ln_z, 1)
                        act.wait_ge(ln_z, 2 * c + 1)
                        nc.scalar.activation(SQ[:, c, :], U[:, c, :], ACT.Tanh,
                                             scale=0.5).then_inc(ln_z, 1)
                    return
                if name == "gnsb":
                    nsa_gate(item, m + 1)
                    return
                if item == ("ln", "silu"):
                    for c in range(4):
                        act.wait_ge(silu_done, c + 1)
                        high(HB, c, CY[:, c, :], 0.5)
                    return
                if name == "brnsa":
                    ahead((name, m))
                    return
                o = (name + "g", m)
                wait_product(act, o)
                i = {"brmem": 0, "brconv": 8}[name] + m
                if i >= 2:
                    act.wait_ge(th_used, i - 1)
                nc.scalar.activation(TH[:, i % 2, :], product(o)[:, 0:S], ACT.Tanh, scale=0.5).then_inc(free(o), 1)
                ahead((name, m))

            for i, unit in enumerate(UNITS2):
                exps(unit, PR2, MEM_SCALE if unit[0] == "mem" else DH ** -0.5)
                if i == 2:
                    turned_high(HB, ("omem", 0), None, 4)
                if i == BIAS_STEP:
                    act.wait_ge(conv_end, 1)
                    for c in range(4):
                        b = COL["conv_b_2"] + c
                        nc.scalar.activation(CY[:, c, :], CY[:, c, :], ACT.Identity, scale=0.5,
                                             bias=CV[:, b:b + 1]).then_inc(ln_biased, 1)
                for item in FILL.get(i, []):
                    fill(item)
                nh, kw, nkb, qt, h0 = unit_shape(unit)
                act.wait_ge(t_ready, TU[unit] + 1)
                act.wait_ge(o_ready, OU[UNITS[UI[unit] - 1]] + 1)
                w, n = min(P, kw), nh * nkb * P
                nc.scalar.activation(PT[0:w, 0:n], TP[0:w, 0:n], ACT.Copy).then_inc(t_free, 1)
                if i in AFTER:
                    fill(AFTER[i])
            for item in FILL_TURNED + FILL_OUT:
                fill(item)
            turned_high(HL, ("onsa", 0), None, 0)
            for item in FILL_SPLIT:
                fill(item)
            for m in range(8):
                fill(("brnsa", m))
                if m:
                    act.wait_ge(th_used, 16 + m)
                    high(HB, m - 1, Y[:, m - 1, :], 0.5)
            warm(ACT.Sqrt)
            act.wait_ge(th_used, 24)
            high(HB, 7, Y[:, 7, :], 0.5)
            for m in range(8):
                o = ("wout", m)
                wait_freed(act, o)
                squares("ffn2", m, X[:, m, :])
                high(HA, m, X[:, m, :], CV[:, COL["norm_ffn_2"] + m:COL["norm_ffn_2"] + m + 1])
                ahead(o)
            root("ffn2", D)
            warm(ACT.Tanh)
            for j in range(FC + 1):
                if j < FC:
                    o = ("up2", 2 * j)
                    wait_freed(act, o)
                    if j >= 2:
                        act.wait_ge(gated, j - 1)
                    nc.scalar.activation(G1[:, j % 2, 0, :], UU[:, j % 2, 0, :], ACT.Tanh,
                                         scale=0.5).then_inc(th_done, 1)
                    ahead(o)
                if j:
                    act.wait_ge(act2_out, j)
                    high(ACTS, j - 1, G1[:, (j - 1) % 2, 1, :])
                if j < FC:
                    ahead(("up2", 2 * j + 1))
            for m in range(8):
                ahead(("down2", m))

        @block.vector
        def _(dve):
            done = {"lo": 2, "links": 0}

            def link(ins):
                done["links"] += 1
                ins.then_inc(vchain, 1)
                dve.wait_ge(vchain, done["links"])

            def weights(upto):
                while done["lo"] < min(upto, NTILES):
                    n = done["lo"]
                    dve.wait_ge(hi_done, n + 1)
                    nc.vector.tensor_tensor(wlo[:, n % NSPLIT, :], raw[:, n % NRAW, :],
                                            whi[:, n % NSPLIT, :].bitcast(F32), ALU.subtract).then_inc(lo_vector, 1)
                    done["lo"] += 3

            def ahead(o):
                weights(end_tile(o) + 1 + NSPLIT)

            def inverse_root(name, width=S, dst=RS):
                dve.wait_ge(rt_ready, RT[name] + 1)
                nc.vector.reciprocal(dst[:, 0:width], RTT[:, RT[name] % 2, 0:width]).then_inc(rs_ready, 1)
                dve.wait_ge(rs_ready, RT[name] + 1)

            def rs2():
                return RS[:, 0:S].unsqueeze(1).to_broadcast((P, 2, S))

            def scaled(name, src, chunks, base=0):
                if SP0[name]:
                    dve.wait_ge(a_lo, SP0[name])
                for c in range(0, chunks, 2):
                    n = min(2, chunks - c)
                    o, i = SQ[:, base + c:base + c + n, :], src[:, c:c + n, :]
                    r = rs2() if n == 2 else RS[:, 0:S].unsqueeze(1)
                    nc.vector.tensor_tensor(o, i, r, ALU.mult).then_inc(tn_ready, 1)
                dve.wait_ge(tn_ready, TN0[name] + (chunks + 1) // 2)

            def low(H, name, c, src, gain=1.0, base=0):
                dve.wait_ge(a_hi, SP0[name] + c + 1)
                nc.vector.scalar_tensor_tensor(out=H[:, base + c, S:2 * S], in0=src, scalar=gain,
                                               in1=H[:, base + c, 0:S].bitcast(F32), op0=ALU.mult,
                                               op1=ALU.subtract).then_inc(a_lo, 1)

            def normed_low(H, name, tn, chunks, gain, base=0):
                for c in range(chunks):
                    low(H, name, c, SQ[:, base + c, :], CV[:, COL[gain] + c:COL[gain] + c + 1], base)

            def copy_out(o, dst, width=S):
                wait_product(dve, o)
                nc.vector.tensor_copy(dst, product(o)[:, 0:width]).then_inc(free(o), 1)
                ahead(o)

            def rope(src, dst, par):
                t1, t2 = Y[64:96, 2 * par, :], Y[64:96, 2 * par + 1, :]
                nc.vector.tensor_tensor(t1, src[64:96, 0:S], COS[64:96, :], ALU.mult).then_inc(vchain, 1)
                last = nc.vector.tensor_tensor(t2, src[96:128, 0:S], SIN[96:128, :], ALU.mult)
                done["links"] += 1
                link(last)
                return nc.vector.tensor_tensor(dst, t1, t2, ALU.add)

            def maxima(unit, scale):
                nh, kw, nkb, qt, h0 = unit_shape(unit)
                b = UI[unit] % 2
                dve.wait_ge(s_ready, SU[unit] + 1)
                step = CMP if unit[0] == "cmp" else S
                dst = mx[:, b, 0:nh]
                if unit[0] in ("mla", "mem"):
                    src = SC[:, 0:nh * step].rearrange("p (h k) -> p h k", h=nh)[:, :, 0:kw]
                else:
                    dst = dst.rearrange("p (i r) -> p r i", r=2)
                    src = SC[:, :].rearrange("p (r n) -> p r n", r=2)[:, :, 0:nh // 2 * step].rearrange(
                        "p r (i k) -> p r i k", k=step)[:, :, :, 0:kw]
                if UI[unit] >= 2:
                    dve.wait_ge(p_ready, UI[unit] - 1)
                link(nc.vector.tensor_reduce(dst, src, AX.X, ALU.max, negate=True))
                nc.vector.tensor_scalar(mx[:, b, 0:nh], mx[:, b, 0:nh], scale, None, ALU.mult).then_inc(mx_ready, 1)

            def take_turned(unit):
                nh, kw, nkb, qt, h0 = unit_shape(unit)
                dve.wait_ge(t_ready, TU[unit] + 1)
                if UI[unit]:
                    dve.wait_ge(o_ready, OU[UNITS[UI[unit] - 1]] + 1)
                w = min(P, kw)
                n = nh * nkb * P
                nc.vector.tensor_copy(PT[0:w, 0:n], TP[0:w, 0:n]).then_inc(t_free, 1)

            def take_out(unit, dst, dv):
                nh, kw, nkb, qt, h0 = unit_shape(unit)
                b = UI[unit] % 2
                dve.wait_ge(p_ready, UI[unit] + 1)
                link(nc.vector.reciprocal(rsum[:, b, 0:nh], sums[:, b, 0:nh]))
                dve.wait_ge(o_ready, OU[unit] + 1)
                nc.vector.tensor_tensor(dst[:, qt, h0 * dv:(h0 + nh) * dv].rearrange("p (h d) -> p h d", h=nh),
                                        OP[:, 0:nh * dv].rearrange("p (h d) -> p h d", h=nh),
                                        rsum[:, b, 0:nh].unsqueeze(2).to_broadcast((P, nh, dv)),
                                        ALU.mult).then_inc(o_free, 1)

            def residual(name, gain=None, split=None):
                for c in range(0, 8, 2):
                    if gain is None:
                        link(nc.vector.tensor_tensor(SQ[:, c:c + 2, :], Y[:, c:c + 2, :], rs2(), ALU.mult))
                    else:
                        for k in range(c, c + 2):
                            ins = nc.vector.scalar_tensor_tensor(
                                out=SQ[:, k, :], in0=Y[:, k, :], scalar=CV[:, COL[gain] + k:COL[gain] + k + 1],
                                in1=RS[:, 0:S], op0=ALU.mult, op1=ALU.mult)
                        link(ins)
                    nc.vector.tensor_tensor(X[:, c:c + 2, :], X[:, c:c + 2, :], SQ[:, c:c + 2, :],
                                            ALU.add).then_inc(x_ready, 1)
                    if split and c:
                        x_low(*split, (c - 2, c - 1))
                if split:
                    x_low(*split, (6, 7))

            def x_low(name, gain, chunks):
                for k in chunks:
                    low(HA, name, k, X[:, k, :], CV[:, COL[gain] + k:COL[gain] + k + 1])

            magic = 1.5 * 2.0 ** 23
            c1 = 6.28125
            c2 = 2029.0 / 2 ** 20
            c3 = 2 * math.pi - c1 - c2
            ang, turns = Y[:, 0, :], Y[:, 2, :]
            dve.wait_ge(consts_in, 16)
            dve.wait_ge(pos_in, 16)
            link(nc.vector.tensor_copy(Y[:, 3, :], Y[:, 1, :].bitcast(I32)))
            link(nc.vector.tensor_scalar(ang, Y[:, 3, :], CV[:, COL["freq"]:COL["freq"] + 1], None, ALU.mult))
            for dst, quarter in ((SIN, 0.0), (COS, 0.25)):
                link(nc.vector.tensor_scalar(turns, ang, 1 / (2 * math.pi), quarter, ALU.mult, ALU.add))
                link(nc.vector.tensor_scalar(turns, turns, magic, None, ALU.add))
                link(nc.vector.tensor_scalar(turns, turns, magic, None, ALU.subtract))
                src = ang
                for c in (c1, c2, c3):
                    link(nc.vector.scalar_tensor_tensor(out=dst[:, :], in0=turns, scalar=-c, in1=src, op0=ALU.mult,
                                                        op1=ALU.add))
                    src = dst[:, :]
                link(nc.vector.tensor_scalar(dst[:, :], dst[:, :], 2 * math.pi * quarter, 3.1415925, ALU.add, ALU.min))
                nc.vector.tensor_scalar(dst[:, :], dst[:, :], -3.1415925, None, ALU.max).then_inc(angles, 1)
            inverse_root("h1")
            scaled("h1", X, 8)
            weights(2)
            normed_low(HA, "h1", "h1", 8, "g_pre_mix")
            weights(NSPLIT)
            dve.wait_ge(sincos, 2)
            link(nc.vector.tensor_scalar(SIN[:, :], SIN[:, :], CV[:, COL["sign"]:COL["sign"] + 1], None, ALU.mult))
            for m in range(3):
                ahead(("lat", m))
            o = ("lat", 3)
            wait_product(dve, o)
            rope(product(o), KM[64:96, 0, :], 0).then_inc(free(o), 1)
            wait_freed(dve, o)
            nc.vector.tensor_copy(KM[64:96, 1:8, :], KM[64:96, 0:1, :].to_broadcast((32, 7, S)))
            ahead(o)
            ahead(("sbq", 0))
            ahead(("sbq", 1))
            inverse_root("qlat")
            scaled("ql", Y[:, 4:6, :], 2)
            normed_low(HL, "ql", "ql", 2, "g_q_lat")
            inverse_root("kvlat")
            scaled("kvl", Y[:, 6:7, :], 1, base=2)
            low(HL, "kvl", 0, SQ[:, 2, :], CV[:, COL["g_kv_lat"]:COL["g_kv_lat"] + 1], base=2)
            for o in (("sbq", 2), ("sbq", 3), ("sbk", 0), ("sbk", 1), ("sbk", 2)):
                wait_product(dve, o)
                ahead(o)
            inverse_root("mem")
            scaled("mem", MEMX, 8)
            normed_low(HB, "mem", "mem", 8, "norm_mem_2")
            ahead(("sbk", 3))
            for qt in range(QT):
                copy_out(("sbv", qt), VS1[:, qt, :], 512)
            for h in range(0, HEADS, 4):
                for k in range(h, h + 4):
                    wait_product(dve, ("qup", k))
                    ahead(("qup", k))
                    if k % 2:
                        u = k // 2
                        dve.wait_ge(s_ready, u + 1)
                        nc.vector.tensor_scalar(Z[:, 2 * u:2 * u + 2, :],
                                                SC[:, :].rearrange("p (h k) -> p h k", h=2)[:, :, 0:384],
                                                DH ** -0.5, None, ALU.mult).then_inc(sb_z, 1)
                wait_freed(dve, ("qup", h + 1)), wait_freed(dve, ("qup", h + 2)), wait_freed(dve, ("qup", h + 3))
                q = QM[:, h:h + 4, :]
                t1, t2 = Y[64:96, 0:4, :], Y[64:96, 4:8, :]
                nc.vector.tensor_tensor(t1, q[64:96], COS[64:96, :].unsqueeze(1).to_broadcast((32, 4, S)),
                                        ALU.mult).then_inc(vchain, 1)
                done["links"] += 1
                link(nc.vector.tensor_tensor(t2, q[96:128], SIN[96:128, :].unsqueeze(1).to_broadcast((32, 4, S)),
                                             ALU.mult))
                link(nc.vector.tensor_tensor(q[64:96], t1, t2, ALU.add))
            for m in range(4):
                wait_product(dve, ("kup", m))
                ahead(("kup", m))
            for u in range(4):
                if u == 1:
                    for qt in range(QT):
                        copy_out(("vup", qt), VM[:, qt, :], 512)
                dve.wait_ge(sb_l, u + 1)
                e, z = E0[:, 2 * u:2 * u + 2, :], Z[:, 2 * u:2 * u + 2, :]
                link(nc.vector.scalar_tensor_tensor(out=e, in0=z, scalar=0.0, in1=e, op0=ALU.max, op1=ALU.add))
                for at in (0, S):
                    last = nc.vector.tensor_tensor(e[:, :, at:at + P], e[:, :, at:at + P],
                                                   strict[:, :].unsqueeze(1).to_broadcast((P, 2, P)), ALU.mult)
                last.then_inc(sb_sp, 1)

            def head_norm(name, dst, gain, g=None):
                inverse_root(name, 2 * S)
                for i in range(2):
                    last = nc.vector.scalar_tensor_tensor(out=dst[i], in0=dst[i], scalar=gain,
                                                          in1=RS[:, i * S:(i + 1) * S], op0=ALU.mult, op1=ALU.mult)
                link(last)

            scale_mla = (DH + ROPE) ** -0.5

            def take_sb(u):
                dve.wait_ge(o_ready, OU[("sb", u)] + 1)
                nc.vector.tensor_copy(OSB[:, :, u * P:(u + 1) * P],
                                      OP[:, 0:S].rearrange("p (q d) -> p q d", q=2)).then_inc(o_free, 1)

            for u in range(4):
                dve.wait_ge(t_ready, TU[("cum", u)] + 1)
                z = Z[:, 2 * u:2 * u + 2, :]
                nc.vector.scalar_tensor_tensor(out=z, in0=TP[:, :].rearrange("p (h k) -> p h k", h=2)[:, :, 0:384],
                                               scalar=-1.0, in1=z, op0=ALU.mult, op1=ALU.add).then_inc(t_free, 1)
                wait_turned(dve, ("cum", u))
                for at in (0, S):
                    last = nc.vector.tensor_tensor(z[:, :, at:at + P], z[:, :, at:at + P],
                                                   negstrict[:, :].unsqueeze(1).to_broadcast((P, 2, P)), ALU.add)
                last.then_inc(sb_arg, 1)
                if u:
                    take_sb(u - 1)
                    take_turned(("mla", u - 1))
                maxima(("mla", u), scale_mla)
                if u:
                    take_out(("mla", u - 1), OMLA, DH)
            take_sb(3)
            take_turned(("mla", 3))
            take_out(("mla", 3), OMLA, DH)

            def token_norm(name, i, dst):
                dve.wait_ge(rt_ready, RT[name] + 1)
                nc.vector.reciprocal(rst[:, i, :], srt[:, i, :]).then_inc(rs_ready, 1)
                dve.wait_ge(rs_ready, RT[name] + 1)
                for qt in range(QT):
                    nc.vector.tensor_scalar(dst[:, qt, :], dst[:, qt, :], rst[:, i, qt:qt + 1], None,
                                            ALU.mult).then_inc(o_normed, 1)

            def turned_low(H, use, name, gain, base, c0=0):
                for c in range(4):
                    g = 1.0 if gain is None else CV[:, COL[gain] + c:COL[gain] + c + 1]
                    dve.wait_ge(a_hi, SP0[name] + c0 + c // 2 * 2 + 2)
                    nc.vector.scalar_tensor_tensor(out=H[:, base + c, S:2 * S], in0=TP[:, c * S:(c + 1) * S],
                                                   scalar=g, in1=H[:, base + c, 0:S].bitcast(F32), op0=ALU.mult,
                                                   op1=ALU.subtract).then_inc(a_lo, 1)

            token_norm("osb", 0, OSB)
            token_norm("omla", 1, OMLA)
            turned_low(HA, ("osb", 0), "o", "g_grp_sb", 0)
            turned_low(HA, ("omla", 0), "o", "g_grp_mla", 4, 4)
            for m in range(8):
                wait_product(dve, ("wo", m))
                ahead(("wo", m))
            inverse_root("postmix")
            residual("postmix", split=("ffn", "g_pre_ffn"))
            for m in range(4):
                wait_product(dve, ("memk", m))
                ahead(("memk", m))
            inverse_root("preffn", dst=RSF)

            def up_scaled(j, g):
                o = ("up", 2 * j + g)
                wait_product(dve, o)
                nc.vector.tensor_tensor(UU[:, j % 2, g, :], product(o)[:, 0:S], RSF[:, :], ALU.mult).then_inc(
                    free(o), 1)
                ahead(o)

            def conv_rest(j, g):
                y, src = YC[:, j % 2, g, :], UU[:, j % 2, g, :]
                dve.wait_ge(conv0, 2 * j + g + 1)
                wait_freed(dve, ("up", 2 * j + g))
                for tap in (1, 0):
                    shift = 2 - tap
                    at = COL["conv_w"] + tap * 2 * FC + g * FC + j
                    ins = nc.vector.scalar_tensor_tensor(out=y[:, shift:S], in0=src[:, 0:S - shift],
                                                         scalar=CV[:, at:at + 1], in1=y[:, shift:S], op0=ALU.mult,
                                                         op1=ALU.add)
                    if tap:
                        link(ins)
                ins.then_inc(conv_done, 1)

            for j in range(FC + 1):
                if j < FC:
                    up_scaled(j, 0)
                if j:
                    conv_rest(j - 1, 1)
                    dve.wait_ge(gelu_done, j)
                    dve.wait_ge(conv_done, 2 * j)
                    if j >= 3:
                        dve.wait_ge(a_lo, SP0["a"] + j - 2)
                    nc.vector.tensor_tensor(G1[:, (j - 1) % 2, 1, :], G1[:, (j - 1) % 2, 0, :],
                                            YC[:, (j - 1) % 2, 1, :], ALU.mult).then_inc(act_out, 1)
                if j < FC:
                    up_scaled(j, 1)
                if j:
                    low(ACTS, "a", j - 1, G1[:, (j - 1) % 2, 1, :])
                if j < FC:
                    conv_rest(j, 0)
                if j in MEMK_AT:
                    i = MEMK_AT[j]
                    head_norm(f"memk{i}", [KMEM[:, 2 * i, :], KMEM[:, 2 * i + 1, :]],
                              CV[:, COL["mem_qk_norm_2"] + 1:COL["mem_qk_norm_2"] + 2])
            for c in range(2):
                low(HL, "p", c, PX[:, c, :])
            for m in range(8):
                wait_product(dve, ("down", m))
                ahead(("down", m))
            ahead(("ple", 1))
            inverse_root("postffn")
            residual("postffn", split=("ph", "g_ple_gate"))
            wait_freed(dve, ("up", 2 * FC - 1))
            inverse_root("plegate", dst=RSF)
            for m in range(9):
                if m < 8:
                    o = ("gate", m)
                    wait_product(dve, o)
                    nc.vector.tensor_tensor(Y[:, m, :], product(o)[:, 0:S], RSF[:, :], ALU.mult).then_inc(
                        free(o), 1)
                    ahead(o)
                if m:
                    dve.wait_ge(gate_tanh, m)
                    nc.vector.scalar_tensor_tensor(out=Y[:, m - 1, :], in0=G1[:, (m - 1) % 2, 0, :], scalar=1.0,
                                                   in1=EE[:, m - 1, :], op0=ALU.add, op1=ALU.mult).then_inc(
                        ge_ready, 1)
            inverse_root("postple")
            residual("postple", "g_post_ple")

            inverse_root("mix2")
            scaled("xn2", X, 8)
            normed_low(HA, "xn2", "xn2", 8, "norm_mix_2")
            ahead(("memv", 1))
            for m in range(2):
                o = ("kv2", m)
                wait_product(dve, o)
                for g in range(2):
                    src = product(o)[64 * g:64 * g + 64, :]
                    nc.vector.tensor_copy(S2[0:64, m, g, :], src[:, 0:S])
                    last = nc.vector.tensor_copy(S2[64:128, m, g, 0:S - 1], src[:, 1:S])
                last.then_inc(free(o), 1)
                ahead(o)
            for kv in range(2):
                wait_freed(dve, ("kv2", kv))
                for g in range(2):
                    for half in range(2):
                        src = S2[:, kv, g, CSTEP * half:CSTEP * half + CMP * CSTEP].rearrange(
                            "p (i c l) -> p c i l", c=8, l=2)[:, :, :, 0]
                        at = COL["cmp_pos_2"] + kv * 16 + 8 * half
                        last = nc.vector.tensor_tensor(
                            TB[:, kv, 8 * half:8 * half + 8, g * CMP:(g + 1) * CMP], src,
                            CV[:, at:at + 8].unsqueeze(2).to_broadcast((P, 8, CMP)), ALU.add)
                last.then_inc(cmp_sum, 1)
            ahead(("q2", 1))
            gains = {n: CV[:, COL["nsa_qk_norm_2"] + i:COL["nsa_qk_norm_2"] + i + 1]
                     for i, n in enumerate(("q", "c", "s", "w"))}
            head_norm("ks", [KSD[:, 0, :], KSD[:, 1, :]], gains["s"])
            head_norm("kw", [KWD[:, 0, :], KWD[:, 1, :]], gains["w"])
            for kv in range(2):
                dve.wait_ge(a_hi, SP0["bk"] + kv + 1)
                nc.vector.tensor_tensor(BS[:, kv, 1, :, :], TB[:, kv, :, :], BS[:, kv, 0, :, :].bitcast(F32),
                                        ALU.subtract).then_inc(a_lo, 1)
            ahead(("q2", 2))
            ahead(("q2", 3))
            for qt in range(QT):
                o = ("tm2", qt)
                wait_product(dve, o)
                nc.vector.tensor_copy(VS2[:, qt, :], product(o)[:, 0:280]).then_inc(free(o), 1)
                wait_freed(dve, o)
                nc.vector.tensor_copy(VS2[:, qt, 0:1], VS2[:, qt, 0:1]).then_inc(gate_in, 1)
                ahead(o)
            dve.wait_ge(gate_th, 1)
            nc.vector.tensor_scalar(GN[:, :, :], GN[:, :, :], 0.5, 0.5, ALU.mult, ALU.add).then_inc(vchain, 1)
            done["links"] += 1

            taps = [(c, k) for c0 in (0, 2) for k in range(KSIZE - 1, -1, -1) for c in (c0, c0 + 1)]
            at_tap = {}
            done["taps"] = 0

            def conv_taps(n):
                for c, k in taps[done["taps"]:done["taps"] + n]:
                    dve.wait_ge(conv_u, c + 1)
                    if c in at_tap:
                        dve.wait_ge(vchain, at_tap[c])
                    w = COL["conv_w_2"] + c * KSIZE + k
                    shift = KSIZE - 1 - k
                    if shift == 0:
                        ins = nc.vector.tensor_scalar(CY[:, c, :], U[:, c, :], CV[:, w:w + 1], None, ALU.mult)
                    else:
                        ins = nc.vector.scalar_tensor_tensor(out=CY[:, c, shift:S], in0=U[:, c, 0:S - shift],
                                                             scalar=CV[:, w:w + 1], in1=CY[:, c, shift:S],
                                                             op0=ALU.mult, op1=ALU.add)
                    ins.then_inc(vchain, 1)
                    done["links"] += 1
                    at_tap[c] = done["links"]
                    done["taps"] += 1

            qg = CV[:, COL["mem_qk_norm_2"]:COL["mem_qk_norm_2"] + 1]
            for c in range(4):
                o = ("conv2", 2 * c)
                wait_product(dve, o)
                ahead(o)
                wait_freed(dve, ("conv2", 2 * c + 1))
                nc.vector.scalar_tensor_tensor(out=U[:, c, :], in0=TH[:, c % 2, :], scalar=1.0,
                                               in1=product(o)[:, 0:S], op0=ALU.add, op1=ALU.mult).then_inc(free(o), 1)
                wait_freed(dve, o)
                nc.vector.tensor_copy(U[:, c, 0:1], U[:, c, 0:1]).then_inc(conv_u, 1)
                ahead(("conv2", 2 * c + 1))
                if c < 2:
                    head_norm(f"q{c}", [QN[:, 2 * c, :], QN[:, 2 * c + 1, :]], gains["q"])
                else:
                    conv_taps(8)
            for m in range(4):
                wait_product(dve, ("qmem", m))
                ahead(("qmem", m))
                conv_taps(6)
            for i in range(2):
                inverse_root(f"qm{i}", 2 * S)
                for k in range(2):
                    q = QME[:, 2 * i + k, :]
                    last = nc.vector.scalar_tensor_tensor(out=q, in0=q, scalar=qg, in1=RS[:, k * S:(k + 1) * S],
                                                          op0=ALU.mult, op1=ALU.mult)
                last.then_inc(qm_normed, 1)
                dve.wait_ge(qm_normed, i + 1)
                if i == 0:
                    wait_product(dve, ("cmpk", 1))
                    ahead(("cmpk", 1))
            conv_taps(4)
            for o in (("gnsa", 0), ("cmpv", 1)):
                wait_product(dve, o)
                ahead(o)
            maxima(UNITS2[0], MEM_SCALE)

            def take_nsa(unit):
                kind, u = unit
                nh, kw, nkb, qt, h0 = unit_shape(unit)
                b = UI[unit] % 2
                branch = ("cmp", "slc", "win").index(kind)
                dve.wait_ge(p_ready, UI[unit] + 1)
                link(nc.vector.reciprocal(rsum[:, b, 0:nh], sums[:, b, 0:nh]))
                gate = GN[:, qt, :].rearrange("p (h r) -> p r h", r=3)[:, branch, h0:h0 + nh]
                link(nc.vector.tensor_tensor(rsum[:, b, 0:nh], rsum[:, b, 0:nh], gate, ALU.mult))
                if kind == "cmp":
                    link(nc.vector.tensor_scalar(rsum[:, b, 0:nh], rsum[:, b, 0:nh], valid[:, qt:qt + 1], None,
                                                 ALU.mult))
                dve.wait_ge(o_ready, OU[unit] + 1)
                dst = ONSA[:, qt, h0 * DH:(h0 + nh) * DH]
                tmp = OMEM[:, 1, 0:nh * DH]
                out_ap = dst if kind == "cmp" else tmp
                nc.vector.tensor_tensor(out_ap.rearrange("p (h d) -> p h d", h=nh),
                                        OP[:, 0:nh * DH].rearrange("p (h d) -> p h d", h=nh),
                                        rsum[:, b, 0:nh].unsqueeze(2).to_broadcast((P, nh, DH)),
                                        ALU.mult).then_inc(o_free, 1)
                dve.wait_ge(o_free, OU[unit] + 1)
                if kind != "cmp":
                    ins = nc.vector.tensor_tensor(dst, dst, tmp, ALU.add)
                    if unit == UNITS2[-1]:
                        ins.then_inc(onsa_done, 1)
                    else:
                        link(ins)

            def fill(item):
                name, m = item
                if item in (("stat", "kcT"), ("stat", "lnvar")):
                    return
                if item == ("stat", "vc"):
                    wait_product(dve, item)
                    nc.vector.tensor_copy(VC[0:CMP, :, :],
                                          product(item)[0:CMP, 0:P].rearrange("p (g d) -> p g d", g=2)).then_inc(
                        free(item), 1)
                    return
                if item == ("stat", "kc"):
                    inverse_root("kc", 2 * CMP)
                    nc.vector.scalar_tensor_tensor(out=KCD[:, :], in0=KCD[:, :], scalar=gains["c"],
                                                   in1=RS[:, 0:2 * CMP], op0=ALU.mult,
                                                   op1=ALU.mult).then_inc(attn_in, 1)
                    return
                if item == ("stat", "lnmean"):
                    wait_product(dve, item)
                    mean = OMEM[:, 0, 0:S]
                    nc.vector.tensor_scalar(mean, product(item)[:, 0:S], 1.0 / 512, None, ALU.mult).then_inc(
                        free(item), 1)
                    wait_freed(dve, item)
                    for c in range(4):
                        nc.vector.tensor_tensor(CY[:, c, :], CY[:, c, :], mean, ALU.subtract).then_inc(ln_centred, 1)
                    return
                if item == ("ln", "norm"):
                    inverse_root("lnvar")
                    dve.wait_ge(ln_centred, 4)
                    for c in range(4):
                        nc.vector.tensor_tensor(CY[:, c, :], CY[:, c, :], RS[:, 0:S], ALU.mult).then_inc(ln_scaled, 1)
                    return
                if item == ("ln", "silu"):
                    for c in range(4):
                        dve.wait_ge(ln_z, 2 * c + 2)
                        nc.vector.scalar_tensor_tensor(out=CY[:, c, :], in0=SQ[:, c, :],
                                                       scalar=1.0, in1=U[:, c, :], op0=ALU.add,
                                                       op1=ALU.mult).then_inc(silu_done, 1)
                    for c in range(4):
                        low(HB, "cv", c, CY[:, c, :], 0.5)
                    return
                i = {"gnsb": 0, "brmem": 0, "brconv": 8, "brnsa": 16}[name] + m
                o = (name, m)
                if name == "gnsb":
                    wait_product(dve, o)
                    ahead(o)
                    return
                if name != "brnsa":
                    wait_product(dve, (name + "g", m))
                    ahead((name + "g", m))
                    wait_freed(dve, (name + "g", m))
                elif m == 0:
                    wait_freed(dve, ("gnsb", 6))
                wait_product(dve, o)
                gate = TG[:, m, :] if name == "brnsa" else TH[:, i % 2, :]
                dst = Y[:, m, :] if name == "brmem" else U[:, m % 2, :]
                nc.vector.scalar_tensor_tensor(out=dst, in0=gate, scalar=1.0, in1=product(o)[:, 0:S],
                                               op0=ALU.add, op1=ALU.mult).then_inc(free(o), 1)
                wait_freed(dve, o)
                if name == "brmem":
                    nc.vector.tensor_copy(Y[:, m, 0:1], Y[:, m, 0:1]).then_inc(th_used, 1)
                else:
                    ins = nc.vector.tensor_tensor(Y[:, m, :], Y[:, m, :], dst, ALU.add)
                    ins.then_inc(th_used, 1)
                    dve.wait_ge(th_used, i + 1)
                ahead(o)

            for i, unit in enumerate(UNITS2):
                if i:
                    maxima(unit, MEM_SCALE if unit[0] == "mem" else DH ** -0.5)
                else:
                    wait_product(dve, ("gnsb", 0))
                    ahead(("gnsb", 0))
                if 1 <= i <= 2:
                    take_out(UNITS2[i - 1], OMEM, P)
                elif i:
                    take_nsa(UNITS2[i - 1])
                if i == 2:
                    turned_low(HB, ("omem", 0), "om", None, 4)
                if i < BIAS_STEP:
                    conv_taps(len(taps) if i == BIAS_STEP - 1 else 14)
                    if i == BIAS_STEP - 1:
                        dve.wait_ge(vchain, done["links"])
                        nc.vector.tensor_copy(CY[:, 0, 0:1], CY[:, 0, 0:1]).then_inc(conv_end, 1)
                for item in FILL.get(i, []):
                    fill(item)
                if i in AFTER:
                    fill(AFTER[i])
            for item in FILL_TURNED:
                fill(item)
            take_nsa(UNITS2[-1])
            for item in FILL_OUT:
                fill(item)
            turned_low(HL, ("onsa", 0), "on", None, 0)
            for item in FILL_SPLIT:
                fill(item)
            for m in range(8):
                fill(("brnsa", m))
                low(HB, "y", m, Y[:, m, :], 0.5)
            for m in range(8):
                o = ("wout", m)
                wait_product(dve, o)
                nc.vector.tensor_tensor(X[:, m, :], product(o)[:, 0:S], X[:, m, :], ALU.add).then_inc(free(o), 1)
                ahead(o)
                if m:
                    x_low("hf", "norm_ffn_2", (m - 1,))
            wait_freed(dve, ("wout", 7))
            x_low("hf", "norm_ffn_2", (7,))
            wait_freed(dve, ("gate", 7))
            inverse_root("ffn2", dst=RSF)
            for j in range(FC):
                g, u = ("up2", 2 * j), ("up2", 2 * j + 1)
                wait_product(dve, g)
                nc.vector.tensor_tensor(UU[:, j % 2, 0, :], product(g)[:, 0:S], RSF[:, :], ALU.mult).then_inc(
                    free(g), 1)
                ahead(g)
                if j:
                    low(ACTS, "a2", j - 1, G1[:, (j - 1) % 2, 1, :])
                dve.wait_ge(th_done, j + 1)
                wait_freed(dve, g)
                nc.vector.scalar_tensor_tensor(out=YC[:, j % 2, 0, :], in0=G1[:, j % 2, 0, :], scalar=1.0,
                                               in1=UU[:, j % 2, 0, :], op0=ALU.add, op1=ALU.mult).then_inc(gated, 1)
                wait_product(dve, u)
                nc.vector.scalar_tensor_tensor(out=UU[:, j % 2, 1, :], in0=product(u)[:, 0:S], scalar=0.5,
                                               in1=RSF[:, :], op0=ALU.mult, op1=ALU.mult).then_inc(free(u), 1)
                dve.wait_ge(gated, j + 1)
                wait_freed(dve, u)
                if j >= 2:
                    dve.wait_ge(a_lo, SP0["a2"] + j - 1)
                nc.vector.tensor_tensor(G1[:, j % 2, 1, :], YC[:, j % 2, 0, :], UU[:, j % 2, 1, :],
                                        ALU.mult).then_inc(act2_out, 1)
                ahead(u)
            low(ACTS, "a2", FC - 1, G1[:, (FC - 1) % 2, 1, :])
            for m in range(8):
                o = ("down2", m)
                wait_product(dve, o)
                nc.vector.tensor_tensor(X[:, m, :], product(o)[:, 0:S], X[:, m, :], ALU.add).then_inc(free(o), 1)
                ahead(o)


def rows_to_partitions(v):
    return v.reshape(-1, P).T


def fm_blocks(w):
    k, m = w.shape
    return w.reshape(k // P, P, m // P, P).transpose(1, 2, 0, 3).reshape(P, -1)


def tm_blocks(w):
    k, m = w.shape
    return w.reshape(k // P, P, m).transpose(1, 0, 2).reshape(P, -1)


def swapped(w):
    return np.concatenate([w[:, ROPE // 2:ROPE], w[:, :ROPE // 2]], axis=1)


def padded(w, m):
    return np.concatenate([w, np.zeros((w.shape[0], m - w.shape[1]), w.dtype)], axis=1)


def lay_out(inp):
    a = {k: np.asarray(v) for k, v in inp.items()}
    w_in = a["w_in"][0]
    sb = HEADS * DH
    cuts = np.cumsum([sb, sb, sb, 256, 128, ROPE])
    q, k, v, ql, kvl, kr = np.split(w_in, cuts[:-1], axis=1)
    kr_block = np.concatenate([np.zeros((D, 64), np.float32), kr, swapped(kr)], axis=1)
    segs = {"lat": fm_blocks(np.concatenate([ql, kvl, kr_block], axis=1)), "sbq": fm_blocks(q), "sbk": fm_blocks(k),
            "sbv": tm_blocks(v)}
    qu = a["w_q_up"][0].reshape(256, HEADS, DH + ROPE)
    qu = np.concatenate([np.concatenate([qu[:, h], swapped(qu[:, h, DH:])], axis=1) for h in range(HEADS)], axis=1)
    segs["qup"] = fm_blocks(qu)
    kvu = a["w_kv_up"][0].reshape(128, HEADS, 2 * DH)
    segs["kup"] = fm_blocks(kvu[:, :, :DH].reshape(128, -1))
    segs["vup"] = tm_blocks(kvu[:, :, DH:].reshape(128, -1))
    mk = a["w_mem_kv_2"][0]
    segs["memk"], segs["memv"] = fm_blocks(mk[:, :512]), tm_blocks(mk[:, 512:])
    segs["wo"] = fm_blocks(a["w_o"][0])

    def pairs(g, u):
        return np.stack([g.reshape(D, FC, P), u.reshape(D, FC, P)], axis=2).reshape(D, -1)

    up = a["w_up"][0]
    segs["up"] = fm_blocks(pairs(up[:, :FF], up[:, FF:]))
    segs["down"] = fm_blocks(a["w_down"][0])
    segs["ple"], segs["gate"] = fm_blocks(a["w_ple"][0]), fm_blocks(a["w_ple_gate"][0])
    w2 = a["w_in_2"][0]
    cuts = np.cumsum([512] + [128] * 6 + [24, 512, 512, 512] + [D] * 3)
    qn, kc, vc, ks, vs, kw, vw, gn, ca, cg, qm, m0, m1, m2 = np.split(w2, cuts[:-1], axis=1)
    segs["kv2"] = fm_blocks(np.concatenate([kc, vc, ks, kw], axis=1))
    segs["q2"] = fm_blocks(qn)
    segs["tm2"] = tm_blocks(padded(np.concatenate([vs, vw, gn], axis=1), 384))
    segs["conv2"] = fm_blocks(np.stack([ca.reshape(D, 4, P), cg.reshape(D, 4, P)], axis=2).reshape(D, -1))
    segs["qmem"] = fm_blocks(qm)
    segs["cmpk"], segs["cmpv"] = tm_blocks(a["cmp_w1_2"][0, 0]), tm_blocks(a["cmp_w1_2"][0, 1])
    for name, g, w in (("brnsa", m0, a["w_nsa_out_2"][0]), ("brconv", m1, a["w_conv_out_2"][0]),
                       ("brmem", m2, a["w_mem_out_2"][0])):
        gb, wb = fm_blocks(g).reshape(P, 8, -1), fm_blocks(w).reshape(P, 8, -1)
        if name == "brnsa":
            segs["gnsa"], segs["gnsb"], segs[name] = fm_blocks(g[:, :P]), fm_blocks(g[:, P:]), fm_blocks(w)
            continue
        segs[name] = np.concatenate([gb, wb], axis=2).reshape(P, -1)
    segs["wout"] = fm_blocks(a["w_out_2"][0])
    segs["up2"] = fm_blocks(pairs(a["w_gate_2"][0], a["w_up_2"][0]))
    segs["down2"] = fm_blocks(a["w_down_2"][0])
    stream = np.empty((NTILES, P, TILE), np.float32)
    at = 0
    for name, kk, mm, _ in STAGES:
        seg = segs[name]
        assert seg.shape == (P, kk * mm * P), name
        n = seg.shape[1]
        while n:
            t, o = divmod(at, TILE)
            if t >= NTILES:
                break
            w = min(n, TILE - o)
            stream[t, :, o:o + w] = seg[:, seg.shape[1] - n:seg.shape[1] - n + w]
            at, n = at + w, n - w

    def features(x):
        return np.ascontiguousarray(x.reshape(S, -1, P).transpose(2, 1, 0))

    cols = {}
    for name in ("g_pre_mix", "g_q_lat", "g_kv_lat", "g_grp_sb", "g_grp_mla", "g_post_mix", "g_pre_ffn", "conv_w",
                 "conv_b", "g_post_ffn", "g_ple_gate", "b_ple_gate", "g_post_ple", "norm_mix_2", "conv_b_2",
                 "conv_ln_g_2", "conv_ln_b_2", "norm_mem_2", "mem_qk_norm_2", "norm_ffn_2"):
        cols[name] = rows_to_partitions(a[name])
    nq = a["nsa_qk_norm_2"][0]
    cols["nsa_qk_norm_2"] = np.concatenate([nq, nq], axis=1).T
    cols["cmp_pos_2"] = a["cmp_pos_2"][0].reshape(2, 16, 2, DH).transpose(2, 3, 0, 1).reshape(P, 32)
    cols["conv_w_2"] = a["conv_w_2"][0, :, 0].reshape(KSIZE, 4, P).transpose(2, 1, 0).reshape(P, -1)
    i = np.arange(P) % 16
    inv = np.float32(1.0) / np.float32(10000.0) ** (np.arange(0, ROPE, 2, dtype=np.float32) / np.float32(ROPE))
    cols["freq"] = inv.astype(np.float32)[i][:, None]
    cols["sign"] = np.where(np.arange(P) % 32 < 16, -1.0, 1.0).astype(np.float32)[:, None]
    consts = np.concatenate([cols[n] for n, _ in CONSTS], axis=1).astype(np.float32, copy=False)
    w2k = a["cmp_w2_2"][0, 0].reshape(2, P, DH)
    w2k = np.concatenate([w2k, w2k], axis=2).transpose(1, 0, 2).reshape(P, 256)
    w2v = a["cmp_w2_2"][0, 1].reshape(2, P, DH).transpose(1, 0, 2).reshape(P, 128)
    return {
        "stream": stream, "xT": features(a["x"][0]), "memT": features(a["mem_2"][0]),
        "pT": features(a["p"][0, 0]), "pos": np.ascontiguousarray(np.broadcast_to(a["positions"], (P, S))),
        "consts": np.ascontiguousarray(consts), "w2": np.ascontiguousarray(np.concatenate([w2k, w2v], axis=1)),
    }


def kernel(**inputs):
    import concourse.bacc as bacc
    from concourse.bass_utils import run_bass_kernel_spmd

    nc = bacc.Bacc("TRN2", target_bir_lowering=False, num_devices=1)
    arrays = lay_out(inputs)
    aps = [nc.dram_tensor(n, v.shape, mybir.dt.from_np(v.dtype), kind="ExternalInput").ap() for n, v in arrays.items()]
    out = nc.dram_tensor("out", (P, DC, S), F32, kind="ExternalOutput").ap()
    program(nc, *aps, out)
    got = run_bass_kernel_spmd(nc, [arrays], core_ids=[0]).results[0]["out"]
    return np.asarray(got).transpose(2, 1, 0).reshape(1, S, D)
```
